# Optimizing a Trainium2 kernel written in Bass

```python
import jax, jax.numpy as jnp
from jax import lax
import numpy as np

D_MODEL = 1024
BATCH = 1
SEQ = 1024
DEPTH = 1
DEC_BATCH = 8
DEC_SEQ = 16
PAST_LEN = 1024

CHUNK = 64
WINDOW = 128
HEAD_DIM = 64
N_HEADS_A = D_MODEL // (2 * HEAD_DIM)
N_KV_A = 2
GQA_GROUP = N_HEADS_A // N_KV_A
N_HEADS_B = D_MODEL // (2 * HEAD_DIM)
DK_B = 64
DV_B = 64
Q_A = N_HEADS_A * HEAD_DIM
KV_A = N_KV_A * HEAD_DIM
W_B = N_HEADS_B * DK_B
V_B = N_HEADS_B * DV_B
IN_WIDTH = Q_A + 2 * KV_A + 2 * W_B + 2 * V_B
SPLITS = (Q_A, Q_A + KV_A, Q_A + 2 * KV_A, Q_A + 2 * KV_A + W_B,
          Q_A + 2 * KV_A + 2 * W_B, Q_A + 2 * KV_A + 2 * W_B + V_B)
MIX_WIDTH = Q_A + V_B
N_EXPERTS = 16
N_GROUPS = 4
EXPERTS_PER_GROUP = N_EXPERTS // N_GROUPS
TOP_K = 2
D_EXPERT = D_MODEL // 2
RMS_EPS = 1e-6
NEG_INF = -1e30

kernel_name = 'hymba_swa_sink_hgrn2_grouped_moe_stream_step'

def rmsnorm(x, g):
    xf = x.astype(jnp.float32)
    y = xf * lax.rsqrt(jnp.mean(xf * xf, axis=-1, keepdims=True) + RMS_EPS)
    return (y * g.astype(jnp.float32)).astype(x.dtype)

def alibi_slopes():
    return jnp.exp2(-8.0 * jnp.arange(1, N_HEADS_A + 1, dtype=jnp.float32) / N_HEADS_A)

def lower_bounds(lb_param):
    cum = jnp.cumsum(jax.nn.softmax(lb_param.astype(jnp.float32), axis=0), axis=0)
    return cum - cum[0:1]

def sink_attention(q, k, v, dist, valid, sinks):
    s = jnp.einsum('bnqkgd,bnskd->bnkgqs', q, k).astype(jnp.float32) * (HEAD_DIM ** -0.5)
    slopes = alibi_slopes().reshape(N_KV_A, GQA_GROUP)
    s = s - slopes[None, None, :, :, None, None] * dist[None, :, None, None, :, :]
    s = jnp.where(valid[None, :, None, None, None, :], s, NEG_INF)
    sink = sinks.astype(jnp.float32).reshape(N_KV_A, GQA_GROUP)[None, None, :, :, None, None]
    sink = jnp.broadcast_to(sink, s.shape[:-1] + (1,))
    p = jax.nn.softmax(jnp.concatenate([s, sink], axis=-1), axis=-1)[..., :-1]
    return jnp.einsum('bnkgqs,bnskd->bnqkgd', p.astype(v.dtype), v)

def swa_prompt(q, k, v, sinks):
    B, T = q.shape[:2]
    nc, nb = T // CHUNK, WINDOW // CHUNK
    qc = q.reshape(B, nc, CHUNK, N_KV_A, GQA_GROUP, HEAD_DIM)

    def band(a):
        ap = jnp.pad(a, ((0, 0), (WINDOW, 0), (0, 0), (0, 0)))
        ap = ap.reshape(B, nc + nb, CHUNK, N_KV_A, HEAD_DIM)
        return jnp.concatenate([ap[:, j:j + nc] for j in range(nb + 1)], axis=2)

    q_pos = jnp.arange(T).reshape(nc, CHUNK)
    k_pos = jnp.arange(nc)[:, None] * CHUNK - WINDOW + jnp.arange(WINDOW + CHUNK)[None, :]
    dist = jnp.abs(q_pos[:, :, None] - k_pos[:, None, :]).astype(jnp.float32)
    o = sink_attention(qc, band(k), band(v), dist, k_pos >= 0, sinks)
    return o.reshape(B, T, Q_A)

def swa_sample(q, k, v, k_cache, v_cache, sinks):
    B, L = q.shape[:2]
    R = k_cache.shape[1]
    k_all = jnp.concatenate([k_cache.astype(k.dtype), k], axis=1)[:, None]
    v_all = jnp.concatenate([v_cache.astype(v.dtype), v], axis=1)[:, None]
    q_pos = R + jnp.arange(L)
    k_pos = jnp.arange(R + L)
    dist = jnp.abs(q_pos[:, None] - k_pos[None, :]).astype(jnp.float32)[None]
    valid = jnp.ones((1, R + L), dtype=bool)
    o = sink_attention(q.reshape(B, 1, L, N_KV_A, GQA_GROUP, HEAD_DIM), k_all, v_all, dist, valid, sinks)
    return o.reshape(B, L, Q_A)

def hgrn_block(S, q, k, i, logf):
    L = q.shape[1]
    b = jnp.cumsum(logf, axis=1)
    causal = jnp.tril(jnp.ones((L, L), dtype=bool))[None, :, :, None, None]
    decay = jnp.exp(jnp.where(causal, b[:, :, None] - b[:, None, :], -jnp.inf))
    a = jnp.sum(q[:, :, None] * k[:, None] * decay, axis=-1)
    o = jnp.einsum('btsh,bshv->bthv', a, i) + jnp.einsum('bthk,bhkv->bthv', q * jnp.exp(b), S)
    b_last = b[:, -1]
    kd = k * jnp.exp(b_last[:, None] - b)
    S_new = jnp.exp(b_last)[..., None] * S + jnp.einsum('bshk,bshv->bhkv', kd, i)
    return S_new, o

def hgrn_scan(S0, q, k, i, logf):
    B, T = q.shape[:2]
    n = T // CHUNK

    def to_blocks(a):
        return jnp.moveaxis(a.reshape((B, n, CHUNK) + a.shape[2:]), 1, 0)

    def step(S, blk):
        return hgrn_block(S, *blk)

    S, o = lax.scan(step, S0, (to_blocks(q), to_blocks(k), to_blocks(i), to_blocks(logf)))
    return S, jnp.moveaxis(o, 0, 1).reshape(B, T, N_HEADS_B, DV_B)

def moe(h, w_router, router_bias, w_e_gate, w_e_up, w_e_down):
    B, T, D = h.shape
    hf = h.reshape(B * T, D)
    aff = jax.nn.sigmoid(jnp.dot(hf, w_router).astype(jnp.float32))
    sel = aff + router_bias.astype(jnp.float32)
    grp = sel.reshape(-1, N_GROUPS, EXPERTS_PER_GROUP)
    g_score = jnp.sum(lax.top_k(grp, TOP_K)[0], axis=-1)
    g_sel = jnp.argmax(g_score, axis=-1)
    in_group = (jnp.arange(N_EXPERTS) // EXPERTS_PER_GROUP)[None, :] == g_sel[:, None]
    _, idx = lax.top_k(jnp.where(in_group, sel, -jnp.inf), TOP_K)
    w = jnp.take_along_axis(aff, idx, axis=-1)
    w = w / jnp.sum(w, axis=-1, keepdims=True)
    gates = jnp.einsum('nk,nke->ne', w, jax.nn.one_hot(idx, N_EXPERTS, dtype=jnp.float32)).astype(h.dtype)
    y = jnp.zeros_like(hf)
    for e in range(N_EXPERTS):
        u = jax.nn.silu(jnp.dot(hf, w_e_gate[e])) * jnp.dot(hf, w_e_up[e])
        y = y + gates[:, e:e + 1] * jnp.dot(u, w_e_down[e])
    return y.reshape(B, T, D)

def trunk_layer(x, c, S0, k_cache, v_cache, lb, w_ada, b_ada, ln1, ln2, w_in, q_norm, k_norm, sinks,
                o_norm, w_out, w_router, router_bias, w_e_gate, w_e_up, w_e_down):
    B, T, _ = x.shape
    mod = jnp.dot(jax.nn.silu(c), w_ada) + b_ada
    sh1, sc1, g1, sh2, sc2, g2 = [m[:, None, :] for m in jnp.split(mod, 6, axis=-1)]

    h = rmsnorm(x, ln1) * (1 + sc1) + sh1
    qa, ka, va, qb, fb, ib, gb = jnp.split(jnp.dot(h, w_in), SPLITS, axis=-1)
    qa = rmsnorm(qa.reshape(B, T, N_HEADS_A, HEAD_DIM), q_norm)
    ka = rmsnorm(ka.reshape(B, T, N_KV_A, HEAD_DIM), k_norm)
    va = va.reshape(B, T, N_KV_A, HEAD_DIM)
    if k_cache is None:
        oa = swa_prompt(qa, ka, va, sinks)
        k_state, v_state = ka[:, -WINDOW:], va[:, -WINDOW:]
    else:
        oa = swa_sample(qa, ka, va, k_cache, v_cache, sinks)
        k_state, v_state = ka, va

    z = fb.astype(jnp.float32).reshape(B, T, N_HEADS_B, DK_B)
    lbh = lb.reshape(N_HEADS_B, DK_B)
    logf = jnp.logaddexp(jnp.log(lbh), jnp.log1p(-lbh) + jax.nn.log_sigmoid(z))
    kb = (1 - lbh) * jax.nn.sigmoid(-z)
    qh = qb.astype(jnp.float32).reshape(B, T, N_HEADS_B, DK_B) * (DK_B ** -0.5)
    ih = ib.astype(jnp.float32).reshape(B, T, N_HEADS_B, DV_B)
    S0 = S0.astype(jnp.float32)
    if k_cache is None:
        S, ob = hgrn_scan(S0, qh, kb, ih, logf)
    else:
        S, ob = hgrn_block(S0, qh, kb, ih, logf)
    ob = rmsnorm(ob, o_norm) * jax.nn.silu(gb.astype(jnp.float32).reshape(B, T, N_HEADS_B, DV_B))

    mix = jnp.concatenate([oa, ob.reshape(B, T, V_B).astype(x.dtype)], axis=-1)
    x = x + g1 * jnp.dot(mix, w_out)

    h2 = rmsnorm(x, ln2) * (1 + sc2) + sh2
    x = x + g2 * moe(h2, w_router, router_bias, w_e_gate, w_e_up, w_e_down)
    return x, k_state, v_state, S

def setup_inputs(seed: int = 0) -> dict:
    key = jax.random.key(seed)
    ks = jax.random.split(key, 24)
    f32 = jnp.float32
    R = min(WINDOW, PAST_LEN)

    def nrm(k, shape, scale):
        return jax.random.normal(k, shape, f32) * scale

    return {
        'x_prompt': nrm(ks[0], (BATCH, SEQ, D_MODEL), 1.0),
        'x_sample': nrm(ks[1], (DEC_BATCH, DEC_SEQ, D_MODEL), 1.0),
        'cache_k': nrm(ks[2], (DEPTH, DEC_BATCH, R, N_KV_A, HEAD_DIM), 1.0),
        'cache_v': nrm(ks[3], (DEPTH, DEC_BATCH, R, N_KV_A, HEAD_DIM), 1.0),
        'state_hgrn': nrm(ks[4], (DEPTH, DEC_BATCH, N_HEADS_B, DK_B, DV_B), 0.5),
        'c_prompt': nrm(ks[5], (BATCH, D_MODEL), 1.0),
        'c_sample': nrm(ks[6], (DEC_BATCH, D_MODEL), 1.0),
        'w_ada': nrm(ks[7], (DEPTH, D_MODEL, 6 * D_MODEL), 0.5 * D_MODEL ** -0.5),
        'b_ada': nrm(ks[8], (DEPTH, 6 * D_MODEL), 0.02),
        'ln1': 1.0 + nrm(ks[9], (DEPTH, D_MODEL), 0.02),
        'ln2': 1.0 + nrm(ks[10], (DEPTH, D_MODEL), 0.02),
        'w_in': nrm(ks[11], (DEPTH, D_MODEL, IN_WIDTH), D_MODEL ** -0.5),
        'q_norm': 1.0 + nrm(ks[12], (DEPTH, HEAD_DIM), 0.02),
        'k_norm': 1.0 + nrm(ks[13], (DEPTH, HEAD_DIM), 0.02),
        'sinks': nrm(ks[14], (DEPTH, N_HEADS_A), 1.0),
        'lb_param': nrm(ks[15], (DEPTH, N_HEADS_B * DK_B), 0.5),
        'o_norm': 1.0 + nrm(ks[16], (DEPTH, DV_B), 0.02),
        'w_out': nrm(ks[17], (DEPTH, MIX_WIDTH, D_MODEL), MIX_WIDTH ** -0.5),
        'w_router': nrm(ks[18], (D_MODEL, N_EXPERTS), D_MODEL ** -0.5),
        'router_bias': nrm(ks[19], (N_EXPERTS,), 0.01),
        'w_e_gate': nrm(ks[20], (DEPTH, N_EXPERTS, D_MODEL, D_EXPERT), D_MODEL ** -0.5),
        'w_e_up': nrm(ks[21], (DEPTH, N_EXPERTS, D_MODEL, D_EXPERT), D_MODEL ** -0.5),
        'w_e_down': nrm(ks[22], (DEPTH, N_EXPERTS, D_EXPERT, D_MODEL), D_EXPERT ** -0.5),
    }

def reference(x_prompt, x_sample, cache_k, cache_v, state_hgrn, c_prompt, c_sample, w_ada, b_ada,
              ln1, ln2, w_in, q_norm, k_norm, sinks, lb_param, o_norm, w_out, w_router, router_bias,
              w_e_gate, w_e_up, w_e_down):
    lbs = lower_bounds(lb_param)
    yp, ys = x_prompt, x_sample
    kp, vp, sp, kss, vss, sss = [], [], [], [], [], []
    s0_prompt = jnp.zeros((x_prompt.shape[0], N_HEADS_B, DK_B, DV_B), jnp.float32)
    for l in range(DEPTH):
        params = (lbs[l], w_ada[l], b_ada[l], ln1[l], ln2[l], w_in[l], q_norm[l], k_norm[l], sinks[l],
                  o_norm[l], w_out[l], w_router, router_bias, w_e_gate[l], w_e_up[l], w_e_down[l])
        yp, k_new, v_new, s_new = trunk_layer(yp, c_prompt, s0_prompt, None, None, *params)
        kp.append(k_new); vp.append(v_new); sp.append(s_new)
        ys, k_new, v_new, s_new = trunk_layer(ys, c_sample, state_hgrn[l], cache_k[l], cache_v[l], *params)
        kss.append(k_new); vss.append(v_new); sss.append(s_new)
    return (yp, ys, jnp.stack(kp), jnp.stack(vp), jnp.stack(sp), jnp.stack(kss), jnp.stack(vss), jnp.stack(sss))


_drawn_inputs = setup_inputs


def setup_inputs(seed=0):
    import zlib

    import numpy as np

    out = dict(_drawn_inputs(seed))
    spreads = {}
    factors = {'ln1': 2.814,
     'q_norm': 22.847,
     'k_norm': 2.798,
     'sinks': 25.248,
     'o_norm': 5.174,
     'cache_v': 4.403,
     'ln2': 6.901,
     'router_bias': 3.51}
    for name, (base, spread) in spreads.items():
        noise = np.random.default_rng([zlib.crc32(name.encode()), seed]).standard_normal(out[name].shape)
        drawn = base * np.exp(spread * noise) if base else spread * noise
        out[name] = __import__('jax').numpy.asarray(drawn.astype(out[name].dtype))
    for name, factor in factors.items():
        out[name] = (out[name] * factor).astype(out[name].dtype)
    return out
```

```python
from contextlib import ExitStack

import concourse.bass as bass
from concourse import mybir

F32 = mybir.dt.float32
I32 = mybir.dt.int32
ALU = mybir.AluOpType
ACT = mybir.ActivationFunctionType
AX_X = mybir.AxisListType.X

P = 128
D = 1024
KC = D // P
TP = 8
NT = TP + 1
NB = 8
L = 16
HD = 64
NKV = 2
G = 4
QW = 512
KW = NKV * HD
IN_W = QW + 2 * KW + 4 * QW
CQ, CK, CV, CQB, CFB, CIB, CGB = 0, 512, 640, 768, 1280, 1792, 2304
WIN = 128
NE = 16
NG = 4
DE = 512
MODS = 6
EPS = 1e-6
FAR = 1e33
LEVELS = (64, 32, 16, 8, 4, 2, 1)
LISTS = 2 * NT + NE - 1
SLOTS = LISTS + 2
ROWS = NT * P
TABLE = ROWS + P


def bc(ap, axis, n):
    ap = ap.unsqueeze(axis)
    shape = list(ap.shape)
    shape[axis] = n
    return ap.to_broadcast(shape)


def last_bc(ap, n):
    return ap.to_broadcast(list(ap.shape)[:-1] + [n])


class Chain:

    def __init__(self, eng, sem, base=0, turn=0, per=0):
        self.eng, self.sem, self.base, self.turn, self.per, self.k = eng, sem, base, turn, per, 0

    def __call__(self, ins):
        self.k += 1
        ins.then_inc(self.sem, 1)
        self.eng.wait_ge(self.sem, self.turn * self.per + (self.base + self.k))

    def done(self):
        assert self.k == self.per, (self.k, self.per)


def retire(nc, sems):
    nc.clear_and_free_semaphores(sems)
    nc.all_engine_barrier()


def stream_layer(nc, x, cond, cache_k, cache_v, state_in, w_ada, b_ada, ln1, ln2, w_in, q_norm, k_norm,
                 sinks, o_norm, w_out, w_router, router_bias, w_gate, w_up, w_down,
                 y, k_prompt, v_prompt, s_prompt, k_sample, v_sample, s_sample):
    mod_rows_d = nc.dram_tensor("mod_rows_d", (NT, 4 * D), F32).ap()
    top = ExitStack()
    with top:
        def sb(ctx, name, shape, dt=F32):
            return ctx.enter_context(nc.sbuf_tensor(name, shape, dt))

        def sem(name):
            return top.enter_context(nc.semaphore(name))

        psum = top.enter_context(nc.psum_tensor("psum", [P, 8, 512], F32))
        ident = sb(top, "ident", [P, P])
        mix_t = sb(top, "mix_t", [P, NT, KC, P])
        s_const = sem("s_const")
        w_in_loaded = sem("w_in_loaded")

        proj_ctx = ExitStack()
        with proj_ctx:
            mod_a = sb(proj_ctx, "mod_a", [P, 2, KC, NB])
            mod_b = sb(proj_ctx, "mod_b", [P, 2, KC, NB])
            x_in = sb(proj_ctx, "x_in", [P, D])
            h_t = sb(proj_ctx, "h_t", [P, KC, P])
            p_qk = sb(proj_ctx, "p_qk", [P, QW + KW])
            p_v = sb(proj_ctx, "p_v", [P, KW])
            p_q = sb(proj_ctx, "p_q", [P, QW])
            p_f = sb(proj_ctx, "p_f", [P, QW])
            p_i = sb(proj_ctx, "p_i", [P, QW])
            p_g = sb(proj_ctx, "p_g", [P, QW])
            norm_w = sb(proj_ctx, "norm_w", [P, 10, HD])
            o_norm_w = sb(proj_ctx, "o_norm_w", [P, HD])
            level_mask = sb(proj_ctx, "level_mask", [P, len(LEVELS), HD])
            consts_loaded = sem("consts_loaded")
            mask_made = sem("mask_made")

            win_ctx = ExitStack()
            with win_ctx:
                w_in_sb = sb(win_ctx, "w_in_sb", [P, KC, IN_W])

                with ExitStack() as ctx:
                    STAGES = 3
                    GROUPS = MODS * D // 512
                    stage = sb(ctx, "stage", [P, STAGES, KC, 512])
                    rows = mix_t[0:NT, :, :, :].rearrange("p n k r -> p (n k r)")
                    mod_row, ln2_row = rows[:, 0:MODS * D], rows[:, MODS * D:(MODS + 1) * D]
                    c_row, c_e = rows[:, (MODS + 1) * D:(MODS + 2) * D], rows[:, (MODS + 2) * D:(MODS + 3) * D]
                    c_t = sb(ctx, "c_t", [P, KC, NT])
                    bias_row = sb(ctx, "bias_row", [NT, 2, 512])
                    ln1_t = sb(ctx, "ln1_t", [P, KC])
                    c_loaded = sem("c_loaded")
                    ln_loaded = sem("ln_loaded")
                    stage_loaded = [sem(f"stage_loaded{i}") for i in range(STAGES)]
                    bias_loaded = [sem(f"bias_loaded{i}") for i in range(2)]
                    c_exp = sem("c_exp")
                    c_chain = sem("c_chain")
                    c_silu = sem("c_silu")
                    c_turned = sem("c_turned")
                    c_t_ready = sem("c_t_ready")
                    group_done = sem("group_done")
                    row_done = sem("row_done")
                    mod_turned = sem("mod_turned")
                    mod_ready = sem("mod_ready")
                    rows_stored = sem("rows_stored")
                    block = ctx.enter_context(nc.Block())

                    @block.sync
                    def _(sp):
                        sp.dma_start(c_row[:, :], cond).then_inc(c_loaded, 16)
                        for g in range(GROUPS):
                            if g >= STAGES:
                                sp.wait_ge(group_done, g - STAGES + 1)
                            sp.dma_start(stage[:, g % STAGES, :, :],
                                         w_ada[:, g * 512:(g + 1) * 512].rearrange("(k p) n -> p k n", p=P)
                                         ).then_inc(stage_loaded[g % STAGES], 16)
                            if g >= 2:
                                sp.wait_ge(row_done, g - 1)
                            sp.dma_start(bias_row[:, g % 2, :],
                                         b_ada[g * 512:(g + 1) * 512].partition_broadcast(NT)
                                         ).then_inc(bias_loaded[g % 2], 16)
                            if g == 0:
                                with nc.allow_non_contiguous_dma("a column of ln1 for each chunk"):
                                    sp.dma_start(ln1_t[:, :], ln1.rearrange("(k p) -> p k", p=P)).then_inc(ln_loaded, 16)
                                sp.dma_start(ln2_row[:, :], ln2.partition_broadcast(NT)).then_inc(ln_loaded, 16)
                                sp.dma_start(o_norm_w[:, :], o_norm.partition_broadcast(P)).then_inc(consts_loaded, 16)
                                for h in range(10):
                                    src = q_norm if h < 8 else k_norm
                                    sp.dma_start(norm_w[:, h, :], src.partition_broadcast(P)).then_inc(consts_loaded, 16)
                        w_in_v = w_in.rearrange("(k p) n -> p k n", p=P)
                        for a in range(0, IN_W, 704):
                            sp.dma_start(w_in_sb[:, :, a:a + 704], w_in_v[:, :, a:a + 704]).then_inc(w_in_loaded, 16)
                        sp.wait_ge(row_done, GROUPS + 2)
                        sp.dma_start(mod_rows_d[:, 0:D], mod_row[:, 2 * D:3 * D]).then_inc(rows_stored, 16)
                        sp.dma_start(mod_rows_d[:, D:4 * D], mod_row[:, 3 * D:6 * D]).then_inc(rows_stored, 16)
                        sp.wait_ge(rows_stored, 32)

                    @block.gpsimd
                    def _(pool):
                        link = Chain(pool, mask_made)
                        link(pool.memset(ident[:, :], 0.0))
                        pool.affine_select(out=ident[:, :], in_=ident[:, :], compare_op=ALU.not_equal, fill=1.0,
                                           base=0, pattern=[[-1, P]], channel_multiplier=1).then_inc(s_const, 1)
                        link(pool.memset(level_mask[:, :, :], 1.0))
                        for i, h in enumerate(LEVELS):
                            n = HD // h
                            m = level_mask[:, i, :].rearrange("p (n h) -> p n h", h=h)
                            link(pool.affine_select(out=m, in_=m, compare_op=ALU.is_ge, fill=0.0, base=0,
                                                    pattern=[[-2 * h, n], [0, h]], channel_multiplier=1))
                            link(pool.affine_select(out=m, in_=m, compare_op=ALU.is_ge, fill=0.0, base=h - 1,
                                                    pattern=[[2 * h, n], [0, h]], channel_multiplier=-1))

                    @block.scalar
                    def _(act):
                        act.wait_ge(c_loaded, 16)
                        act.activation(c_e[:, :], c_row[:, :], ACT.Exp, scale=-1.0).then_inc(c_exp, 1)

                    @block.vector
                    def _(dve):
                        link = Chain(dve, c_chain)
                        dve.wait_ge(c_exp, 1)
                        link(dve.tensor_scalar(c_e[:, :], c_e[:, :], 1.0, None, ALU.add))
                        link(dve.reciprocal(c_e[:, :], c_e[:, :]))
                        dve.tensor_tensor(c_row[:, :], c_row[:, :], c_e[:, :], ALU.mult).then_inc(c_silu, 1)
                        dve.wait_ge(consts_loaded, 11 * 16)
                        link(dve.tensor_scalar(norm_w[:, 0:8, :], norm_w[:, 0:8, :], HD ** -0.5, None, ALU.mult))
                        dve.wait_ge(c_turned, 1)
                        dve.tensor_copy(c_t[:, :, :], psum[:, 0, 0:KC * NT].rearrange("p (k n) -> p k n", n=NT)).then_inc(c_t_ready, 1)
                        for g in range(GROUPS):
                            dve.wait_ge(group_done, g + 1)
                            dve.wait_ge(bias_loaded[g % 2], 16 * (g // 2 + 1))
                            dve.tensor_tensor(mod_row[:, g * 512:(g + 1) * 512], psum[0:NT, 1 + g % 2, :],
                                              bias_row[:, g % 2, :], ALU.add).then_inc(row_done, 1)
                            if g == 4:
                                dve.wait_ge(mod_turned, 1)
                                dve.wait_ge(ln_loaded, 32)
                                turned = psum[:, 3, 0:2 * KC * NT].rearrange("p (k n) -> p k n", n=NT)
                                for kind, cols in ((0, slice(0, 1)), (1, slice(1, NT))):
                                    sh, sc = turned[:, 0:KC, cols], turned[:, KC:2 * KC, cols]
                                    if kind == 0:
                                        sh, sc = last_bc(sh, NB), last_bc(sc, NB)
                                    dve.tensor_copy(mod_b[:, kind, :, :], sh)
                                    link(dve.tensor_scalar(mod_a[:, kind, :, :], sc, 1.0, None, ALU.add))
                                    dve.tensor_tensor(mod_a[:, kind, :, :], mod_a[:, kind, :, :],
                                                      bc(ln1_t[:, :], 2, NB), ALU.mult).then_inc(mod_ready, 1)
                        dve.wait_ge(row_done, GROUPS)
                        dve.tensor_scalar(mod_row[:, 4 * D:5 * D], mod_row[:, 4 * D:5 * D], 1.0, None, ALU.add).then_inc(row_done, 1)
                        dve.wait_ge(row_done, GROUPS + 1)
                        dve.tensor_tensor(mod_row[:, 4 * D:5 * D], mod_row[:, 4 * D:5 * D], ln2_row[:, :], ALU.mult).then_inc(row_done, 1)

                    @block.tensor
                    def _(pe):
                        pe.wait_ge(s_const, 1)
                        pe.wait_ge(c_silu, 1)
                        for k in range(KC):
                            last = pe.transpose(psum[:, 0, k * NT:(k + 1) * NT], c_row[:, k * P:(k + 1) * P], ident[0:NT, 0:NT])
                        last.then_inc(c_turned, 1)
                        pe.wait_ge(c_t_ready, 1)
                        for g in range(GROUPS):
                            pe.wait_ge(stage_loaded[g % STAGES], 16 * (g // STAGES + 1))
                            if g >= 2:
                                pe.wait_ge(row_done, g - 1)
                            for k in range(KC):
                                last = pe.matmul(psum[0:NT, 1 + g % 2, :], c_t[:, k, :], stage[:, g % STAGES, k, :],
                                                 start=(k == 0), stop=(k == KC - 1))
                            last.then_inc(group_done, 1)
                            if g == 4:
                                pe.wait_ge(row_done, 4)
                                for k in range(2 * KC):
                                    last = pe.transpose(psum[:, 3, k * NT:(k + 1) * NT], mod_row[:, k * P:(k + 1) * P],
                                                        ident[0:NT, 0:NT])
                                last.then_inc(mod_turned, 1)

                b = dict(
                    psum=psum, ident=ident, mix_t=mix_t, w_in_loaded=w_in_loaded, mod_a=mod_a, mod_b=mod_b,
                    x_in=x_in, h_t=h_t, p_qk=p_qk, p_v=p_v, p_q=p_q, p_f=p_f, p_i=p_i, p_g=p_g,
                    norm_w=norm_w, o_norm_w=o_norm_w, level_mask=level_mask, w_in_sb=w_in_sb)
                mixing(nc, b, x, sinks, k_prompt, v_prompt, s_prompt)
            sampling(nc, b, sinks, cache_k, cache_v, state_in, k_sample, v_sample, s_sample)
        b = dict(
            psum=psum, ident=ident, mix_t=mix_t, x2=sb(top, "x2", [P, NT, D]), logit=sb(top, "logit", [P, NT, NE]),
            gate=sb(top, "gates", [P, 2, NT]), list_info=sb(top, "list_info", [1, SLOTS + NE + 1], I32),
            list_from=sb(top, "list_from", [P, SLOTS], I32), list_to=sb(top, "list_to", [P, SLOTS], I32))
        d = dict(
            mod_rows=mod_rows_d, h2=nc.dram_tensor("h2_d", (TABLE, D), F32).ap(),
            list_rows=nc.dram_tensor("list_rows_d", (SLOTS * P, 1), F32).ap(),
            y_rows=nc.dram_tensor("y_rows_d", (2 * TABLE, D), F32).ap())
        output(nc, b, d, x, w_out, w_router)
        route(nc, b, d, router_bias)
        experts(nc, b, d, w_gate, w_up, w_down)
        combine(nc, b, d, y)


OUT_A, OUT_B, M0, M1, M2, M3, PJ0, PJ1 = range(8)
PROJ = (("f", CFB, QW), ("q", CQB, QW), ("qa", CQ, QW), ("kv", CK, 2 * KW), ("i", CIB, QW), ("g", CGB, QW))
NP = len(PROJ)


def slope(h):
    return 2.0 ** (-8.0 * (h + 1) / (NKV * G))


DVE_LINKS = 15


def mixing(nc, b, x, sinks, k_prompt, v_prompt, s_prompt):
    psum, ident, mix_t = b["psum"], b["ident"], b["mix_t"]
    x_in, h_t = b["x_in"], b["h_t"]
    with ExitStack() as ctx:
        def sb(name, shape, dt=F32):
            return ctx.enter_context(nc.sbuf_tensor(name, shape, dt))

        sems = []

        def sem(name):
            sems.append(nc.alloc_semaphore(name))
            return sems[-1]

        ss, rs = sb("ss", [P, 1]), sb("rs", [P, 1])
        qk_ss, qk_rs = sb("qk_ss", [P, 10]), sb("qk_rs", [P, 10])
        eps = sb("eps", [P, 1])
        qk_n = sb("qk_n", [P, QW + KW])
        q_t = sb("q_t", [P, G, P])
        k_t = sb("k_t", [P, 2 * P])
        v_sb = sb("v_sb", [P, 2, KW])
        i_sb = sb("i_sb", [P, QW])
        dist = sb("dist", [P, 2, 2 * P])
        sink = sb("sink", [P, NKV * G])
        score = sb("score", [P, G, 2 * P])
        qk_sq = score[:, :, :].rearrange("p g n -> p (g n)")[:, 0:QW + KW].rearrange("p (h d) -> p h d", d=HD)
        p_t = sb("p_t", [P, 2 * G, P])
        top_s = sb("top_s", [P, G])
        neg_top = sb("neg_top", [P, G])
        sink_e = sb("sink_e", [P, G])
        den = sb("den", [P, NKV, G])
        rec = sb("rec", [P, NKV, G])
        o_a = sb("o_a", [P, G, NKV, HD])
        z_e = sb("z_e", [P, QW])
        log_f = sb("log_f", [P, QW])
        k_b = sb("k_b", [P, QW])
        q_b = sb("q_b", [P, QW])
        cum = sb("cum", [P, QW])
        scan_mask = sb("scan_mask", [P, QW])
        exp_b = sb("exp_b", [P, QW])
        q_e = sb("q_e", [P, QW])
        k_d = sb("k_d", [P, QW])
        kd_tok = z_e
        gap = sb("gap", [P, 2, QW])
        k_l = sb("k_l", [P, 2, QW])
        q_l = sb("q_l", [P, 2, QW // 2])
        pair = sb("pair", [P, 2, 4, P])
        state = sb("state", [P, 4, HD])
        gate = sb("gate", [P, QW])
        gate_e = sb("gate_e", [P, QW])
        o_sq = z_e[:, :].rearrange("p (h d) -> p h d", d=HD)
        o_ss, o_rs = sb("o_ss", [P, 8]), sb("o_rs", [P, 8])
        o_n = log_f

        names = """x_loaded sinks_loaded x_squared x_rs x_normed x_turned h_ready proj_mm proj_out
            act_chain dve_chain pool_chain dist_made state_ready qk_squared qkn_ready qf_turned qk_turned
            z_ready q_ready f_ready k_ready cum_ready expb_ready kgap_ready kexp_ready qt_ready kd_ready
            v_ready i_ready gneg_ready gexp_ready gate_ready
            gap_ready gap_exp lv_ready diag_mm pair_clear lv_mm pair_ready
            score_mm top_ready sinkgap_ready probs_ready probs_turned pt_ready pv_mm oa_ready
            kd_turned kdt_ready state_mm ob_mm osq_ready ob_ready oa_turned ob_turned mix_ready
            stored qkss_ready qk_rs oss_ready o_rs eps_made waits_alone""".split()
        s = {n: sem(n) for n in names}
        ctx.callback(retire, nc, sems)
        block = ctx.enter_context(nc.Block())

        def f4(ap):
            return ap.rearrange("p (c t) -> p c t", t=P)

        def alone(eng):
            eng.sem_inc(s["waits_alone"], 1)

        def inverse_root(squares, out, n, link):
            link(nc.scalar.activation(out, squares, ACT.Ln, scale=1.0 / n, bias=eps[:, :]))
            link(nc.scalar.activation(out, out, ACT.Exp, scale=-0.5))

        def act_norm(act, f):
            act.wait_ge(s["x_loaded"], (f + 1) * 16)
            nc.scalar.activation(p_t[:, :, :].rearrange("p n t -> p (n t)"), x_in[:, :], ACT.Square, accum_out=ss[:, :]).then_inc(s["x_squared"], 1)
            act.wait_ge(s["x_squared"], f + 1)
            inverse_root(ss[:, :], rs[:, :], D, Chain(act, s["x_rs"], 0, f, 2))
            nc.scalar.activation(x_in[:, :], x_in[:, :], ACT.Copy, scale=rs[:, 0:1]).then_inc(s["x_normed"], 1)

        def pe_turn_x(pe, f):
            pe.wait_ge(s["x_normed"], f + 1)
            if not isinstance(f, int) or f > 0:
                pe.wait_ge(s["proj_out"], f * NP)
            for k in range(KC):
                last = pe.transpose(psum[:, PJ0 + k // 4, (k % 4) * P:(k % 4 + 1) * P], x_in[:, k * P:(k + 1) * P], ident[:, :])
            last.then_inc(s["x_turned"], 1)

        def dve_h(dve, f, link):
            kind = bass.ds(f // TP, 1) if not isinstance(f, int) else slice(f // TP, f // TP + 1)
            a = b["mod_a"][:, kind, :, :].rearrange("p a k n -> p (a k) n")
            sh = b["mod_b"][:, kind, :, :].rearrange("p a k n -> p (a k) n")
            dve.wait_ge(s["x_turned"], f + 1)
            h4 = h_t[:, :, :].rearrange("p k (n l) -> p k n l", l=L)
            x4 = psum[:, PJ0:PJ0 + 2, :].rearrange("p a (k n l) -> p (a k) n l", k=4, l=L)
            link(dve.tensor_tensor(h4, x4, bc(a, 3, L), ALU.mult))
            dve.tensor_tensor(h4, h4, bc(sh, 3, L), ALU.add).then_inc(s["h_ready"], 1)

        def pe_project(pe, p, j):
            _, a, n = PROJ[j]
            if j == 0:
                pe.wait_ge(s["h_ready"], p + 1)
            if j >= 2:
                pe.wait_ge(s["proj_out"], p * NP + (j - 1))
            for k in range(KC):
                last = pe.matmul(psum[:, PJ0 + j % 2, 0:n], h_t[:, k, :], b["w_in_sb"][:, k, a:a + n],
                                 start=(k == 0), stop=(k == KC - 1))
            last.then_inc(s["proj_mm"], 1)

        def act_project(act, p, j):
            dst = {"f": b["p_f"][:, :], "q": b["p_q"][:, :], "qa": b["p_qk"][:, 0:QW], "i": b["p_i"][:, :], "g": b["p_g"][:, :]}
            used = {"f": s["qf_turned"], "q": s["qf_turned"], "qa": s["qkn_ready"], "kv": s["v_ready"], "i": s["i_ready"],
                    "g": s["gate_ready"]}
            name, _, n = PROJ[j]
            act.wait_ge(s["proj_mm"], p * NP + (j + 1))
            if not isinstance(p, int):
                act.wait_ge(used[name], p)
            src = psum[:, PJ0 + j % 2, :]
            if name == "kv":
                nc.scalar.activation(b["p_qk"][:, QW:QW + KW], src[:, 0:KW], ACT.Copy)
                nc.scalar.activation(b["p_v"][:, :], src[:, KW:2 * KW], ACT.Copy).then_inc(s["proj_out"], 1)
            else:
                nc.scalar.activation(dst[name], src[:, 0:n], ACT.Copy).then_inc(s["proj_out"], 1)

        @block.sync
        def _(sp):
            sp.dma_start(sink[:, :], sinks.partition_broadcast(P)).then_inc(s["sinks_loaded"], 16)
            for f in range(2):
                if f > 0:
                    sp.wait_ge(s["x_turned"], f)
                sp.dma_start(x_in[:, :], x[f * P:(f + 1) * P, :]).then_inc(s["x_loaded"], 16)
            with sp.Fori(0, TP) as t:
                sp.wait_ge(s["x_turned"], t + 2)
                sp.dma_start(x_in[:, :], x[bass.ds((t + 2) * P, P), :]).then_inc(s["x_loaded"], 16)
            sp.wait_ge(s["state_ready"], TP + 1)
            sp.wait_ge(s["v_ready"], TP)
            sp.dma_start(k_prompt, qk_n[:, QW:QW + KW]).then_inc(s["stored"], 16)
            sp.dma_start(v_prompt, v_sb[:, 1, :]).then_inc(s["stored"], 16)
            for h in range(2):
                sp.dma_start(s_prompt.rearrange("(c h) k v -> h k c v", h=2)[h], state[h * HD:(h + 1) * HD, :, :]).then_inc(s["stored"], 16)
            sp.wait_ge(s["stored"], 4 * 16)

        @block.tensor
        def _(pe):
            for k in range(4):
                pe.wait_ge(b["w_in_loaded"], 16 * (k + 1))
            pe_turn_x(pe, 0)
            for j in range(NP):
                pe_project(pe, 0, j)
            pe_turn_x(pe, 1)

            def turn4(dst, src, done):
                for c in range(4):
                    last = pe.transpose(psum[:, dst, c * P:(c + 1) * P], src[:, c * P:(c + 1) * P], ident[:, :])
                last.then_inc(done, 1)

            def scores(t, kv):
                for g in range(G):
                    last = pe.matmul(psum[:, M2 + g // 2, (g % 2) * 256:(g % 2) * 256 + 256],
                                     q_t[kv * HD:(kv + 1) * HD, g, :], k_t[kv * HD:(kv + 1) * HD, :], start=True, stop=True)
                last.then_inc(s["score_mm"], 1)

            def turn_probs(t, kv):
                pe.wait_ge(s["probs_ready"], t * 2 + (kv + 1))
                for g in range(G):
                    for half in range(2):
                        n = 2 * g + half
                        last = pe.transpose(psum[:, M2 + n // 4, (n % 4) * P:(n % 4 + 1) * P],
                                            score[:, g, half * P:(half + 1) * P], ident[:, :])
                last.then_inc(s["probs_turned"], 1)

            def values(t, kv):
                pe.wait_ge(s["pt_ready"], t * 2 + (kv + 1))
                pe.wait_ge(s["v_ready"], t + 1)
                for g in range(G):
                    col = (g * NKV + kv) * HD
                    for half in range(2):
                        last = pe.matmul(psum[:, OUT_A, col:col + HD], p_t[:, 2 * g + half, :],
                                         v_sb[:, half, kv * HD:(kv + 1) * HD], start=(half == 0), stop=(half == 1))
                last.then_inc(s["pv_mm"], 1)

            def level(t, i):
                pe.wait_ge(s["lv_ready"], t * len(LEVELS) + (i + 1))
                if i >= 1:
                    pe.wait_ge(s["pair_ready"], t * len(LEVELS) + i)
                for h in range(8):
                    r = slice((h % 2) * HD, (h % 2 + 1) * HD)
                    c = h // 2
                    last = pe.matmul(psum[:, M0 + h % 2, c * HD:(c + 1) * HD], k_l[r, i % 2, c * P:(c + 1) * P],
                                     q_l[r, i % 2, c * HD:(c + 1) * HD], start=True, stop=True)
                    if h >= 6:
                        last.then_inc(s["lv_mm"], 1)

            with pe.Fori(0, TP) as t:
                pe.wait_ge(s["proj_out"], t * NP + NP)
                pe.wait_ge(s["state_ready"], t + 1)
                turn4(M0, b["p_q"][:, :], s["qf_turned"])
                turn4(M1, b["p_f"][:, :], s["qf_turned"])
                pe.wait_ge(s["qkn_ready"], t + 1)
                for c in range(5):
                    last = pe.transpose(psum[:, M2 + c // 4, (c % 4) * P:(c % 4 + 1) * P], qk_n[:, c * P:(c + 1) * P], ident[:, :])
                last.then_inc(s["qk_turned"], 1)
                pe_project(pe, t + 1, 0)
                pe.wait_ge(s["q_ready"], t + 1)
                pe.wait_ge(s["k_ready"], t + 1)
                for h in range(8):
                    r = slice((h % 2) * HD, (h % 2 + 1) * HD)
                    c = slice((h // 2) * P, (h // 2 + 1) * P)
                    last = pe.matmul(psum[:, M0 + h % 2, c], k_b[r, c], q_b[r, c], start=True, stop=True)
                    if h >= 6:
                        last.then_inc(s["diag_mm"], 1)
                pe.wait_ge(s["qt_ready"], t + 1)
                scores(t, 0)
                pe_project(pe, t + 1, 1)
                pe.wait_ge(s["pair_clear"], t + 1)
                level(t, 0)
                level(t, 1)
                turn_probs(t, 0)
                pe_project(pe, t + 1, 2)
                level(t, 2)
                values(t, 0)
                scores(t, 1)
                level(t, 3)
                pe_project(pe, t + 1, 3)
                level(t, 4)
                turn_probs(t, 1)
                level(t, 5)
                pe_project(pe, t + 1, 4)
                values(t, 1)
                level(t, 6)
                pe.wait_ge(s["kd_ready"], t + 1)
                turn4(OUT_B, k_d[:, :], s["kd_turned"])
                pe_project(pe, t + 1, 5)
                pe.wait_ge(s["kdt_ready"], t + 1)
                pe.wait_ge(s["i_ready"], t + 1)
                pe.wait_ge(s["pair_ready"], t * len(LEVELS) + len(LEVELS))
                for h in range(8):
                    c = h // 2
                    last = pe.matmul(psum[(h % 2) * HD:(h % 2 + 1) * HD, M1, c * HD:(c + 1) * HD],
                                     kd_tok[:, h * HD:(h + 1) * HD], i_sb[:, h * HD:(h + 1) * HD], start=True, stop=True)
                last.then_inc(s["state_mm"], 1)
                pe.wait_ge(s["oa_ready"], t + 1)
                for h in range(8):
                    c = slice((h // 2) * HD, (h // 2 + 1) * HD)
                    pe.matmul(psum[:, OUT_A + h % 2, c], pair[:, h % 2, h // 2, :], i_sb[:, h * HD:(h + 1) * HD],
                              start=(h < 2), stop=False, skip_group_check=True)
                for h in range(8):
                    r = slice((h % 2) * HD, (h % 2 + 1) * HD)
                    c = slice((h // 2) * HD, (h // 2 + 1) * HD)
                    last = pe.matmul(psum[:, OUT_A + h % 2, c], q_e[r, (h // 2) * P:(h // 2 + 1) * P], state[r, h // 2, :],
                                     start=False, stop=True, skip_group_check=True)
                    if h >= 6:
                        last.then_inc(s["ob_mm"], 1)
                turn4(M2, o_a[:, :, :, :].rearrange("p g k d -> p (g k d)"), s["oa_turned"])
                pe_turn_x(pe, t + 2)
                pe.wait_ge(s["ob_ready"], t + 1)
                turn4(M3, o_n[:, :], s["ob_turned"])

        @block.scalar
        def _(act):
            act.wait_ge(s["eps_made"], 1)
            for f in range(2):
                act_norm(act, f)
                if f == 0:
                    for j in range(NP):
                        act_project(act, 0, j)

            def probs(t, kv):
                act.wait_ge(s["top_ready"], t * 2 + (kv + 1))
                for g in range(G):
                    nc.scalar.activation(score[:, g, :], score[:, g, :], ACT.Exp, bias=neg_top[:, g:g + 1],
                                         accum_out=den[:, kv, g:g + 1])
                act.wait_ge(s["sinkgap_ready"], t * 2 + (kv + 1))
                nc.scalar.activation(sink_e[:, :], sink_e[:, :], ACT.Exp).then_inc(s["probs_ready"], 1)

            def copy_probs(t, kv):
                act.wait_ge(s["probs_turned"], t * 2 + (kv + 1))
                nc.scalar.activation(p_t[:, :, :], psum[:, M2:M2 + 2, :].rearrange("p a (n t) -> p (a n) t", t=P),
                                     ACT.Copy).then_inc(s["pt_ready"], 1)

            def gap_exp(t, i):
                act.wait_ge(s["gap_ready"], t * len(LEVELS) + (i + 1))
                nc.scalar.activation(gap[:, i % 2, :], gap[:, i % 2, :], ACT.Exp).then_inc(s["gap_exp"], 1)

            with act.Fori(0, TP) as t:
                link = Chain(act, s["act_chain"], 0, t, 3)
                act.wait_ge(s["proj_out"], t * NP + NP)
                nc.scalar.activation(qk_sq[:, :, :].rearrange("p h d -> p (h d)"), b["p_qk"][:, :], ACT.Square).then_inc(s["qk_squared"], 1)
                act.wait_ge(s["qkss_ready"], t + 1)
                inverse_root(qk_ss[:, :], qk_rs[:, :], HD, Chain(act, s["qk_rs"], 0, t, 2))
                act.wait_ge(s["qf_turned"], t * 2 + 2)
                link(nc.scalar.activation(z_e[:, :], psum[:, M1, :], ACT.Abs))
                link(nc.scalar.activation(z_e[:, :], z_e[:, :], ACT.Exp, scale=-1.0))
                nc.scalar.activation(z_e[:, :], z_e[:, :], ACT.Ln, bias=1.0).then_inc(s["z_ready"], 1)
                nc.scalar.activation(q_b[:, :], psum[:, M0, :], ACT.Copy, scale=HD ** -0.5).then_inc(s["q_ready"], 1)
                act.wait_ge(s["qk_turned"], t + 1)
                nc.scalar.activation(q_t[:, :, :], f4(psum[:, M2, :]), ACT.Copy)
                link(nc.scalar.activation(k_t[:, 0:P], k_t[:, P:2 * P], ACT.Copy))
                nc.scalar.activation(k_t[:, P:2 * P], psum[:, M3, 0:P], ACT.Copy).then_inc(s["qt_ready"], 1)
                act.wait_ge(s["f_ready"], t + 1)
                nc.scalar.activation(k_b[:, :], k_b[:, :], ACT.Exp).then_inc(s["k_ready"], 1)
                gap_exp(t, 0)
                act_project(act, t + 1, 0)
                act.wait_ge(s["cum_ready"], t + 1)
                nc.scalar.activation(exp_b[:, :], cum[:, :], ACT.Exp).then_inc(s["expb_ready"], 1)
                act.wait_ge(s["kgap_ready"], t + 1)
                nc.scalar.activation(k_d[:, :], k_d[:, :], ACT.Exp).then_inc(s["kexp_ready"], 1)
                gap_exp(t, 1)
                act.wait_ge(s["gneg_ready"], t + 1)
                glink = Chain(act, s["gexp_ready"], 0, t, 3)
                glink(nc.scalar.activation(gate_e[:, :], gate_e[:, :], ACT.Exp, scale=-1.0))
                glink(nc.scalar.activation(gate_e[:, :], gate_e[:, :], ACT.Ln, bias=1.0))
                glink(nc.scalar.activation(gate_e[:, :], gate_e[:, :], ACT.Exp, scale=-1.0))
                act_norm(act, t + 2)
                act_project(act, t + 1, 1)
                probs(t, 0)
                gap_exp(t, 2)
                copy_probs(t, 0)
                act_project(act, t + 1, 2)
                gap_exp(t, 3)
                probs(t, 1)
                act_project(act, t + 1, 3)
                gap_exp(t, 4)
                copy_probs(t, 1)
                gap_exp(t, 5)
                act_project(act, t + 1, 4)
                gap_exp(t, 6)
                act.wait_ge(s["kd_turned"], t + 1)
                nc.scalar.activation(kd_tok[:, :], psum[:, OUT_B, :], ACT.Copy).then_inc(s["kdt_ready"], 1)
                act_project(act, t + 1, 5)
                act.wait_ge(s["ob_mm"], t * 2 + 2)
                nc.scalar.activation(o_sq.rearrange("p (a c) d -> p a (c d)", a=2), psum[:, OUT_A:OUT_B + 1, 0:4 * HD],
                                     ACT.Square).then_inc(s["osq_ready"], 1)
                act.wait_ge(s["oss_ready"], t + 1)
                inverse_root(o_ss[:, :], o_rs[:, :], HD, Chain(act, s["o_rs"], 0, t, 2))
                mix_cur = mix_t[:, bass.ds(t, 1), :, :].rearrange("p a k r -> p (a k) r")
                act.wait_ge(s["oa_turned"], t + 1)
                nc.scalar.activation(mix_cur[:, 0:4, :], f4(psum[:, M2, :]), ACT.Copy)
                act.wait_ge(s["ob_turned"], t + 1)
                nc.scalar.activation(mix_cur[:, 4:8, :], f4(psum[:, M3, :]), ACT.Copy).then_inc(s["mix_ready"], 1)
                link.done()

        @block.vector
        def _(dve):
            start = Chain(dve, s["state_ready"])
            dve.memset(eps[:, :], EPS).then_inc(s["eps_made"], 1)
            dve.memset(k_t[:, :], 0.0)
            dve.memset(v_sb[:, :, :], 0.0)
            dve.memset(scan_mask[:, :], 1.0)
            link = Chain(dve, s["dve_chain"])
            dve.wait_ge(s["dist_made"], 1)
            link(dve.scalar_tensor_tensor(out=dist[:, 1, :], in0=dist[:, 0, :], scalar=-1.0, in1=dist[:, 0, :],
                                          op0=ALU.mult, op1=ALU.max))
            dve.memset(dist[0:HD, 1, P + HD:2 * P], FAR)
            link(dve.memset(dist[HD:P, 1, 0:HD], FAR))
            link(dve.tensor_copy(dist[:, 0, :], dist[:, 1, :]))
            dve.memset(dist[:, 0, 0:P], FAR)
            link(dve.memset(f4(scan_mask[:, :])[:, :, 0:1], 0.0))
            start(dve.memset(state[:, :, :], 0.0))
            base = link.k
            for f in range(2):
                n = Chain(dve, s["dve_chain"], base)
                dve_h(dve, f, n)
                base += n.k

            def gaps(t, i):
                h = LEVELS[i]
                if i >= 2:
                    dve.wait_ge(s["lv_ready"], t * len(LEVELS) + (i - 1))
                c = cum[:, :].rearrange("p (n two h) -> p n two h", two=2, h=h)
                g = gap[:, i % 2, :].rearrange("p (n two h) -> p n two h", two=2, h=h)
                mid = last_bc(c[:, :, 0, h - 1:h], h)
                dve.tensor_tensor(g[:, :, 0, :], mid, c[:, :, 0, :], ALU.subtract)
                dve.tensor_tensor(g[:, :, 1, :], c[:, :, 1, :], mid, ALU.subtract).then_inc(s["gap_ready"], 1)

            def decayed(t, i):
                h = LEVELS[i]
                dve.wait_ge(s["gap_exp"], t * len(LEVELS) + (i + 1))
                if i >= 2:
                    dve.wait_ge(s["lv_mm"], t * 2 * len(LEVELS) + 2 * (i - 1))
                second = lambda a: a.rearrange("p (n two h) -> p n two h", two=2, h=h)[:, :, 1, :]
                dve.tensor_tensor(k_l[:, i % 2, :], k_b[:, :], gap[:, i % 2, :], ALU.mult)
                dve.tensor_tensor(q_l[:, i % 2, :].rearrange("p (n h) -> p n h", h=h), second(q_b[:, :]),
                                  second(gap[:, i % 2, :]), ALU.mult).then_inc(s["lv_ready"], 1)

            def place(t, i):
                h = LEVELS[i]
                dve.wait_ge(s["lv_mm"], t * 2 * len(LEVELS) + 2 * (i + 1))
                alone(dve)
                for a in range(2):
                    out = pair[:, a, :, :].rearrange("p e (n two h) -> p e n two h", two=2, h=h)[:, :, :, 1, :]
                    m = bc(b["level_mask"][:, i, :].rearrange("p (n h) -> p n h", h=h).bitcast(I32), 1, 4)
                    src = psum[:, M0 + a, 0:4 * HD].rearrange("p (e n h) -> p e n h", e=4, h=h)
                    last = dve.copy_predicated(out, m, src)
                last.then_inc(s["pair_ready"], 1)

            def tops(t, kv, link):
                dve.wait_ge(s["score_mm"], t * 2 + (kv + 1))
                first = bass.ds((t + (TP - 1)) // TP, 1)
                d = dist[:, first, :].rearrange("p a n -> p (a n)")
                for g in range(G):
                    ins = dve.scalar_tensor_tensor(out=score[:, g, :], in0=d, scalar=-slope(kv * G + g),
                                                   in1=psum[:, M2 + g // 2, (g % 2) * 256:(g % 2) * 256 + 256],
                                                   op0=ALU.mult, op1=ALU.add)
                link(ins)
                link(dve.tensor_reduce(top_s[:, :], score[:, :, :], AX_X, ALU.max))
                link(dve.tensor_tensor(top_s[:, :], top_s[:, :], sink[:, kv * G:(kv + 1) * G], ALU.max))
                dve.tensor_scalar(neg_top[:, :], top_s[:, :], -1.0, None, ALU.mult).then_inc(s["top_ready"], 1)
                dve.tensor_tensor(sink_e[:, :], sink[:, kv * G:(kv + 1) * G], top_s[:, :], ALU.subtract).then_inc(s["sinkgap_ready"], 1)

            def denominators(t, kv, link):
                dve.wait_ge(s["probs_ready"], t * 2 + (kv + 1))
                link(dve.tensor_tensor(den[:, kv, :], den[:, kv, :], sink_e[:, :], ALU.add))
                link(dve.reciprocal(rec[:, kv, :], den[:, kv, :]))

            with dve.Fori(0, TP) as t:
                link = Chain(dve, s["dve_chain"], base, t, DVE_LINKS)
                dve.wait_ge(s["qk_squared"], t + 1)
                dve.tensor_reduce(qk_ss[:, :], qk_sq[:, :, :], AX_X, ALU.add).then_inc(s["qkss_ready"], 1)
                dve.wait_ge(s["qk_rs"], t * 2 + 2)
                link(dve.tensor_tensor(qk_sq[:, :, :], b["p_qk"][:, :].rearrange("p (h d) -> p h d", d=HD), bc(qk_rs[:, :], 2, HD), ALU.mult))
                dve.tensor_tensor(qk_n[:, 0:QW].rearrange("p (g k d) -> p k g d", g=G, d=HD),
                                  qk_sq[:, 0:8, :].rearrange("p (k g) d -> p k g d", g=G),
                                  b["norm_w"][:, 0:8, :].rearrange("p (k g) d -> p k g d", g=G), ALU.mult)
                dve.tensor_tensor(qk_n[:, QW:QW + KW].rearrange("p (k d) -> p k d", d=HD), qk_sq[:, 8:10, :],
                                  b["norm_w"][:, 8:10, :], ALU.mult).then_inc(s["qkn_ready"], 1)
                dve.wait_ge(s["z_ready"], t + 1)
                link(dve.scalar_tensor_tensor(out=log_f[:, :], in0=psum[:, M1, :], scalar=0.0, in1=z_e[:, :],
                                              op0=ALU.min, op1=ALU.subtract))
                dve.tensor_tensor(k_b[:, :], log_f[:, :], psum[:, M1, :], ALU.subtract).then_inc(s["f_ready"], 1)
                dve.tensor_tensor_scan(cum[:, :], scan_mask[:, :], log_f[:, :], 0.0, ALU.mult, ALU.add).then_inc(s["cum_ready"], 1)
                dve.wait_ge(s["cum_ready"], t + 1)
                gaps(t, 0)
                dve.tensor_tensor(f4(k_d[:, :]), last_bc(f4(cum[:, :])[:, :, P - 1:P], P), f4(cum[:, :]), ALU.subtract).then_inc(s["kgap_ready"], 1)
                gaps(t, 1)
                dve.wait_ge(s["k_ready"], t + 1)
                dve.wait_ge(s["q_ready"], t + 1)
                decayed(t, 0)
                dve.wait_ge(s["diag_mm"], t * 2 + 2)
                dve.tensor_tensor(pair[:, :, :, :].rearrange("p a h t -> p (a h) t"), psum[:, M0:M0 + 2, :].rearrange("p a (h t) -> p (a h) t", t=P),
                                  bc(ident[:, :], 1, 8), ALU.mult).then_inc(s["pair_clear"], 1)
                gaps(t, 2)
                decayed(t, 1)
                tops(t, 0, link)
                dve.wait_ge(s["pair_clear"], t + 1)
                place(t, 0)
                place(t, 1)
                gaps(t, 3)
                decayed(t, 2)
                denominators(t, 0, link)
                place(t, 2)
                decayed(t, 3)
                gaps(t, 4)
                tops(t, 1, link)
                place(t, 3)
                decayed(t, 4)
                gaps(t, 5)
                place(t, 4)
                decayed(t, 5)
                gaps(t, 6)
                denominators(t, 1, link)
                place(t, 5)
                decayed(t, 6)
                dve.wait_ge(s["pv_mm"], t * 2 + 2)
                dve.tensor_tensor(o_a[:, :, :, :], psum[:, OUT_A, :].rearrange("p (g k d) -> p g k d", g=G, d=HD),
                                  bc(rec[:, :, :].rearrange("p k g -> p g k"), 3, HD), ALU.mult).then_inc(s["oa_ready"], 1)
                place(t, 6)
                dve.wait_ge(s["osq_ready"], t + 1)
                dve.tensor_reduce(o_ss[:, :], o_sq[:, :, :], AX_X, ALU.add).then_inc(s["oss_ready"], 1)
                dve.wait_ge(s["o_rs"], t * 2 + 2)
                for a in range(2):
                    ins = dve.tensor_tensor(o_n[:, :].rearrange("p (c a d) -> p a c d", a=2, d=HD)[:, a],
                                            psum[:, OUT_A + a, 0:4 * HD].rearrange("p (c d) -> p c d", d=HD),
                                            bc(o_rs[:, 4 * a:4 * a + 4], 2, HD), ALU.mult)
                link(ins)
                dve.wait_ge(s["gate_ready"], t + 1)
                dve.tensor_tensor(o_n[:, :], o_n[:, :], gate[:, :], ALU.mult).then_inc(s["ob_ready"], 1)
                link(dve.tensor_tensor(state[:, :, :], state[:, :, :],
                                       last_bc(f4(exp_b[:, :])[:, :, P - 1:P], HD), ALU.mult))
                dve.tensor_tensor(state[:, :, :], state[:, :, :], psum[:, M1, 0:4 * HD].rearrange("p (c v) -> p c v", v=HD),
                                  ALU.add).then_inc(s["state_ready"], 1)
                dve_h(dve, t + 2, link)
                link.done()

        @block.gpsimd
        def _(pool):
            pool.iota(dist[:, 0, :], pattern=[[-1, 2 * P]], base=P, channel_multiplier=1,
                      allow_small_or_imprecise_dtypes=True).then_inc(s["dist_made"], 1)
            with pool.Fori(0, TP) as t:
                link = Chain(pool, s["pool_chain"], 0, t, 2)
                pool.wait_ge(s["proj_out"], t * NP + NP)
                alone(pool)
                pool.tensor_scalar(gate_e[:, :], b["p_g"][:, :], -87.0, None, ALU.max).then_inc(s["gneg_ready"], 1)
                pool.wait_ge(s["qk_turned"], t + 1)
                alone(pool)
                link(pool.tensor_copy(v_sb[:, 0, :], v_sb[:, 1, :]))
                alone(pool)
                pool.tensor_copy(v_sb[:, 1, :], b["p_v"][:, :]).then_inc(s["v_ready"], 1)
                pool.tensor_copy(i_sb[:, :], b["p_i"][:, :]).then_inc(s["i_ready"], 1)
                pool.wait_ge(s["expb_ready"], t + 1)
                pool.wait_ge(s["q_ready"], t + 1)
                pool.tensor_tensor(q_e[:, :], q_b[:, :], exp_b[:, :], ALU.mult)
                pool.wait_ge(s["kexp_ready"], t + 1)
                pool.wait_ge(s["k_ready"], t + 1)
                pool.tensor_tensor(k_d[:, :], k_b[:, :], k_d[:, :], ALU.mult).then_inc(s["kd_ready"], 1)
                pool.wait_ge(s["gexp_ready"], t * 3 + 3)
                link(pool.tensor_tensor(gate[:, :], b["p_g"][:, :], gate_e[:, :], ALU.mult))
                g3 = gate[:, :].rearrange("p (h d) -> p h d", d=HD)
                pool.tensor_tensor(g3, g3, bc(b["o_norm_w"][:, :], 1, 8), ALU.mult).then_inc(s["gate_ready"], 1)
                link.done()



def sampling(nc, b, sinks, cache_k, cache_v, state_in, k_sample, v_sample, s_sample):
    psum, ident, mix_t = b["psum"], b["ident"], b["mix_t"]
    KS = WIN + L
    BP = NB // 2
    FIRST_LEVEL = LEVELS.index(L // 2)
    NL = len(LEVELS) - FIRST_LEVEL
    with ExitStack() as ctx:
        def sb(name, shape, dt=F32):
            return ctx.enter_context(nc.sbuf_tensor("s_" + name, shape, dt))

        def sem(name):
            return ctx.enter_context(nc.semaphore("s_" + name))

        cache_k_sb = sb("cache_k_sb", [P, NB, KW])
        cache_v_sb = sb("cache_v_sb", [P, NB, KW])
        v_new = sb("v_new", [L, NB, KW])
        state = sb("state", [P, 4, NB, HD])
        sink = sb("sink", [P, NKV])
        rows_i = sb("rows_i", [P, 4], I32)
        frame = sb("frame", [P, 1])
        slope_p = sb("slope_p", [P, 1])
        dist = sb("dist", [P, KS])
        dist_n = sb("dist_n", [P, KS])
        penalty = sb("penalty", [P, NKV, KS])
        sq = sb("sq", [P, 10, HD])
        ss, rs = sb("ss", [P, 10]), sb("rs", [P, 10])
        eps = sb("eps", [P, 1])
        qk_n = sb("qk_n", [P, QW + KW])
        q_t = sb("q_t", [P, NB, G * L])
        k_new_t = sb("k_new_t", [P, P])
        cache_t = sb("cache_t", [P, NB, P])
        score = sb("score", [P, NKV, BP, KS])
        top_s, neg_top, sink_e = (sb(n, [P, NKV, BP]) for n in ("top_s", "neg_top", "sink_e"))
        den, rec = sb("den", [P, NKV, BP]), sb("rec", [P, NKV, BP])
        pc_t = sb("pc_t", [P, 8, P])
        pn_t = sb("pn_t", [L, 8, P])
        o_a = sb("o_a", [P, BP, NKV, HD])
        z_e, log_f, k_b, q_b, cum, scan_mask, exp_b, q_e, k_d, kd_tok, gate, gate_e, o_n = (
            sb(n, [P, QW]) for n in "z_e log_f k_b q_b cum scan_mask exp_b q_e k_d kd_tok gate gate_e o_n".split())
        gap, k_l = sb("gap", [P, NL, QW]), sb("k_l", [P, NL, QW])
        q_l = sb("q_l", [P, NL, QW // 2])
        pair = sb("pair", [P, 2, 4, P])
        row_of = sb("row_of", [P, NB])
        q_m = sb("q_m", [P, 4, NB * (P + L)])
        i_m = sb("i_m", [P, 8, NB, HD])
        o_sq = sb("o_sq", [P, 8, HD])
        o_ss, o_rs = sb("o_ss", [P, 8]), sb("o_rs", [P, 8])

        names = """cache_loaded cachev_loaded sink_loaded state_loaded vnew_loaded consts act_chain dve_chain pool_chain rows_made
            q_squared ss_ready qk_rs qkn_ready cache_turned qk_turned qf_turned cache_t_ready qt_ready z_ready
            q_ready f_ready k_ready cum_ready expb_ready kgap_ready kexp_ready qe_ready kd_ready
            gneg_ready gate_exp gate_ready gap_ready gap_exp lv_ready diag_mm pair_clear lv_mm pair_ready score_mm
            top_ready probs_ready pc_turned pt_ready pv_mm oa_ready kd_turned kdt_ready im_ready state_mm
            ob_mm osq_ready oss_ready o_rs ob_ready oa_turned ob_turned state_ready stored penalty_ready""".split()
        s = {n: sem(n) for n in names}
        block = ctx.enter_context(nc.Block())

        def f4(ap):
            return ap.rearrange("p (c t) -> p c t", t=P)

        def by_request(ap):
            return ap.rearrange("p (n l) -> p n l", l=L)

        @block.sync
        def _(sp):
            sp.dma_start(cache_k_sb[:, :, :], cache_k.rearrange("b r n -> r b n")).then_inc(s["cache_loaded"], 16)
            for n in range(NB):
                sp.dma_start(v_new[:, n, :], b["p_v"][n * L:(n + 1) * L, :]).then_inc(s["vnew_loaded"], 16)
            with nc.allow_non_contiguous_dma("one sink a row"):
                for par in range(2):
                    for g in range(G):
                        r = slice(par * HD + g * L, par * HD + (g + 1) * L)
                        sp.dma_start(sink[r, :], sinks.rearrange("(k g) -> g k", g=G)[g].partition_broadcast(L)).then_inc(s["sink_loaded"], 16)
            for n in range(NB):
                for h in range(2):
                    sp.dma_start(state[h * HD:(h + 1) * HD, :, n, :],
                                 state_in[n].rearrange("(c h) k v -> h k c v", h=2)[h]).then_inc(s["state_loaded"], 16)
            sp.dma_start(cache_v_sb[:, :, :], cache_v.rearrange("b r n -> r b n")).then_inc(s["cachev_loaded"], 16)
            sp.dma_start(v_sample, b["p_v"][:, :]).then_inc(s["stored"], 16)
            sp.wait_ge(s["qkn_ready"], 1)
            sp.dma_start(k_sample, qk_n[:, QW:QW + KW]).then_inc(s["stored"], 16)
            sp.wait_ge(s["state_ready"], 1)
            for n in range(NB):
                for h in range(2):
                    sp.dma_start(s_sample[n].rearrange("(c h) k v -> h k c v", h=2)[h],
                                 state[h * HD:(h + 1) * HD, :, n, :]).then_inc(s["stored"], 16)
            sp.wait_ge(s["stored"], 18 * 16)

        @block.gpsimd
        def _(pool):
            link = Chain(pool, s["pool_chain"])
            pool.iota(rows_i[:, 0:1], pattern=[[0, 1]], base=0, channel_multiplier=1).then_inc(s["rows_made"], 1)
            pool.iota(dist[:, :], pattern=[[-1, KS]], base=WIN, channel_multiplier=0,
                      allow_small_or_imprecise_dtypes=True).then_inc(s["rows_made"], 1)
            link(pool.memset(row_of[:, :], 1.0))
            link(pool.affine_select(out=row_of[:, :], in_=row_of[:, :], compare_op=ALU.is_ge, fill=0.0, base=0,
                                    pattern=[[-L, NB]], channel_multiplier=1))
            link(pool.affine_select(out=row_of[:, :], in_=row_of[:, :], compare_op=ALU.is_ge, fill=0.0, base=L - 1,
                                    pattern=[[L, NB]], channel_multiplier=-1))
            pool.tensor_scalar(gate_e[:, :], b["p_g"][:, :], -87.0, None, ALU.max).then_inc(s["gneg_ready"], 1)
            link(pool.memset(q_m[:, :, :], 0.0))
            for h in range(8):
                ins = pool.tensor_tensor(i_m[:, h, :, :], bc(b["p_i"][:, h * HD:(h + 1) * HD], 1, NB),
                                         bc(row_of[:, :], 2, HD), ALU.mult)
            ins.then_inc(s["im_ready"], 1)
            pool.wait_ge(s["expb_ready"], 1)
            pool.wait_ge(s["q_ready"], 1)
            for c in range(4):
                ins = pool.tensor_tensor(q_m[:, c, :].rearrange("p (n w) -> p n w", w=P + L)[:, :, 0:L],
                                         by_request(q_b[:, c * P:(c + 1) * P]), by_request(exp_b[:, c * P:(c + 1) * P]), ALU.mult)
            ins.then_inc(s["qe_ready"], 1)
            pool.wait_ge(s["kexp_ready"], 1)
            pool.wait_ge(s["k_ready"], 1)
            pool.tensor_tensor(k_d[:, :], k_b[:, :], k_d[:, :], ALU.mult).then_inc(s["kd_ready"], 1)
            pool.wait_ge(s["gate_exp"], 3)
            link(pool.tensor_tensor(gate[:, :], b["p_g"][:, :], gate_e[:, :], ALU.mult))
            g3 = gate[:, :].rearrange("p (h d) -> p h d", d=HD)
            pool.tensor_tensor(g3, g3, bc(b["o_norm_w"][:, :], 1, 8), ALU.mult).then_inc(s["gate_ready"], 1)

        @block.tensor
        def _(pe):
            for c in range(4):
                pe.transpose(psum[:, PJ0, c * P:(c + 1) * P], b["p_q"][:, c * P:(c + 1) * P], ident[:, :])
            for c in range(4):
                last = pe.transpose(psum[:, PJ1, c * P:(c + 1) * P], b["p_f"][:, c * P:(c + 1) * P], ident[:, :])
            last.then_inc(s["qf_turned"], 1)
            pe.wait_ge(s["cache_loaded"], 16)
            for n in range(NB):
                last = pe.transpose(psum[:, M0 + n // 4, (n % 4) * P:(n % 4 + 1) * P], cache_k_sb[:, n, :], ident[:, :])
            last.then_inc(s["cache_turned"], 1)
            pe.wait_ge(s["qkn_ready"], 1)
            for c in range(5):
                last = pe.transpose(psum[:, M2 + c // 4, (c % 4) * P:(c % 4 + 1) * P], qk_n[:, c * P:(c + 1) * P], ident[:, :])
            last.then_inc(s["qk_turned"], 1)
            pe.wait_ge(s["cache_t_ready"], 1)
            pe.wait_ge(s["qt_ready"], 1)
            for kv in range(NKV):
                r = slice(kv * HD, (kv + 1) * HD)
                for n in range(NB):
                    bp, par = n // 2, n % 2
                    o = psum[par * HD:(par + 1) * HD, M0 + 2 * kv + bp // 2, (bp % 2) * 256:(bp % 2) * 256 + KS]
                    q = q_t[r, n, :]
                    pe.matmul(o[:, 0:WIN], q, cache_t[r, n, :], start=True, stop=True)
                    last = pe.matmul(o[:, WIN:KS], q, k_new_t[r, n * L:(n + 1) * L], start=True, stop=True)
                last.then_inc(s["score_mm"], 1)
            pe.wait_ge(s["q_ready"], 1)
            pe.wait_ge(s["k_ready"], 1)
            for h in range(8):
                r = slice((h % 2) * HD, (h % 2 + 1) * HD)
                c = slice((h // 2) * P, (h // 2 + 1) * P)
                last = pe.matmul(psum[:, PJ0 + h % 2, c], k_b[r, c], q_b[r, c], start=True, stop=True)
                if h >= 6:
                    last.then_inc(s["diag_mm"], 1)

            def level(i):
                pe.wait_ge(s["lv_ready"], i + 1)
                if i == 0:
                    pe.wait_ge(s["pair_clear"], 1)
                else:
                    pe.wait_ge(s["pair_ready"], i)
                for h in range(8):
                    r = slice((h % 2) * HD, (h % 2 + 1) * HD)
                    c = h // 2
                    last = pe.matmul(psum[:, PJ0 + h % 2, c * HD:(c + 1) * HD], k_l[r, i, c * P:(c + 1) * P],
                                     q_l[r, i, c * HD:(c + 1) * HD], start=True, stop=True)
                    if h >= 6:
                        last.then_inc(s["lv_mm"], 1)

            level(0)
            level(1)
            pe.wait_ge(s["probs_ready"], 1)
            for n in range(8):
                kv, bp = n // BP, n % BP
                last = pe.transpose(psum[:, M0 + n // 4, (n % 4) * P:(n % 4 + 1) * P], score[:, kv, bp, 0:WIN], ident[:, :])
            for n in range(8):
                kv, bp = n // BP, n % BP
                last = pe.transpose(psum[0:L, M2 + n // 4, (n % 4) * P:(n % 4 + 1) * P], score[:, kv, bp, WIN:KS], ident[:, :])
            last.then_inc(s["pc_turned"], 1)
            level(2)
            level(3)
            pe.wait_ge(s["pt_ready"], 2)
            pe.wait_ge(s["cachev_loaded"], 16)
            pe.wait_ge(s["vnew_loaded"], NB * 16)
            for n in range(8):
                kv, bp = n // BP, n % BP
                v = slice(kv * HD, (kv + 1) * HD)
                for par in range(2):
                    q = slice(par * HD, (par + 1) * HD)
                    o = psum[q, OUT_A, n * HD:(n + 1) * HD]
                    pe.matmul(o, pc_t[:, n, q], cache_v_sb[:, 2 * bp + par, v], start=True, stop=False)
                    last = pe.matmul(o, pn_t[:, n, q], v_new[:, 2 * bp + par, v], start=False, stop=True)
            last.then_inc(s["pv_mm"], 1)
            pe.wait_ge(s["kd_ready"], 1)
            for c in range(4):
                last = pe.transpose(psum[:, OUT_B, c * P:(c + 1) * P], k_d[:, c * P:(c + 1) * P], ident[:, :])
            last.then_inc(s["kd_turned"], 1)
            pe.wait_ge(s["kdt_ready"], 1)
            pe.wait_ge(s["im_ready"], 1)
            pe.wait_ge(s["pair_ready"], NL)
            for h in range(8):
                last = pe.matmul(psum[(h % 2) * HD:(h % 2 + 1) * HD, M0 + h // 2, :], kd_tok[:, h * HD:(h + 1) * HD],
                                 i_m[:, h, :, :].rearrange("p n v -> p (n v)"), start=True, stop=True)
            last.then_inc(s["state_mm"], 1)
            pe.wait_ge(s["oa_ready"], 1)
            pe.wait_ge(s["qe_ready"], 1)
            pe.wait_ge(s["state_loaded"], 2 * NB * 16)
            for h in range(8):
                c = slice((h // 2) * HD, (h // 2 + 1) * HD)
                pe.matmul(psum[:, PJ0 + h % 2, c], pair[:, h % 2, h // 2, :], b["p_i"][:, h * HD:(h + 1) * HD],
                          start=(h < 2), stop=False, skip_group_check=True)
            for n in range(NB):
                for h in range(8):
                    r = slice((h % 2) * HD, (h % 2 + 1) * HD)
                    c = slice((h // 2) * HD, (h // 2 + 1) * HD)
                    last = pe.matmul(psum[:, PJ0 + h % 2, c], q_m[r, h // 2, n * P:(n + 1) * P], state[r, h // 2, n, :],
                                     start=False, stop=(n == NB - 1), skip_group_check=True)
                    if n == NB - 1 and h >= 6:
                        last.then_inc(s["ob_mm"], 1)
            for bp in range(BP):
                last = pe.transpose(psum[:, OUT_A, bp * P:(bp + 1) * P], o_a[:, bp, :, :].rearrange("p k d -> p (k d)"), ident[:, :])
            last.then_inc(s["oa_turned"], 1)
            pe.wait_ge(s["ob_ready"], 1)
            for c in range(4):
                last = pe.transpose(psum[:, OUT_B, c * P:(c + 1) * P], o_n[:, c * P:(c + 1) * P], ident[:, :])
            last.then_inc(s["ob_turned"], 1)

        @block.scalar
        def _(act):
            a = nc.scalar.activation
            link = Chain(act, s["act_chain"])

            def inverse_root(squares, out, n, link):
                link(a(out, squares, ACT.Ln, scale=1.0 / n, bias=eps[:, :]))
                link(a(out, out, ACT.Exp, scale=-0.5))

            a(sq[:, :, :].rearrange("p h d -> p (h d)"), b["p_qk"][:, :], ACT.Square).then_inc(s["q_squared"], 1)
            act.wait_ge(s["qf_turned"], 1)
            link(a(z_e[:, :], psum[:, PJ1, :], ACT.Abs))
            link(a(z_e[:, :], z_e[:, :], ACT.Exp, scale=-1.0))
            a(z_e[:, :], z_e[:, :], ACT.Ln, bias=1.0).then_inc(s["z_ready"], 1)
            a(q_b[:, :], psum[:, PJ0, :], ACT.Copy, scale=HD ** -0.5).then_inc(s["q_ready"], 1)
            act.wait_ge(s["consts"], 1)
            act.wait_ge(s["ss_ready"], 1)
            inverse_root(ss[:, :], rs[:, :], HD, Chain(act, s["qk_rs"]))
            act.wait_ge(s["cache_turned"], 1)
            a(cache_t[:, :, :], psum[:, M0:M0 + 2, :].rearrange("p a (n t) -> p (a n) t", t=P), ACT.Copy).then_inc(s["cache_t_ready"], 1)
            act.wait_ge(s["f_ready"], 1)
            a(k_b[:, :], k_b[:, :], ACT.Exp).then_inc(s["k_ready"], 1)
            act.wait_ge(s["qk_turned"], 1)
            a(q_t[:, :, :].rearrange("p n (g l) -> p g n l", g=G), psum[:, M2, :].rearrange("p (g n l) -> p g n l", g=G, l=L), ACT.Copy)
            a(k_new_t[:, :], psum[:, M3, 0:P], ACT.Copy).then_inc(s["qt_ready"], 1)
            for i in range(NL):
                act.wait_ge(s["gap_ready"], i + 1)
                a(gap[:, i, :], gap[:, i, :], ACT.Exp).then_inc(s["gap_exp"], 1)
            act.wait_ge(s["cum_ready"], 1)
            a(exp_b[:, :], cum[:, :], ACT.Exp).then_inc(s["expb_ready"], 1)
            act.wait_ge(s["kgap_ready"], 1)
            a(k_d[:, :], k_d[:, :], ACT.Exp).then_inc(s["kexp_ready"], 1)
            act.wait_ge(s["top_ready"], 2)
            for n in range(8):
                kv, bp = n // BP, n % BP
                a(score[:, kv, bp, :], score[:, kv, bp, :], ACT.Exp, bias=neg_top[:, kv, bp:bp + 1],
                  accum_out=den[:, kv, bp:bp + 1])
            a(sink_e[:, :, :], sink_e[:, :, :], ACT.Exp).then_inc(s["probs_ready"], 1)
            act.wait_ge(s["pc_turned"], 1)
            a(pc_t[:, :, :], psum[:, M0:M0 + 2, :].rearrange("p a (n t) -> p (a n) t", t=P), ACT.Copy).then_inc(s["pt_ready"], 1)
            a(pn_t[:, :, :], psum[0:L, M2:M2 + 2, :].rearrange("p a (n t) -> p (a n) t", t=P), ACT.Copy).then_inc(s["pt_ready"], 1)
            act.wait_ge(s["gneg_ready"], 1)
            glink = Chain(act, s["gate_exp"])
            glink(a(gate_e[:, :], gate_e[:, :], ACT.Exp, scale=-1.0))
            glink(a(gate_e[:, :], gate_e[:, :], ACT.Ln, bias=1.0))
            glink(a(gate_e[:, :], gate_e[:, :], ACT.Exp, scale=-1.0))
            act.wait_ge(s["kd_turned"], 1)
            a(kd_tok[:, :], psum[:, OUT_B, :], ACT.Copy).then_inc(s["kdt_ready"], 1)
            act.wait_ge(s["ob_mm"], 2)
            a(o_sq[:, :, :].rearrange("p (a c) d -> p a (c d)", a=2), psum[:, PJ0:PJ0 + 2, 0:4 * HD], ACT.Square).then_inc(s["osq_ready"], 1)
            act.wait_ge(s["oss_ready"], 1)
            inverse_root(o_ss[:, :], o_rs[:, :], HD, Chain(act, s["o_rs"]))
            act.wait_ge(s["oa_turned"], 1)
            for bp in range(BP):
                a(mix_t[:, TP, 0:G, bp * 2 * L:(bp + 1) * 2 * L].rearrange("p g (a l) -> p a g l", a=2),
                  psum[:, OUT_A, bp * P:(bp + 1) * P].rearrange("p (a g l) -> p a g l", a=2, g=G), ACT.Copy)
            act.wait_ge(s["ob_turned"], 1)
            a(mix_t[:, TP, 4:8, :], f4(psum[:, OUT_B, :]), ACT.Copy)

        @block.vector
        def _(dve):
            link = Chain(dve, s["dve_chain"])
            link(dve.memset(scan_mask[:, :], 1.0))
            dve.memset(by_request(scan_mask[:, :])[:, :, 0:1], 0.0)
            dve.memset(eps[:, :], EPS).then_inc(s["consts"], 1)
            dve.wait_ge(s["q_squared"], 1)
            dve.tensor_reduce(ss[:, :], sq[:, :, :], AX_X, ALU.add).then_inc(s["ss_ready"], 1)
            dve.wait_ge(s["z_ready"], 1)
            link(dve.scalar_tensor_tensor(out=log_f[:, :], in0=psum[:, PJ1, :], scalar=0.0, in1=z_e[:, :],
                                          op0=ALU.min, op1=ALU.subtract))
            dve.tensor_tensor(k_b[:, :], log_f[:, :], psum[:, PJ1, :], ALU.subtract).then_inc(s["f_ready"], 1)
            dve.tensor_tensor_scan(cum[:, :], scan_mask[:, :], log_f[:, :], 0.0, ALU.mult, ALU.add).then_inc(s["cum_ready"], 1)
            dve.wait_ge(s["qk_rs"], 2)
            link(dve.tensor_tensor(sq[:, :, :], b["p_qk"][:, :].rearrange("p (h d) -> p h d", d=HD), bc(rs[:, :], 2, HD), ALU.mult))
            dve.tensor_tensor(qk_n[:, 0:QW].rearrange("p (g k d) -> p k g d", g=G, d=HD),
                              sq[:, 0:8, :].rearrange("p (k g) d -> p k g d", g=G),
                              b["norm_w"][:, 0:8, :].rearrange("p (k g) d -> p k g d", g=G), ALU.mult)
            dve.tensor_tensor(qk_n[:, QW:QW + KW].rearrange("p (k d) -> p k d", d=HD), sq[:, 8:10, :],
                              b["norm_w"][:, 8:10, :], ALU.mult).then_inc(s["qkn_ready"], 1)
            dve.wait_ge(s["rows_made"], 2)
            link(dve.tensor_scalar(rows_i[:, 1:2], rows_i[:, 0:1], L - 1, None, ALU.bitwise_and))
            link(dve.tensor_scalar(rows_i[:, 2:3], rows_i[:, 0:1], 4, G - 1, ALU.logical_shift_right, ALU.bitwise_and))
            link(dve.tensor_scalar(rows_i[:, 2:3], rows_i[:, 2:3], -1, 126, ALU.mult, ALU.add))
            link(dve.tensor_scalar(rows_i[:, 2:3], rows_i[:, 2:3], 23, None, ALU.logical_shift_left))
            dve.tensor_copy(frame[:, :], rows_i[:, 1:2])
            link(dve.tensor_copy(slope_p[:, :], rows_i[:, 2:3].bitcast(F32)))
            link(dve.tensor_scalar(dist[:, :], dist[:, :], frame[:, 0:1], None, ALU.add))
            link(dve.tensor_scalar(dist_n[:, :], dist[:, :], -1.0, None, ALU.mult))
            link(dve.tensor_tensor(dist[:, :], dist[:, :], dist_n[:, :], ALU.max))
            link(dve.tensor_scalar(dist[:, :], dist[:, :], slope_p[:, 0:1], None, ALU.mult))
            for kv in range(NKV):
                ins = dve.tensor_scalar(penalty[:, kv, :], dist[:, :], -slope(kv * G) / slope(0), None, ALU.mult)
            link(ins)
            dve.wait_ge(s["cum_ready"], 1)
            for i in range(NL):
                h = LEVELS[FIRST_LEVEL + i]
                c = cum[:, :].rearrange("p (n two h) -> p n two h", two=2, h=h)
                g = gap[:, i, :].rearrange("p (n two h) -> p n two h", two=2, h=h)
                mid = last_bc(c[:, :, 0, h - 1:h], h)
                dve.tensor_tensor(g[:, :, 0, :], mid, c[:, :, 0, :], ALU.subtract)
                dve.tensor_tensor(g[:, :, 1, :], c[:, :, 1, :], mid, ALU.subtract).then_inc(s["gap_ready"], 1)
            dve.tensor_tensor(by_request(k_d[:, :]), last_bc(by_request(cum[:, :])[:, :, L - 1:L], L),
                              by_request(cum[:, :]), ALU.subtract).then_inc(s["kgap_ready"], 1)
            dve.wait_ge(s["score_mm"], 2)
            for kv in range(NKV):
                src = psum[:, M0 + 2 * kv:M0 + 2 * kv + 2, :].rearrange("p a (b n) -> p a b n", b=2)[:, :, :, 0:KS]
                for a in range(2):
                    ins = dve.tensor_tensor(score[:, kv, 2 * a:2 * a + 2, :], src[:, a], bc(penalty[:, kv, :], 1, 2), ALU.add)
            link(ins)
            link(dve.tensor_reduce(top_s[:, :, :].rearrange("p k n -> p (k n)"), score[:, :, :, :].rearrange("p k n j -> p (k n) j"),
                                   AX_X, ALU.max))
            dve.wait_ge(s["sink_loaded"], 8 * 16)
            link(dve.tensor_tensor(top_s[:, :, :], top_s[:, :, :], bc(sink[:, :], 2, BP), ALU.max))
            dve.tensor_scalar(neg_top[:, :, :], top_s[:, :, :], -1.0, None, ALU.mult).then_inc(s["top_ready"], 1)
            dve.tensor_tensor(sink_e[:, :, :], bc(sink[:, :], 2, BP), top_s[:, :, :], ALU.subtract).then_inc(s["top_ready"], 1)
            dve.wait_ge(s["diag_mm"], 2)
            dve.tensor_tensor(pair[:, :, :, :].rearrange("p a h t -> p (a h) t"),
                              psum[:, PJ0:PJ0 + 2, :].rearrange("p a (h t) -> p (a h) t", t=P),
                              bc(ident[:, :], 1, 8), ALU.mult).then_inc(s["pair_clear"], 1)
            dve.wait_ge(s["k_ready"], 1)
            for i in range(NL):
                h = LEVELS[FIRST_LEVEL + i]
                dve.wait_ge(s["gap_exp"], i + 1)
                second = lambda a: a.rearrange("p (n two h) -> p n two h", two=2, h=h)[:, :, 1, :]
                dve.tensor_tensor(k_l[:, i, :], k_b[:, :], gap[:, i, :], ALU.mult)
                dve.tensor_tensor(q_l[:, i, :].rearrange("p (n h) -> p n h", h=h), second(q_b[:, :]),
                                  second(gap[:, i, :]), ALU.mult).then_inc(s["lv_ready"], 1)
            dve.wait_ge(s["pair_clear"], 1)
            for i in range(NL):
                h = LEVELS[FIRST_LEVEL + i]
                dve.wait_ge(s["lv_mm"], 2 * (i + 1))
                for a in range(2):
                    out = pair[:, a, :, :].rearrange("p e (n two h) -> p e n two h", two=2, h=h)[:, :, :, 1, :]
                    m = bc(b["level_mask"][:, FIRST_LEVEL + i, :].rearrange("p (n h) -> p n h", h=h).bitcast(I32), 1, 4)
                    src = psum[:, PJ0 + a, 0:4 * HD].rearrange("p (e n h) -> p e n h", e=4, h=h)
                    ins = dve.copy_predicated(out, m, src)
                ins.then_inc(s["pair_ready"], 1)
            dve.wait_ge(s["probs_ready"], 1)
            link(dve.tensor_tensor(den[:, :, :], den[:, :, :], sink_e[:, :, :], ALU.add))
            link(dve.reciprocal(rec[:, :, :], den[:, :, :]))
            dve.wait_ge(s["pv_mm"], 1)
            dve.tensor_tensor(o_a[:, :, :, :], psum[:, OUT_A, :].rearrange("p (k n d) -> p n k d", k=NKV, d=HD),
                              bc(rec[:, :, :].rearrange("p k n -> p n k"), 3, HD), ALU.mult).then_inc(s["oa_ready"], 1)
            dve.wait_ge(s["osq_ready"], 1)
            dve.tensor_reduce(o_ss[:, :], o_sq[:, :, :], AX_X, ALU.add).then_inc(s["oss_ready"], 1)
            dve.wait_ge(s["o_rs"], 2)
            for a in range(2):
                ins = dve.tensor_tensor(o_n[:, :].rearrange("p (c a d) -> p a c d", a=2, d=HD)[:, a],
                                        psum[:, PJ0 + a, 0:4 * HD].rearrange("p (c d) -> p c d", d=HD),
                                        bc(o_rs[:, 4 * a:4 * a + 4], 2, HD), ALU.mult)
            link(ins)
            dve.wait_ge(s["gate_ready"], 1)
            dve.tensor_tensor(o_n[:, :], o_n[:, :], gate[:, :], ALU.mult).then_inc(s["ob_ready"], 1)
            dve.wait_ge(s["state_mm"], 1)
            by = by_request(exp_b[:, :])[:, :, L - 1:L]
            st = state[:, :, :, :].rearrange("p c n v -> p (c n) v")
            dve.wait_ge(s["ob_mm"], 2)
            link(dve.tensor_tensor(st, st, last_bc(by, HD), ALU.mult))
            dve.tensor_tensor(st, st, psum[:, M0:M0 + 4, :].rearrange("p c (n v) -> p (c n) v", v=HD), ALU.add).then_inc(s["state_ready"], 1)


def one(t):
    return slice(t, t + 1) if isinstance(t, int) else bass.ds(t, 1)


def tile_kind(t):
    return one(t // TP)


def output(nc, b, d, x, w_out, w_router):
    psum, ident, mix_t, x2 = b["psum"], b["ident"], b["mix_t"], b["x2"]
    with ExitStack() as ctx:
        def sb(name, shape, dt=F32):
            return ctx.enter_context(nc.sbuf_tensor("r_" + name, shape, dt))

        def sem(name):
            return ctx.enter_context(nc.semaphore("r_" + name))

        w_out_sb = sb("w_out_sb", [P, KC, D])
        w_r = sb("w_r", [P, KC, NE])
        table = sb("table", [P, 3, 2, D])
        x_in = sb("x_in", [P, 2, D])
        lhs = sb("lhs", [P, KC, P])
        h2 = sb("h2", [P, D])
        h2_t = sb("h2_t", [P, KC, P])
        zeros = sb("zeros", [P, D])
        ss, rs, eps = sb("ss", [P, 1]), sb("rs", [P, 1]), sb("eps", [P, 1])

        names = """w_loaded r_loaded table_loaded x0_loaded x1_loaded zeros_made eps_made zeros_stored lhs_ready lhs_used
            x1_ready x2_ready waits_alone squared rs_ready xn_ready scaled h2_ready h2_stored h2_turned h2t_ready
            logit_mm logit_ready""".split()
        s = {n: sem(n) for n in names}
        x_loaded = (s["x0_loaded"], s["x1_loaded"])
        block = ctx.enter_context(nc.Block())

        @block.sync
        def _(sp):
            for par in range(2):
                sp.dma_start(x_in[:, par, :], x[par * P:(par + 1) * P, :]).then_inc(x_loaded[par], 16)
            for kv in range(NKV):
                sp.dma_start(w_out_sb[kv * HD:(kv + 1) * HD, 0:G, :],
                             w_out[kv * G * HD:(kv + 1) * G * HD, :].rearrange("(g d) n -> d g n", d=HD)).then_inc(s["w_loaded"], 16)
            sp.dma_start(w_out_sb[:, G:KC, :], w_out[QW:2 * QW, :].rearrange("(c p) n -> p c n", p=P)).then_inc(s["w_loaded"], 16)
            for i in range(3):
                sp.dma_start(table[:, i, 0, :], d["mod_rows"][0, i * D:(i + 1) * D].partition_broadcast(P)).then_inc(s["table_loaded"], 16)
                for n in range(NB):
                    sp.dma_start(table[n * L:(n + 1) * L, i, 1, :],
                                 d["mod_rows"][n + 1, i * D:(i + 1) * D].partition_broadcast(L)).then_inc(s["table_loaded"], 16)
            sp.dma_start(w_r[:, :, :], w_router.rearrange("(k p) n -> p k n", p=P)).then_inc(s["r_loaded"], 16)
            sp.wait_ge(s["zeros_made"], 1)
            sp.dma_start(d["h2"][ROWS:TABLE, :], zeros[:, :]).then_inc(s["zeros_stored"], 16)

            def store(t):
                rows = slice(t * P, (t + 1) * P) if isinstance(t, int) else bass.ds(t * P, P)
                sp.wait_ge(s["h2_ready"], t + 1)
                sp.dma_start(d["h2"][rows, :], h2[:, :]).then_inc(s["h2_stored"], 16)

            with sp.Fori(0, TP // 2) as i:
                for par in range(2):
                    store(i * 2 + par)
                    sp.wait_ge(s["x2_ready"], i * 2 + (par + 1))
                    sp.dma_start(x_in[:, par, :], x[bass.ds((i * 2 + (par + 2)) * P, P), :]).then_inc(x_loaded[par], 16)
            store(NT - 1)
            sp.wait_ge(s["x1_loaded"], 16 * (TP // 2 + 1))
            sp.wait_ge(s["h2_stored"], 16 * NT)
            sp.wait_ge(s["zeros_stored"], 16)

        @block.gpsimd
        def _(pool):
            pool.memset(zeros[:, :], 0.0).then_inc(s["zeros_made"], 1)

            def copy(t, half):
                if not isinstance(t, int):
                    pool.wait_ge(s["lhs_used"], t * 2 + (half - 1))
                    pool.sem_inc(s["waits_alone"], 1)
                pool.tensor_copy(lhs[:, 4 * half:4 * half + 4, :], mix_t[:, one(t), 4 * half:4 * half + 4, :]
                                 .rearrange("p a k r -> p (a k) r")).then_inc(s["lhs_ready"], 1)

            copy(0, 0)
            copy(0, 1)
            with pool.Fori(1, NT) as t:
                copy(t, 0)
                copy(t, 1)

        @block.tensor
        def _(pe):
            def project(t, par, half):
                pe.wait_ge(s["lhs_ready"], t * 2 + (half + 1))
                if half == 0 and not (isinstance(t, int) and t < 2):
                    pe.wait_ge(s["x1_ready"], t - 1)
                for k in range(4 * half, 4 * half + 4):
                    for n in range(2):
                        last = pe.matmul(psum[:, par * 2 + n, :], lhs[:, k, :], w_out_sb[:, k, n * 512:(n + 1) * 512],
                                         start=(k == 0), stop=(k == KC - 1))
                last.then_inc(s["lhs_used"], 1)

            def turn(t):
                pe.wait_ge(s["h2_ready"], t + 1)
                for k in range(KC):
                    last = pe.transpose(psum[:, 4 + k // 4, (k % 4) * P:(k % 4 + 1) * P], h2[:, k * P:(k + 1) * P], ident[:, :])
                last.then_inc(s["h2_turned"], 1)

            def logits(t):
                pe.wait_ge(s["h2t_ready"], t + 1)
                for k in range(KC):
                    last = pe.matmul(psum[:, 6, 0:NE], h2_t[:, k, :], w_r[:, k, :], start=(k == 0), stop=(k == KC - 1))
                last.then_inc(s["logit_mm"], 1)

            def turn_one(t, par):
                project(t, par, 0)
                turn(t - 1)
                project(t, par, 1)
                logits(t - 1)

            pe.wait_ge(s["w_loaded"], 48)
            pe.wait_ge(s["r_loaded"], 16)
            project(0, 0, 0)
            project(0, 0, 1)
            turn_one(1, 1)
            turn_one(2, 0)
            with pe.Fori(1, TP // 2) as i:
                turn_one(i * 2 + 1, 1)
                turn_one(i * 2 + 2, 0)
            turn(NT - 1)
            logits(NT - 1)

        @block.scalar
        def _(act):
            a = nc.scalar.activation

            def norm(t):
                act.wait_ge(s["x2_ready"], t + 1)
                act.sem_inc(s["waits_alone"], 1)
                x2t = x2[:, one(t), :].rearrange("p a n -> p (a n)")
                a(h2[:, :], x2t, ACT.Square, accum_out=ss[:, :]).then_inc(s["squared"], 1)
                act.wait_ge(s["squared"], t + 1)
                link = Chain(act, s["rs_ready"], 0, t, 2)
                link(a(rs[:, :], ss[:, :], ACT.Ln, scale=1.0 / D, bias=eps[:, :]))
                link(a(rs[:, :], rs[:, :], ACT.Exp, scale=-0.5))
                act.sem_inc(s["waits_alone"], 1)
                a(h2[:, :], x2t, ACT.Copy, scale=rs[:, 0:1]).then_inc(s["xn_ready"], 1)

            def keep(t):
                act.wait_ge(s["h2_turned"], t + 1)
                a(h2_t[:, :, :], psum[:, 4:6, :].rearrange("p a (k r) -> p (a k) r", r=P), ACT.Copy).then_inc(s["h2t_ready"], 1)

            act.wait_ge(s["eps_made"], 1)
            norm(0)
            with act.Fori(1, NT) as t:
                keep(t - 1)
                act.wait_ge(s["h2_stored"], t * 16)
                norm(t)
            keep(NT - 1)

        @block.vector
        def _(dve):
            dve.memset(eps[:, :], EPS).then_inc(s["eps_made"], 1)
            dve.wait_ge(s["table_loaded"], 27 * 16)

            def row(i, t):
                return table[:, i, tile_kind(t), :].rearrange("p a n -> p (a n)")

            def residual(t, par):
                x2t = x2[:, one(t), :].rearrange("p a n -> p (a n)")
                dve.wait_ge(s["lhs_used"], t * 2 + 2)
                dve.tensor_tensor(x2t.rearrange("p (a n) -> p a n", a=2), psum[:, par * 2:par * 2 + 2, :],
                                  row(0, t).rearrange("p (a n) -> p a n", a=2), ALU.mult).then_inc(s["x1_ready"], 1)
                dve.wait_ge(s["x1_ready"], t + 1)
                dve.tensor_tensor(x2t, x2t, x_in[:, par, :], ALU.add).then_inc(s["x2_ready"], 1)
                dve.wait_ge(s["xn_ready"], t + 1)
                dve.tensor_tensor(h2[:, :], h2[:, :], row(2, t), ALU.mult).then_inc(s["scaled"], 1)
                dve.wait_ge(s["scaled"], t + 1)
                dve.tensor_tensor(h2[:, :], h2[:, :], row(1, t), ALU.add).then_inc(s["h2_ready"], 1)

            def keep_logits(t):
                dve.wait_ge(s["logit_mm"], t + 1)
                dve.tensor_copy(b["logit"][:, one(t), :].rearrange("p a n -> p (a n)"), psum[:, 6, 0:NE]).then_inc(s["logit_ready"], 1)

            dve.wait_ge(s["x0_loaded"], 16)
            residual(0, 0)
            with dve.Fori(0, TP // 2) as i:
                for par in (1, 0):
                    t = i * 2 + (2 - par)
                    keep_logits(t - 1)
                    dve.wait_ge(x_loaded[par], (i + (2 - par)) * 16)
                    residual(t, par)
            keep_logits(NT - 1)


def route(nc, b, d, router_bias):
    psum, ident = b["psum"], b["ident"]
    with ExitStack() as ctx:
        def sb(name, shape, dt=F32):
            return ctx.enter_context(nc.sbuf_tensor("q_" + name, shape, dt))

        def sem(name):
            return ctx.enter_context(nc.semaphore("q_" + name))

        NG4 = NT * NG
        bias = sb("bias", [P, NE])
        aff, sel, tmp = (sb(n, [P, NT, NE]) for n in ("aff", "sel", "tmp"))
        beats, equal = (sb(n, [P, NG4, 4, 4]) for n in ("beats", "equal"))
        lower = sb("lower", [P, 4, 4])
        rank, best2, vs = (sb(n, [P, NG4, 4]) for n in ("rank", "best2", "vs"))
        g_score, g_rank, g_sel = (sb(n, [P, NT, NG]) for n in ("g_score", "g_rank", "g_sel"))
        pick = sb("pick", [P, 2, NT, NE])
        both = sb("both", [P, NT, NE])
        before_row = sb("before_row", [P, P])
        ones = sb("ones", [P, P])
        tile_sum, before = sb("tile_sum", [P, NT, NE]), sb("before", [P, NT, NE])
        count, n_list, end, first, ones_e = (sb(n, [P, NE]) for n in ("count", "n_list", "end", "first", "ones_e"))
        steps = sb("steps", [P, NT])
        many = sb("many", [P, NE, NT])
        place = sb("place", [P, NT, NE])
        chosen = sb("chosen", [P, 2, NT, NE])
        pos = sb("pos", [P, 2, NT])
        pos_i = sb("pos_i", [P, 2, NT], I32)
        number = sb("number", [P, 2, NT])
        w_k, w_sum = sb("w_k", [P, 2, NT]), sb("w_sum", [P, NT])
        padding = sb("padding", [SLOTS, P])
        list_rows = sb("list_rows", [SLOTS, P])
        is_second, row_of = sb("is_second", [P, SLOTS]), sb("row_of", [P, SLOTS])
        list_no = sb("list_no", [P, SLOTS])
        over = sb("over", [P, SLOTS, NE])
        expert = sb("expert", [P, SLOTS])

        names = "bias_loaded pool_made pad_stored chain nlogit_ready e_ready counted both_ready pos_ready scattered lists_loaded turned counts_turned".split()
        s = {n: sem(n) for n in names}
        block = ctx.enter_context(nc.Block())

        @block.sync
        def _(sp):
            sp.dma_start(bias[:, :], router_bias.partition_broadcast(P)).then_inc(s["bias_loaded"], 16)
            sp.wait_ge(s["pool_made"], 1)
            sp.dma_start(d["list_rows"].rearrange("(s p) o -> s (p o)", p=P), padding[:, :]).then_inc(s["pad_stored"], 16)
            sp.wait_ge(s["scattered"], 2 * NT * 16)
            sp.dma_start(list_rows[:, :], d["list_rows"].rearrange("(s p) o -> s (p o)", p=P)).then_inc(s["lists_loaded"], 16)

        @block.gpsimd
        def _(pool):
            small = dict(allow_small_or_imprecise_dtypes=True)
            pool.iota(padding[:, :], pattern=[[1, P]], base=ROWS, channel_multiplier=0, **small).then_inc(s["pool_made"], 1)
            pool.iota(number[:, :, :], pattern=[[TABLE, 2], [P, NT]], base=0, channel_multiplier=1, **small)
            pool.iota(steps[:, :], pattern=[[P, NT]], base=0, channel_multiplier=0, **small)
            pool.iota(list_no[:, :], pattern=[[1, SLOTS]], base=0, channel_multiplier=0, **small)
            pool.memset(ones[:, :], 1.0)
            pool.memset(ones_e[:, :], 1.0)
            pool.memset(before[:, 0, :], 0.0).then_inc(s["pool_made"], 1)
            pool.wait_ge(s["pool_made"], 2)
            pool.affine_select(out=before_row[:, :], in_=ones[:, :], compare_op=ALU.is_gt, fill=0.0, base=0,
                               pattern=[[1, P]], channel_multiplier=-1)
            pool.affine_select(out=lower[:, :, :], in_=ones[:, 0:16].rearrange("p (e j) -> p e j", e=4), compare_op=ALU.is_gt,
                               fill=0.0, base=0, pattern=[[1, 4], [-1, 4]], channel_multiplier=0).then_inc(s["pool_made"], 1)
            pool.wait_ge(s["pos_ready"], 1)
            pool.wait_ge(s["pad_stored"], 16)
            for k in range(2):
                for t in range(NT):
                    pool.indirect_dma_start(out=d["list_rows"], out_offset=bass.IndirectOffsetOnAxis(ap=pos_i[:, k, t:t + 1], axis=0),
                                            in_=number[:, k, t:t + 1], in_offset=None).then_inc(s["scattered"], 16)
            pool.wait_ge(s["scattered"], 2 * NT * 16)

        @block.scalar
        def _(act):
            act.wait_ge(s["nlogit_ready"], 1)
            nc.scalar.activation(tmp[:, :, :], tmp[:, :, :], ACT.Exp, scale=-1.0).then_inc(s["e_ready"], 1)

        @block.tensor
        def _(pe):
            pe.wait_ge(s["pool_made"], 3)
            pe.wait_ge(s["both_ready"], 1)
            flat = both[:, :, :].rearrange("p t e -> p (t e)")
            pe.matmul(psum[:, 0, 0:NT * NE], before_row[:, :], flat, start=True, stop=True)
            pe.matmul(psum[:, 1, 0:NT * NE], ones[:, :], flat, start=True, stop=True).then_inc(s["counted"], 1)
            pe.wait_ge(s["lists_loaded"], 16)
            pe.transpose(psum[:, 2, 0:SLOTS], list_rows[:, :], ident[0:SLOTS, 0:SLOTS]).then_inc(s["turned"], 1)

        @block.vector
        def _(dve):
            link = Chain(dve, s["chain"])

            def outrank(values, out, n):
                v_e, v_j = bc(values, 3, 4), bc(values, 2, 4)
                link(dve.tensor_tensor(beats[:, 0:n], v_j, v_e, ALU.is_gt))
                link(dve.tensor_tensor(equal[:, 0:n], v_j, v_e, ALU.is_equal))
                link(dve.tensor_tensor(equal[:, 0:n], equal[:, 0:n], bc(lower[:, :, :], 1, n), ALU.mult))
                link(dve.tensor_tensor(beats[:, 0:n], beats[:, 0:n], equal[:, 0:n], ALU.add))
                link(dve.tensor_reduce(out, beats[:, 0:n], AX_X, ALU.add))

            dve.tensor_scalar(tmp[:, :, :], b["logit"][:, :, :], -87.0, None, ALU.max).then_inc(s["nlogit_ready"], 1)
            dve.wait_ge(s["e_ready"], 1)
            link(dve.tensor_scalar(tmp[:, :, :], tmp[:, :, :], 1.0, None, ALU.add))
            link(dve.reciprocal(aff[:, :, :], tmp[:, :, :]))
            dve.wait_ge(s["bias_loaded"], 16)
            link(dve.tensor_tensor(sel[:, :, :], aff[:, :, :], bc(bias[:, :], 1, NT), ALU.add))
            dve.wait_ge(s["pool_made"], 3)
            by_group = sel[:, :, :].rearrange("p t (g e) -> p (t g) e", e=4)
            outrank(by_group, rank[:, :, :], NG4)
            link(dve.tensor_scalar(best2[:, :, :], rank[:, :, :], 1.5, None, ALU.is_lt))
            link(dve.tensor_tensor(vs[:, :, :], by_group, best2[:, :, :], ALU.mult))
            link(dve.tensor_reduce(g_score[:, :, :].rearrange("p t g -> p (t g)"), vs[:, :, :], AX_X, ALU.add))
            outrank(g_score[:, :, :], g_rank[:, :, :], NT)
            link(dve.tensor_scalar(g_sel[:, :, :], g_rank[:, :, :], 0.5, None, ALU.is_lt))
            g_all = g_sel[:, :, :].rearrange("p t g -> p (t g)")
            for k in range(2):
                ins = dve.scalar_tensor_tensor(out=pick[:, k].rearrange("p t (g e) -> p (t g) e", e=4), in0=rank[:, :, :],
                                               scalar=float(k), in1=bc(g_all, 2, 4), op0=ALU.is_equal, op1=ALU.mult)
            link(ins)
            dve.tensor_tensor(both[:, :, :], pick[:, 0], pick[:, 1], ALU.add).then_inc(s["both_ready"], 1)
            dve.wait_ge(s["counted"], 1)
            link(dve.tensor_copy(tile_sum[:, :, :].rearrange("p t e -> p (t e)"), psum[:, 1, 0:NT * NE]))
            for t in range(1, NT):
                link(dve.tensor_tensor(before[:, t, :], before[:, t - 1, :], tile_sum[:, t - 1, :], ALU.add))
            link(dve.tensor_tensor(count[:, :], before[:, NT - 1, :], tile_sum[:, NT - 1, :], ALU.add))
            link(dve.tensor_tensor(many[:, :, :], bc(count[:, :], 2, NT), bc(steps[:, :], 1, NE), ALU.is_gt))
            link(dve.tensor_reduce(n_list[:, :], many[:, :, :], AX_X, ALU.add))
            link(dve.tensor_tensor_scan(end[:, :], ones_e[:, :], n_list[:, :], 0.0, ALU.mult, ALU.add))
            link(dve.tensor_tensor(first[:, :], end[:, :], n_list[:, :], ALU.subtract))
            link(dve.tensor_tensor(place[:, :, :].rearrange("p t e -> p (t e)"), psum[:, 0, 0:NT * NE],
                                   before[:, :, :].rearrange("p t e -> p (t e)"), ALU.add))
            link(dve.scalar_tensor_tensor(out=place[:, :, :], in0=bc(first[:, :], 1, NT), scalar=float(P), in1=place[:, :, :],
                                          op0=ALU.mult, op1=ALU.add))
            link(dve.tensor_tensor(chosen[:, :, :, :], pick[:, :, :, :], bc(place[:, :, :], 1, 2), ALU.mult))
            link(dve.tensor_reduce(pos[:, :, :], chosen[:, :, :, :], AX_X, ALU.add))
            dve.tensor_copy(pos_i[:, :, :], pos[:, :, :]).then_inc(s["pos_ready"], 1)
            link(dve.tensor_tensor(chosen[:, :, :, :], pick[:, :, :, :], bc(aff[:, :, :], 1, 2), ALU.mult))
            link(dve.tensor_reduce(w_k[:, :, :], chosen[:, :, :, :], AX_X, ALU.add))
            link(dve.tensor_tensor(w_sum[:, :], w_k[:, 0], w_k[:, 1], ALU.add))
            link(dve.reciprocal(w_sum[:, :], w_sum[:, :]))
            link(dve.tensor_tensor(b["gate"][:, :, :], w_k[:, :, :], bc(w_sum[:, :], 1, 2), ALU.mult))
            link(dve.tensor_tensor(over[:, :, :], bc(list_no[:, :], 2, NE), bc(end[:, :], 1, SLOTS), ALU.is_ge))
            link(dve.tensor_reduce(expert[:, :], over[:, :, :], AX_X, ALU.add))
            dve.tensor_copy(b["list_info"][:, 0:SLOTS], expert[0:1, :])
            dve.tensor_copy(b["list_info"][:, SLOTS:SLOTS + NE], end[0:1, :])
            dve.tensor_scalar(b["list_info"][:, SLOTS + NE:SLOTS + NE + 1], end[0:1, NE - 1:NE], -1.0, None, ALU.add)
            dve.wait_ge(s["turned"], 1)
            link(dve.tensor_scalar(is_second[:, :], psum[:, 2, 0:SLOTS], float(TABLE), None, ALU.is_ge))
            link(dve.scalar_tensor_tensor(out=row_of[:, :], in0=is_second[:, :], scalar=-float(TABLE), in1=psum[:, 2, 0:SLOTS],
                                          op0=ALU.mult, op1=ALU.add))
            dve.tensor_copy(b["list_from"][:, :], row_of[:, :])
            dve.tensor_copy(b["list_to"][:, :], psum[:, 2, 0:SLOTS])


def experts(nc, b, d, w_gate, w_up, w_down):
    psum, ident = b["psum"], b["ident"]
    KD = DE // P
    with ExitStack() as ctx:
        def sb(name, shape, dt=F32):
            return ctx.enter_context(nc.sbuf_tensor("e_" + name, shape, dt))

        def sem(name):
            return ctx.enter_context(nc.semaphore("e_" + name))

        w_gu = sb("w_gu", [P, 2, 2, KC, DE])
        w_dn = sb("w_dn", [P, 2, KD, D])
        x_g = sb("x_g", [P, 2, D])
        x_t = sb("x_t", [P, KC, P])
        silu = sb("silu", [P, DE])
        u = sb("u", [P, DE])
        u_t = sb("u_t", [P, KD, P])
        y_s = sb("y_s", [P, 2, D])
        y_end = sb("y_end", [P, D])
        from_now = [sb(f"from{par}", [P, 1], I32) for par in range(2)]
        to_now = [sb(f"to{par}", [P, 1], I32) for par in range(2)]
        to_end = sb("to_end", [P, 1], I32)

        def by_parity(name):
            return [sem(f"{name}{par}") for par in range(2)]

        gu_loaded, dn_loaded, gathered, stored = (by_parity(n) for n in ("gu_loaded", "dn_loaded", "gathered", "stored"))
        names = "index_ready waits_alone x_turned xt_ready gu_mm silu_ready u_ready u_turned ut_ready dn_mm y_ready end_stored".split()
        s = {n: sem(n) for n in names}
        block = ctx.enter_context(nc.Block())


        def steps(eng, body):
            end = eng.value_load(b["list_info"][0:1, SLOTS + NE:SLOTS + NE + 1], min_val=2 * NT - 1, max_val=LISTS - 1)
            body(0, 0, -1)
            body(1, 1, 0)
            body(2, 0, 0)
            with eng.Fori(1, (LISTS - 1) // 2) as i:
                with eng.If(end > i * 2):
                    body(i * 2 + 1, 1, i)
                with eng.If(end > i * 2 + 1):
                    body(i * 2 + 2, 0, i)
            return end

        def is_first(t):
            return isinstance(t, int) and t == 0

        def stored_before(eng, t, par, i):
            if not isinstance(t, int):
                eng.wait_ge(stored[1 - par], i * 16)

        @block.sync
        def _(sp):
            sp.sem_inc(gu_loaded[1], 1)
            sp.sem_inc(dn_loaded[1], 1)

            def load(e, par, first=False):
                if not first:
                    done = sp.value_load(b["list_info"][0:1, bass.ds(e + (SLOTS - 2), 1)], min_val=0, max_val=LISTS)
                    sp.wait_ge(s["gu_mm"], done + 1)
                for j, w in enumerate((w_gate, w_up)):
                    sp.dma_start(w_gu[:, par, j, :, :], w[one(e), :, :].rearrange("a (k p) n -> p (a k) n", p=P)).then_inc(gu_loaded[par], 16)
                if not first:
                    sp.wait_ge(s["dn_mm"], done + 1)
                sp.dma_start(w_dn[:, par, :, :], w_down[one(e), :, :].rearrange("a (k p) n -> p (a k) n", p=P)).then_inc(dn_loaded[par], 16)

            load(0, 0, True)
            load(1, 1, True)
            with sp.Fori(1, NE // 2) as i:
                load(i * 2, 0)
                load(i * 2 + 1, 1)
            for par in range(2):
                sp.wait_ge(gu_loaded[par], NE * 16 + par)
                sp.wait_ge(dn_loaded[par], NE // 2 * 16 + par)

        @block.gpsimd
        def _(pool):
            def index(now, of, count):
                alone()
                pool.tensor_copy(now[:, :], of).then_inc(s["index_ready"], 1)
                pool.wait_ge(s["index_ready"], count)

            def alone():
                pool.sem_inc(s["waits_alone"], 1)

            def fetch(par):
                alone()
                pool.indirect_dma_start(out=x_g[:, par, :], out_offset=None, in_=d["h2"],
                                        in_offset=bass.IndirectOffsetOnAxis(ap=from_now[par][:, 0:1], axis=0)).then_inc(gathered[par], 16)

            for par in range(2):
                index(from_now[par], b["list_from"][:, par:par + 1], par + 1)
                fetch(par)

            def step(t, par, i):
                pool.wait_ge(s["x_turned"], t + 1)
                index(from_now[par], b["list_from"][:, one(t + 2)], t * 2 + (3 if is_first(t) else 2))
                fetch(par)
                if not is_first(t):
                    stored_before(pool, t, par, i)
                    index(to_now[1 - par], b["list_to"][:, one(t - 1)], t * 2 + 3)
                    if not (isinstance(t, int) and t < 2):
                        pool.wait_ge(stored[par], (i + (1 - par)) * 16)
                        alone()
                    pool.wait_ge(s["y_ready"], t + 1)
                    alone()
                    pool.indirect_dma_start(out=d["y_rows"], out_offset=bass.IndirectOffsetOnAxis(ap=to_now[1 - par][:, 0:1], axis=0),
                                            in_=y_s[:, 1 - par, :], in_offset=None).then_inc(stored[1 - par], 16)

            end = steps(pool, step)
            index(to_end, b["list_to"][:, bass.ds(end, 1)], end * 2 + 4)
            pool.wait_ge(s["y_ready"], end + 2)
            alone()
            pool.wait_ge(stored[0], (end + 1) // 2 * 16)
            alone()
            pool.wait_ge(stored[1], end // 2 * 16)
            alone()
            pool.indirect_dma_start(out=d["y_rows"], out_offset=bass.IndirectOffsetOnAxis(ap=to_end[:, 0:1], axis=0),
                                    in_=y_end[:, :], in_offset=None).then_inc(s["end_stored"], 16)
            pool.wait_ge(s["end_stored"], 16)
            pool.wait_ge(gathered[0], (end + 4) // 2 * 16)
            pool.wait_ge(gathered[1], (end + 3) // 2 * 16)

        @block.tensor
        def _(pe):
            pe.sem_inc(s["gu_mm"], 1)
            pe.sem_inc(s["dn_mm"], 1)

            def expert(t):
                return pe.value_load(b["list_info"][0:1, one(t)], min_val=0, max_val=NE - 1)

            def turn_x(t, par, nth):
                pe.wait_ge(gathered[par], nth * 16)
                for k in range(KC):
                    last = pe.transpose(psum[:, 2 + k // 4, (k % 4) * P:(k % 4 + 1) * P], x_g[:, par, k * P:(k + 1) * P], ident[:, :])
                last.then_inc(s["x_turned"], 1)

            def hidden(t):
                e = expert(t)
                slot = bass.ds(e % 2, 1)
                pe.wait_ge(gu_loaded[0], (e // 2 + 1) * 32)
                pe.wait_ge(gu_loaded[1], (e + 1) // 2 * 32 + 1)
                pe.wait_ge(s["xt_ready"], t + 1)
                if not is_first(t):
                    pe.wait_ge(s["u_ready"], t)
                for k in range(KC):
                    for j in range(2):
                        w = w_gu[:, slot, j, k, :].rearrange("p a n -> p (a n)")
                        last = pe.matmul(psum[:, j, :], x_t[:, k, :], w, start=(k == 0), stop=(k == KC - 1))
                last.then_inc(s["gu_mm"], 1)

            def down(t):
                e = expert(t)
                slot = bass.ds(e % 2, 1)
                pe.wait_ge(dn_loaded[0], (e // 2 + 1) * 16)
                pe.wait_ge(dn_loaded[1], (e + 1) // 2 * 16 + 1)
                pe.wait_ge(s["ut_ready"], t + 1)
                pe.wait_ge(s["y_ready"], t + 1)
                for k in range(KD):
                    for j in range(2):
                        w = w_dn[:, slot, k, j * 512:(j + 1) * 512].rearrange("p a n -> p (a n)")
                        last = pe.matmul(psum[:, 5 + j, :], u_t[:, k, :], w, start=(k == 0), stop=(k == KD - 1))
                last.then_inc(s["dn_mm"], 1)

            def turn_u(t):
                pe.wait_ge(s["u_ready"], t + 1)
                for k in range(KD):
                    last = pe.transpose(psum[:, 4, k * P:(k + 1) * P], u[:, k * P:(k + 1) * P], ident[:, :])
                last.then_inc(s["u_turned"], 1)

            turn_x(0, 0, 1)

            def step(t, par, i):
                hidden(t)
                turn_x(t + 1, 1 - par, i + 2)
                if not is_first(t):
                    down(t - 1)
                turn_u(t)

            end = steps(pe, step)
            down(end)

        @block.scalar
        def _(act):
            act.sem_inc(s["y_ready"], 1)

            def keep_x(t):
                act.wait_ge(s["x_turned"], t + 1)
                nc.scalar.activation(x_t[:, :, :], psum[:, 2:4, :].rearrange("p a (k r) -> p (a k) r", r=P), ACT.Copy).then_inc(s["xt_ready"], 1)

            keep_x(0)

            def step(t, par, i):
                if not is_first(t):
                    act.wait_ge(s["u_ready"], t)
                act.wait_ge(s["gu_mm"], t + 2)
                nc.scalar.activation(silu[:, :], psum[:, 0, :], ACT.Silu).then_inc(s["silu_ready"], 1)
                keep_x(t + 1)

            steps(act, step)

        @block.vector
        def _(dve):
            def step(t, par, i):
                dve.wait_ge(s["silu_ready"], t + 1)
                dve.tensor_tensor(u[:, :], silu[:, :], psum[:, 1, :], ALU.mult).then_inc(s["u_ready"], 1)
                if not is_first(t):
                    dve.wait_ge(s["dn_mm"], t + 1)
                    stored_before(dve, t, par, i)
                    dve.tensor_copy(y_s[:, 1 - par, :].rearrange("p (a n) -> p a n", a=2), psum[:, 5:7, :]).then_inc(s["y_ready"], 1)
                dve.wait_ge(s["u_turned"], t + 1)
                dve.tensor_copy(u_t[:, :, :], psum[:, 4, :].rearrange("p (k r) -> p k r", r=P)).then_inc(s["ut_ready"], 1)

            end = steps(dve, step)
            dve.wait_ge(s["dn_mm"], end + 2)
            dve.tensor_copy(y_end[:, :].rearrange("p (a n) -> p a n", a=2), psum[:, 5:7, :]).then_inc(s["y_ready"], 1)


def combine(nc, b, d, y):
    with ExitStack() as ctx:
        def sb(name, shape, dt=F32):
            return ctx.enter_context(nc.sbuf_tensor("c_" + name, shape, dt))

        def sem(name):
            return ctx.enter_context(nc.semaphore("c_" + name))

        table = sb("table", [P, 2, D])
        y_in = sb("y_in", [P, 2, 2, D])
        out = sb("out", [P, 2, D])
        loaded = [sem("loaded0"), sem("loaded1")]
        stored = [sem("stored0"), sem("stored1")]
        s = {n: sem(n) for n in "table_loaded scaled summed gated ready".split()}
        block = ctx.enter_context(nc.Block())

        def rows(t, base=0):
            return slice(base + t * P, base + (t + 1) * P) if isinstance(t, int) else bass.ds(t * P + base, P)

        def tiles(eng, body):
            for par in range(2):
                body(par, par, 0)
            with eng.Fori(1, TP // 2) as i:
                for par in range(2):
                    body(i * 2 + par, par, i)
            body(TP, 0, TP // 2)

        @block.sync
        def _(sp):
            def load(t, par):
                for k in range(2):
                    sp.dma_start(y_in[:, par, k, :], d["y_rows"][rows(t, k * TABLE), :]).then_inc(loaded[par], 16)

            load(0, 0)
            load(1, 1)
            g2 = slice(3 * D, 4 * D)
            sp.dma_start(table[:, 0, :], d["mod_rows"][0, g2].partition_broadcast(P)).then_inc(s["table_loaded"], 16)
            for n in range(NB):
                sp.dma_start(table[n * L:(n + 1) * L, 1, :], d["mod_rows"][n + 1, g2].partition_broadcast(L)).then_inc(s["table_loaded"], 16)

            def tile(t, par, i):
                sp.wait_ge(s["ready"], t + 1)
                sp.dma_start(y[rows(t), :], out[:, par, :]).then_inc(stored[par], 16)

            with sp.Fori(0, TP // 2 - 1) as i:
                for par in range(2):
                    tile(i * 2 + par, par, i)
                    load(i * 2 + (par + 2), par)
            tile(TP - 2, 0, 0)
            load(TP, 0)
            tile(TP - 1, 1, 0)
            tile(TP, 0, 0)
            sp.wait_ge(stored[0], (TP // 2 + 1) * 16)
            sp.wait_ge(stored[1], TP // 2 * 16)

        @block.scalar
        def _(act):
            def tile(t, par, i):
                act.wait_ge(loaded[par], (i + 1) * 32)
                nc.scalar.activation(y_in[:, par, 0, :], y_in[:, par, 0, :], ACT.Copy, scale=b["gate"][:, 0, one(t)]).then_inc(s["scaled"], 1)

            tiles(act, tile)

        @block.vector
        def _(dve):
            dve.wait_ge(s["table_loaded"], 9 * 16)

            def tile(t, par, i):
                dve.wait_ge(s["scaled"], t + 1)
                if not (isinstance(t, int) and t < 2):
                    dve.wait_ge(stored[par], i * 16)
                o = out[:, par, :]
                dve.scalar_tensor_tensor(out=o, in0=y_in[:, par, 1, :], scalar=b["gate"][:, 1, one(t)], in1=y_in[:, par, 0, :],
                                         op0=ALU.mult, op1=ALU.add).then_inc(s["summed"], 1)
                dve.wait_ge(s["summed"], t + 1)
                dve.tensor_tensor(o, o, table[:, tile_kind(t), :].rearrange("p a n -> p (a n)"), ALU.mult).then_inc(s["gated"], 1)
                dve.wait_ge(s["gated"], t + 1)
                dve.tensor_tensor(o, o, b["x2"][:, one(t), :].rearrange("p a n -> p (a n)"), ALU.add).then_inc(s["ready"], 1)

            tiles(dve, tile)



def program(nc, args):
    stream_layer(nc, *args)


_OUTS = [((ROWS, D)), (P, KW), (P, KW), (8, HD, HD), (P, KW), (P, KW), (NB, 8, HD, HD)]


def kernel(**inputs):
    import numpy as np
    import concourse.bacc as bacc
    from concourse.bass_utils import run_bass_kernel_spmd

    a = {k: np.asarray(v) for k, v in inputs.items()}
    nc = bacc.Bacc("TRN2", target_bir_lowering=False, num_devices=1)
    arrays = {
        "x": np.concatenate([a["x_prompt"].reshape(-1, D), a["x_sample"].reshape(-1, D), np.zeros((P, D), np.float32)]),
        "cond": np.concatenate([a["c_prompt"], a["c_sample"]]),
        "cache_k": a["cache_k"][0].reshape(NB, WIN, KW),
        "cache_v": a["cache_v"][0].reshape(NB, WIN, KW),
        "state_in": a["state_hgrn"][0],
        **{k: a[k][0] for k in ("w_ada", "b_ada", "ln1", "ln2", "w_in", "q_norm", "k_norm", "sinks", "o_norm", "w_out")},
        "w_router": a["w_router"], "router_bias": a["router_bias"],
        **{k: a[k][0] for k in ("w_e_gate", "w_e_up", "w_e_down")},
    }
    arrays = {f"in_{k}": np.ascontiguousarray(v) for k, v in arrays.items()}
    args = [nc.dram_tensor(k, v.shape, F32, kind="ExternalInput").ap() for k, v in arrays.items()]
    args += [nc.dram_tensor(f"out_{i}", s, F32, kind="ExternalOutput").ap() for i, s in enumerate(_OUTS)]
    program(nc, args)
    r = run_bass_kernel_spmd(nc, [arrays], core_ids=[0]).results[0]
    y, kp, vp, sp, ks, vs, ss = (r[f"out_{i}"] for i in range(len(_OUTS)))
    return (y[:TP * P].reshape(1, TP * P, D), y[TP * P:].reshape(NB, L, D), kp.reshape(1, 1, P, NKV, HD),
            vp.reshape(1, 1, P, NKV, HD), sp.reshape(1, 1, 8, HD, HD), ks.reshape(1, NB, L, NKV, HD),
            vs.reshape(1, NB, L, NKV, HD), ss.reshape(1, NB, 8, HD, HD))
```

```python
from contextlib import ExitStack

import concourse.bass as bass
from concourse import mybir

F32 = mybir.dt.float32
F32R = mybir.dt.float32r
I32 = mybir.dt.int32
ALU = mybir.AluOpType
ACT = mybir.ActivationFunctionType
AX_X = mybir.AxisListType.X

P = 128
D = 1024
KC = D // P
TP = 8
NT = TP + 1
NB = 8
L = 16
HD = 64
NKV = 2
G = 4
QW = 512
KW = NKV * HD
IN_W = QW + 2 * KW + 4 * QW
CQ, CK, CV, CQB, CFB, CIB, CGB = 0, 512, 640, 768, 1280, 1792, 2304
WIN = 128
NE = 16
NG = 4
DE = 512
MODS = 6
EPS = 1e-6
FAR = 1e33
LEVELS = (64, 32, 16, 8, 4, 2, 1)
LISTS = 2 * NT + NE - 1
SLOTS = LISTS + 2
ENDS, LAST, SPLIT, NTH, INFO_W = SLOTS, SLOTS + NE, SLOTS + NE + 1, 2 * SLOTS + NE + 1, 3 * SLOTS + NE + 1
ROWS = NT * P
TABLE = ROWS + P


def bc(ap, axis, n):
    ap = ap.unsqueeze(axis)
    shape = list(ap.shape)
    shape[axis] = n
    return ap.to_broadcast(shape)


def last_bc(ap, n):
    return ap.to_broadcast(list(ap.shape)[:-1] + [n])


class Chain:

    def __init__(self, eng, sem, base=0, turn=0, per=0):
        self.eng, self.sem, self.base, self.turn, self.per, self.k = eng, sem, base, turn, per, 0

    def __call__(self, ins):
        self.k += 1
        ins.then_inc(self.sem, 1)
        self.eng.wait_ge(self.sem, self.turn * self.per + (self.base + self.k))

    def done(self):
        assert self.k == self.per, (self.k, self.per)


def one(t):
    return slice(t, t + 1) if isinstance(t, int) else bass.ds(t, 1)


def tile_kind(t):
    return one(t // TP)


def retire(nc, sems):
    nc.clear_and_free_semaphores(sems)
    nc.all_engine_barrier()


def stream_layer(nc, x, cond, cache_k, cache_v, state_in, w_ada, b_ada, ln1, ln2, w_in, q_norm, k_norm,
                 sinks, o_norm, w_out, w_router, router_bias, w_gate, w_up, w_down,
                 y, k_prompt, v_prompt, s_prompt, k_sample, v_sample, s_sample):
    mod_rows_d = nc.dram_tensor("mod_rows_d", (NT, 3 * D), F32).ap()
    out_gate_d = nc.dram_tensor("out_gate_d", (NT, D), F32).ap()
    top = ExitStack()
    with top:
        def sb(ctx, name, shape, dt=F32):
            return ctx.enter_context(nc.sbuf_tensor(name, shape, dt))

        def sem(name):
            return top.enter_context(nc.semaphore(name))

        psum = top.enter_context(nc.psum_tensor("psum", [P, 8, 512], F32))
        ident = sb(top, "ident", [P, P])
        mix_t = sb(top, "mix_t", [P, NT, KC, P])
        logit = sb(top, "logit", [P, NT, NE])
        list_info = sb(top, "list_info", [1, INFO_W], I32)
        list_row, list_kind = sb(top, "list_row", [P, SLOTS], I32), sb(top, "list_kind", [P, SLOTS], I32)
        list_gate = sb(top, "list_gate", [P, SLOTS])
        s_const = sem("s_const")
        x_loaded, rows_stored = sem("x_loaded"), sem("rows_stored")
        w_in_loaded = [sem(f"w_in_loaded_{name}") for name, _, _ in PROJ]

        proj_ctx = ExitStack()
        with proj_ctx:
            mod_a = sb(proj_ctx, "mod_a", [P, 2, KC, NB])
            mod_b = sb(proj_ctx, "mod_b", [P, 2, KC, NB])
            x_res = sb(proj_ctx, "x_res", [P, 2, D])
            x_in, h_t = x_res[:, 0, :], x_res[:, 1, :].rearrange("p (k r) -> p k r", r=P)
            p_qk = sb(proj_ctx, "p_qk", [P, QW + KW])
            p_v = sb(proj_ctx, "p_v", [P, KW])
            p_q = sb(proj_ctx, "p_q", [P, QW])
            p_f = sb(proj_ctx, "p_f", [P, QW])
            p_i = sb(proj_ctx, "p_i", [P, QW])
            p_g = sb(proj_ctx, "p_g", [P, QW])
            norm_w = sb(proj_ctx, "norm_w", [P, 2, HD])
            o_norm_w = sb(proj_ctx, "o_norm_w", [P, HD])
            level_mask = sb(proj_ctx, "level_mask", [P, len(LEVELS), HD])
            consts_loaded = sem("consts_loaded")
            mask_made = sem("mask_made")

            win_ctx = ExitStack()
            with win_ctx:
                w_in_sb = sb(win_ctx, "w_in_sb", [P, KC, IN_W])

                with ExitStack() as ctx:
                    STAGES = 3
                    GROUPS = MODS * D // 512
                    stage = sb(ctx, "stage", [P, STAGES, KC, 512])
                    rows = mix_t[0:NT, :, :, :].rearrange("p n k r -> p (n k r)")
                    mod_row, ln2_row = rows[:, 0:MODS * D], rows[:, MODS * D:(MODS + 1) * D]
                    c_row, c_e = rows[:, (MODS + 1) * D:(MODS + 2) * D], rows[:, (MODS + 2) * D:(MODS + 3) * D]
                    c_t = sb(ctx, "c_t", [P, KC, NT])
                    bias_row = sb(ctx, "bias_row", [NT, 2, 512])
                    ln1_t = sb(ctx, "ln1_t", [P, KC])
                    c_loaded = sem("c_loaded")
                    ln_loaded = sem("ln_loaded")
                    stage_loaded = [sem(f"stage_loaded{i}") for i in range(STAGES)]
                    bias_loaded = [sem(f"bias_loaded{i}") for i in range(2)]
                    c_exp = sem("c_exp")
                    c_chain = sem("c_chain")
                    c_silu = sem("c_silu")
                    c_turned = sem("c_turned")
                    c_t_ready = sem("c_t_ready")
                    group_done = sem("group_done")
                    row_done = sem("row_done")
                    mod_turned = sem("mod_turned")
                    mod_ready = sem("mod_ready")
                    block = ctx.enter_context(nc.Block())

                    @block.sync
                    def _(sp):
                        sp.dma_start(c_row[:, :], cond).then_inc(c_loaded, 16)
                        for g in range(GROUPS):
                            if g >= STAGES:
                                sp.wait_ge(group_done, g - STAGES + 1)
                            sp.dma_start(stage[:, g % STAGES, :, :],
                                         w_ada[:, g * 512:(g + 1) * 512].rearrange("(k p) n -> p k n", p=P)
                                         ).then_inc(stage_loaded[g % STAGES], 16)
                            if g >= 2:
                                sp.wait_ge(row_done, g - 1)
                            sp.dma_start(bias_row[:, g % 2, :],
                                         b_ada[g * 512:(g + 1) * 512].partition_broadcast(NT)
                                         ).then_inc(bias_loaded[g % 2], 16)
                            if g == 0:
                                with nc.allow_non_contiguous_dma("a column of ln1 for each chunk"):
                                    sp.dma_start(ln1_t[:, :], ln1.rearrange("(k p) -> p k", p=P)).then_inc(ln_loaded, 16)
                                sp.dma_start(ln2_row[:, :], ln2.partition_broadcast(NT)).then_inc(ln_loaded, 16)
                                sp.dma_start(o_norm_w[:, :], o_norm.partition_broadcast(P)).then_inc(consts_loaded, 16)
                                for i, src in enumerate((q_norm, k_norm)):
                                    sp.dma_start(norm_w[:, i, :], src.partition_broadcast(P)).then_inc(consts_loaded, 16)
                        sp.dma_start(x_in[:, :], x[0:P, :]).then_inc(x_loaded, 16)
                        w_in_v = w_in.rearrange("(k p) n -> p k n", p=P)
                        for j, (_, a, n) in enumerate(PROJ):
                            sp.dma_start(w_in_sb[:, :, a:a + n], w_in_v[:, :, a:a + n]).then_inc(w_in_loaded[j], 16)
                        sp.wait_ge(row_done, GROUPS + 2)
                        sp.dma_start(mod_rows_d[:, 0:D], mod_row[:, 2 * D:3 * D]).then_inc(rows_stored, 16)
                        sp.dma_start(mod_rows_d[:, D:3 * D], mod_row[:, 3 * D:5 * D]).then_inc(rows_stored, 16)
                        sp.dma_start(out_gate_d, mod_row[:, 5 * D:6 * D]).then_inc(rows_stored, 16)

                    @block.gpsimd
                    def _(pool):
                        link = Chain(pool, mask_made)
                        link(pool.memset(ident[:, :], 0.0))
                        pool.affine_select(out=ident[:, :], in_=ident[:, :], compare_op=ALU.not_equal, fill=1.0,
                                           base=0, pattern=[[-1, P]], channel_multiplier=1).then_inc(s_const, 1)
                        link(pool.memset(level_mask[:, :, :], 1.0))
                        for i, h in enumerate(LEVELS):
                            n = HD // h
                            m = level_mask[:, i, :].rearrange("p (n h) -> p n h", h=h)
                            link(pool.affine_select(out=m, in_=m, compare_op=ALU.is_ge, fill=0.0, base=0,
                                                    pattern=[[-2 * h, n], [0, h]], channel_multiplier=1))
                            link(pool.affine_select(out=m, in_=m, compare_op=ALU.is_ge, fill=0.0, base=h - 1,
                                                    pattern=[[2 * h, n], [0, h]], channel_multiplier=-1))

                    @block.scalar
                    def _(act):
                        act.wait_ge(c_loaded, 16)
                        act.activation(c_e[:, :], c_row[:, :], ACT.Exp, scale=-1.0).then_inc(c_exp, 1)

                    @block.vector
                    def _(dve):
                        link = Chain(dve, c_chain)
                        dve.wait_ge(c_exp, 1)
                        link(dve.tensor_scalar(c_e[:, :], c_e[:, :], 1.0, None, ALU.add))
                        link(dve.reciprocal(c_e[:, :], c_e[:, :]))
                        dve.tensor_tensor(c_row[:, :], c_row[:, :], c_e[:, :], ALU.mult).then_inc(c_silu, 1)
                        dve.wait_ge(consts_loaded, 3 * 16)
                        link(dve.tensor_scalar(norm_w[:, 0, :], norm_w[:, 0, :], HD ** -0.5, None, ALU.mult))
                        dve.wait_ge(c_turned, 1)
                        dve.tensor_copy(c_t[:, :, :], psum[:, 0, 0:KC * NT].rearrange("p (k n) -> p k n", n=NT)).then_inc(c_t_ready, 1)
                        for g in range(GROUPS):
                            dve.wait_ge(group_done, g + 1)
                            dve.wait_ge(bias_loaded[g % 2], 16 * (g // 2 + 1))
                            dve.tensor_tensor(mod_row[:, g * 512:(g + 1) * 512], psum[0:NT, 1 + g % 2, :],
                                              bias_row[:, g % 2, :], ALU.add).then_inc(row_done, 1)
                            if g == 4:
                                dve.wait_ge(mod_turned, 1)
                                dve.wait_ge(ln_loaded, 32)
                                turned = psum[:, 3, 0:2 * KC * NT].rearrange("p (k n) -> p k n", n=NT)
                                for kind, cols in ((0, slice(0, 1)), (1, slice(1, NT))):
                                    sh, sc = turned[:, 0:KC, cols], turned[:, KC:2 * KC, cols]
                                    if kind == 0:
                                        sh, sc = last_bc(sh, NB), last_bc(sc, NB)
                                    dve.tensor_copy(mod_b[:, kind, :, :], sh)
                                    link(dve.tensor_scalar(mod_a[:, kind, :, :], sc, 1.0, None, ALU.add))
                                    dve.tensor_tensor(mod_a[:, kind, :, :], mod_a[:, kind, :, :],
                                                      bc(ln1_t[:, :], 2, NB), ALU.mult).then_inc(mod_ready, 1)
                        dve.wait_ge(row_done, GROUPS)
                        dve.tensor_scalar(mod_row[:, 4 * D:5 * D], mod_row[:, 4 * D:5 * D], 1.0, None, ALU.add).then_inc(row_done, 1)
                        dve.wait_ge(row_done, GROUPS + 1)
                        dve.tensor_tensor(mod_row[:, 4 * D:5 * D], mod_row[:, 4 * D:5 * D], ln2_row[:, :], ALU.mult).then_inc(row_done, 1)

                    @block.tensor
                    def _(pe):
                        pe.wait_ge(s_const, 1)
                        pe.wait_ge(c_silu, 1)
                        for k in range(KC):
                            last = pe.transpose(psum[:, 0, k * NT:(k + 1) * NT], c_row[:, k * P:(k + 1) * P], ident[0:NT, 0:NT])
                        last.then_inc(c_turned, 1)
                        pe.wait_ge(c_t_ready, 1)
                        for g in range(GROUPS):
                            pe.wait_ge(stage_loaded[g % STAGES], 16 * (g // STAGES + 1))
                            if g >= 2:
                                pe.wait_ge(row_done, g - 1)
                            for k in range(KC):
                                last = pe.matmul(psum[0:NT, 1 + g % 2, :], c_t[:, k, :], stage[:, g % STAGES, k, :],
                                                 start=(k == 0), stop=(k == KC - 1))
                            last.then_inc(group_done, 1)
                            if g == 4:
                                pe.wait_ge(row_done, 4)
                                for k in range(2 * KC):
                                    last = pe.transpose(psum[:, 3, k * NT:(k + 1) * NT], mod_row[:, k * P:(k + 1) * P],
                                                        ident[0:NT, 0:NT])
                                last.then_inc(mod_turned, 1)

                b = dict(
                    psum=psum, ident=ident, mix_t=mix_t, w_in_loaded=w_in_loaded, x_loaded=x_loaded, rows_stored=rows_stored, mod_a=mod_a, mod_b=mod_b,
                    x_in=x_in, h_t=h_t, p_qk=p_qk, p_v=p_v, p_q=p_q, p_f=p_f, p_i=p_i, p_g=p_g,
                    norm_w=norm_w, o_norm_w=o_norm_w, level_mask=level_mask, w_in_sb=w_in_sb)
                mixing(nc, b, x, sinks, k_prompt, v_prompt, s_prompt)
            d = dict(
                x=x, w_out=w_out, w_router=w_router, w_gate=w_gate, w_up=w_up, w_down=w_down,
                mod_rows=mod_rows_d, out_gate=out_gate_d, y=y,
                h2=nc.dram_tensor("h2_d", (TABLE, D), F32).ap())
            b.update(
                logit=logit, list_info=list_info, list_row=list_row, list_kind=list_kind, list_gate=list_gate,
                w_out_a=sb(proj_ctx, "w_out_a", [P, G, D]), w_r=sb(proj_ctx, "w_r", [P, KC, NE]),
                x_res=x_res, w_out_loaded=sem("w_out_loaded"), w_r_loaded=sem("w_r_loaded"),
                x_res_loaded=[sem("x_res_loaded0"), sem("x_res_loaded1")])
            sampling(nc, b, d, sinks, cache_k, cache_v, state_in, k_sample, v_sample, s_sample)
            output(nc, b, d)
        b.update(
            w_gu=sb(top, "w_gu", [P, 2, 2, KC, DE]), w_dn=sb(top, "w_dn", [P, 2, DE // P, D]),
            gu_loaded=[sem("gu_loaded0"), sem("gu_loaded1")], dn_loaded=[sem("dn_loaded0"), sem("dn_loaded1")])
        route(nc, b, d, router_bias)
        experts(nc, b, d)


def load_output_operands(sp, b, d):
    for par in range(2):
        sp.dma_start(b["x_res"][:, par, :], d["x"][par * P:(par + 1) * P, :]).then_inc(b["x_res_loaded"][par], 16)
    for kv in range(NKV):
        sp.dma_start(b["w_out_a"][kv * HD:(kv + 1) * HD, :, :],
                     d["w_out"][kv * G * HD:(kv + 1) * G * HD, :].rearrange("(g d) n -> d g n", d=HD)).then_inc(b["w_out_loaded"], 16)
    sp.dma_start(b["w_r"][:, :, :], d["w_router"].rearrange("(k p) n -> p k n", p=P)).then_inc(b["w_r_loaded"], 16)


def load_expert(sp, b, d, e, par, after_gu=None, after_dn=None):
    if after_gu:
        sp.wait_ge(*after_gu)
    for j, w in enumerate((d["w_gate"], d["w_up"])):
        sp.dma_start(b["w_gu"][:, par, j, :, :], w[one(e), :, :].rearrange("a (k p) n -> p (a k) n", p=P)).then_inc(b["gu_loaded"][par], 16)
    if after_dn:
        sp.wait_ge(*after_dn)
    sp.dma_start(b["w_dn"][:, par, :, :], d["w_down"][one(e), :, :].rearrange("a (k p) n -> p (a k) n", p=P)).then_inc(b["dn_loaded"][par], 16)


OUT_A, OUT_B, M0, M1, M2, M3, PJ0, PJ1 = range(8)
PROJ = (("f", CFB, QW), ("q", CQB, QW), ("qa", CQ, QW), ("kv", CK, 2 * KW), ("i", CIB, QW), ("g", CGB, QW))
NP = len(PROJ)


def slope(h):
    return 2.0 ** (-8.0 * (h + 1) / (NKV * G))


DVE_LINKS = 15


def mixing(nc, b, x, sinks, k_prompt, v_prompt, s_prompt):
    psum, ident, mix_t = b["psum"], b["ident"], b["mix_t"]
    x_in, h_t = b["x_in"], b["h_t"]
    with ExitStack() as ctx:
        def sb(name, shape, dt=F32):
            return ctx.enter_context(nc.sbuf_tensor(name, shape, dt))

        sems = []

        def sem(name):
            sems.append(nc.alloc_semaphore(name))
            return sems[-1]

        ss, rs = sb("ss", [P, 1]), sb("rs", [P, 1])
        qk_ss, qk_rs = sb("qk_ss", [P, 10]), sb("qk_rs", [P, 10])
        eps = sb("eps", [P, 1])
        qk_n = sb("qk_n", [P, QW + KW])
        q_t = sb("q_t", [P, G, P])
        k_t = sb("k_t", [P, 2 * P])
        v_sb = sb("v_sb", [P, 2, KW])
        i_sb = sb("i_sb", [P, QW])
        dist = sb("dist", [P, 2, 2 * P])
        sink = sb("sink", [P, NKV * G])
        score = sb("score", [P, G, 2 * P])
        qk_sq = score[:, :, :].rearrange("p g n -> p (g n)")[:, 0:QW + KW].rearrange("p (h d) -> p h d", d=HD)
        p_t = sb("p_t", [P, 2 * G, P])
        top_s = sb("top_s", [P, G])
        neg_top = sb("neg_top", [P, G])
        sink_e = sb("sink_e", [P, G])
        den = sb("den", [P, NKV, G])
        rec = sb("rec", [P, NKV, G])
        o_a = sb("o_a", [P, G, NKV, HD])
        z_e = sb("z_e", [P, QW])
        log_f = sb("log_f", [P, QW])
        k_b = sb("k_b", [P, QW])
        q_b = sb("q_b", [P, QW])
        cum = sb("cum", [P, QW])
        scan_mask = sb("scan_mask", [P, QW])
        exp_b = sb("exp_b", [P, QW])
        q_e = sb("q_e", [P, QW])
        k_d = sb("k_d", [P, QW])
        kd_tok = z_e
        gap = sb("gap", [P, 2, QW])
        k_l = sb("k_l", [P, 2, QW])
        q_l = sb("q_l", [P, 2, QW // 2])
        pair = sb("pair", [P, 2, 4, P])
        state = sb("state", [P, 4, HD])
        gate = sb("gate", [P, QW])
        gate_e = sb("gate_e", [P, QW])
        o_sq = z_e[:, :].rearrange("p (h d) -> p h d", d=HD)
        o_ss, o_rs = sb("o_ss", [P, 8]), sb("o_rs", [P, 8])
        o_n = k_l[:, 1, :]

        names = """sinks_loaded x_squared x_rs x_normed x_turned h_ready proj_mm proj_out
            act_chain dve_chain pool_chain dist_made state_ready qk_squared qkn_ready qf_turned qk_turned
            z_ready q_ready f_ready k_ready cum_ready expb_ready kgap_ready kexp_ready qt_ready kd_ready
            v_ready i_ready gneg_ready gexp_ready gate_ready
            gap_ready gap_exp lv_ready diag_mm pair_clear lv_mm pair_ready
            score_mm top_ready sinkgap_ready probs_ready probs_turned pt_ready pv_mm oa_ready
            kd_turned kdt_ready state_mm ob_mm osq_ready ob_ready oa_turned ob_turned mix_ready
            stored qkss_ready qk_rs oss_ready o_rs eps_made waits_alone""".split()
        s = {n: sem(n) for n in names}
        ctx.callback(retire, nc, sems)
        block = ctx.enter_context(nc.Block())

        def f4(ap):
            return ap.rearrange("p (c t) -> p c t", t=P)

        def alone(eng):
            eng.sem_inc(s["waits_alone"], 1)

        def inverse_root(squares, out, n, link):
            link(nc.scalar.activation(out, squares, ACT.Ln, scale=1.0 / n, bias=eps[:, :]))
            link(nc.scalar.activation(out, out, ACT.Exp, scale=-0.5))

        def act_norm(act, f):
            act.wait_ge(b["x_loaded"], (f + 1) * 16)
            nc.scalar.activation(p_t[:, :, :].rearrange("p n t -> p (n t)"), x_in[:, :], ACT.Square, accum_out=ss[:, :]).then_inc(s["x_squared"], 1)
            act.wait_ge(s["x_squared"], f + 1)
            inverse_root(ss[:, :], rs[:, :], D, Chain(act, s["x_rs"], 0, f, 2))
            nc.scalar.activation(x_in[:, :], x_in[:, :], ACT.Copy, scale=rs[:, 0:1]).then_inc(s["x_normed"], 1)

        def pe_turn_x(pe, f):
            pe.wait_ge(s["x_normed"], f + 1)
            if not isinstance(f, int) or f > 0:
                pe.wait_ge(s["proj_out"], f * NP)
            for k in range(KC):
                last = pe.transpose(psum[:, PJ0 + k // 4, (k % 4) * P:(k % 4 + 1) * P], x_in[:, k * P:(k + 1) * P], ident[:, :])
            last.then_inc(s["x_turned"], 1)

        def dve_h(dve, f, link):
            kind = bass.ds(f // TP, 1) if not isinstance(f, int) else slice(f // TP, f // TP + 1)
            a = b["mod_a"][:, kind, :, :].rearrange("p a k n -> p (a k) n")
            sh = b["mod_b"][:, kind, :, :].rearrange("p a k n -> p (a k) n")
            dve.wait_ge(s["x_turned"], f + 1)
            h4 = h_t[:, :, :].rearrange("p k (n l) -> p k n l", l=L)
            x4 = psum[:, PJ0:PJ0 + 2, :].rearrange("p a (k n l) -> p (a k) n l", k=4, l=L)
            link(dve.tensor_tensor(h4, x4, bc(a, 3, L), ALU.mult))
            dve.tensor_tensor(h4, h4, bc(sh, 3, L), ALU.add).then_inc(s["h_ready"], 1)

        def pe_project(pe, p, j):
            _, a, n = PROJ[j]
            if j == 0:
                pe.wait_ge(s["h_ready"], p + 1)
            if j >= 2:
                pe.wait_ge(s["proj_out"], p * NP + (j - 1))
            for k in range(KC):
                last = pe.matmul(psum[:, PJ0 + j % 2, 0:n], h_t[:, k, :], b["w_in_sb"][:, k, a:a + n],
                                 start=(k == 0), stop=(k == KC - 1))
            last.then_inc(s["proj_mm"], 1)

        def act_project(act, p, j):
            dst = {"f": b["p_f"][:, :], "q": b["p_q"][:, :], "qa": b["p_qk"][:, 0:QW], "i": b["p_i"][:, :], "g": b["p_g"][:, :]}
            used = {"f": s["qf_turned"], "q": s["qf_turned"], "qa": s["qkn_ready"], "kv": s["v_ready"], "i": s["i_ready"],
                    "g": s["gate_ready"]}
            name, _, n = PROJ[j]
            act.wait_ge(s["proj_mm"], p * NP + (j + 1))
            if not isinstance(p, int):
                act.wait_ge(used[name], p)
            src = psum[:, PJ0 + j % 2, :]
            if name == "kv":
                nc.scalar.activation(b["p_qk"][:, QW:QW + KW], src[:, 0:KW], ACT.Copy)
                nc.scalar.activation(b["p_v"][:, :], src[:, KW:2 * KW], ACT.Copy).then_inc(s["proj_out"], 1)
            else:
                nc.scalar.activation(dst[name], src[:, 0:n], ACT.Copy).then_inc(s["proj_out"], 1)

        @block.sync
        def _(sp):
            sp.dma_start(sink[:, :], sinks.partition_broadcast(P)).then_inc(s["sinks_loaded"], 16)
            sp.wait_ge(s["x_turned"], 1)
            sp.dma_start(x_in[:, :], x[P:2 * P, :]).then_inc(b["x_loaded"], 16)
            with sp.Fori(0, TP) as t:
                sp.wait_ge(s["x_turned"], t + 2)
                sp.dma_start(x_in[:, :], x[bass.ds((t + 2) * P, P), :]).then_inc(b["x_loaded"], 16)
            sp.wait_ge(s["state_ready"], TP + 1)
            sp.wait_ge(s["v_ready"], TP)
            sp.dma_start(k_prompt, qk_n[:, QW:QW + KW]).then_inc(s["stored"], 16)
            sp.dma_start(v_prompt, v_sb[:, 1, :]).then_inc(s["stored"], 16)
            for h in range(2):
                sp.dma_start(s_prompt.rearrange("(c h) k v -> h k c v", h=2)[h], state[h * HD:(h + 1) * HD, :, :]).then_inc(s["stored"], 16)
            sp.wait_ge(s["stored"], 4 * 16)

        @block.tensor
        def _(pe):
            pe_turn_x(pe, 0)
            for j in range(NP):
                pe.wait_ge(b["w_in_loaded"][j], 16)
                pe_project(pe, 0, j)
            pe_turn_x(pe, 1)

            def turn4(dst, src, done):
                for c in range(4):
                    last = pe.transpose(psum[:, dst, c * P:(c + 1) * P], src[:, c * P:(c + 1) * P], ident[:, :])
                last.then_inc(done, 1)

            def turn_qf(t):
                pe.wait_ge(s["proj_out"], t * NP + NP)
                turn4(M0, b["p_q"], s["qf_turned"])
                pe.wait_ge(s["state_ready"], t + 1)
                turn4(M1, b["p_f"], s["qf_turned"])

            turn_qf(0)

            def scores(t, kv):
                for g in range(G):
                    last = pe.matmul(psum[:, M2 + g // 2, (g % 2) * 256:(g % 2) * 256 + 256],
                                     q_t[kv * HD:(kv + 1) * HD, g, :], k_t[kv * HD:(kv + 1) * HD, :], start=True, stop=True)
                last.then_inc(s["score_mm"], 1)

            def turn_probs(t, kv):
                pe.wait_ge(s["probs_ready"], t * 2 + (kv + 1))
                for g in range(G):
                    for half in range(2):
                        n = 2 * g + half
                        last = pe.transpose(psum[:, M2 + n // 4, (n % 4) * P:(n % 4 + 1) * P],
                                            score[:, g, half * P:(half + 1) * P], ident[:, :])
                last.then_inc(s["probs_turned"], 1)

            def values(t, kv):
                pe.wait_ge(s["pt_ready"], t * 2 + (kv + 1))
                pe.wait_ge(s["v_ready"], t + 1)
                for g in range(G):
                    col = (g * NKV + kv) * HD
                    for half in range(2):
                        last = pe.matmul(psum[:, OUT_A, col:col + HD], p_t[:, 2 * g + half, :],
                                         v_sb[:, half, kv * HD:(kv + 1) * HD], start=(half == 0), stop=(half == 1))
                last.then_inc(s["pv_mm"], 1)

            def level(t, i):
                pe.wait_ge(s["lv_ready"], t * len(LEVELS) + (i + 1))
                if i == 0:
                    pe.wait_ge(s["pair_clear"], t + 1)
                else:
                    pe.wait_ge(s["pair_ready"], t * len(LEVELS) + i)
                for h in range(8):
                    r = slice((h % 2) * HD, (h % 2 + 1) * HD)
                    c = h // 2
                    o = psum[:, M0 + h % 2, c * HD:(c + 1) * HD]
                    last = pe.matmul(o, k_l[r, i % 2, c * P:(c + 1) * P], q_l[r, i % 2, c * HD:(c + 1) * HD],
                                     start=True, stop=True)
                    if h >= 6:
                        last.then_inc(s["lv_mm"], 1)

            with pe.Fori(0, TP) as t:
                pe_project(pe, t + 1, 0)
                pe.wait_ge(s["ob_ready"], t + 1)
                turn4(OUT_B, o_n, s["ob_turned"])
                pe.wait_ge(s["qkn_ready"], t + 1)
                for c in range(5):
                    last = pe.transpose(psum[:, M2 + c // 4, (c % 4) * P:(c % 4 + 1) * P], qk_n[:, c * P:(c + 1) * P], ident[:, :])
                last.then_inc(s["qk_turned"], 1)
                pe_project(pe, t + 1, 1)
                pe.wait_ge(s["q_ready"], t + 1)
                pe.wait_ge(s["k_ready"], t + 1)
                for h in range(8):
                    r = slice((h % 2) * HD, (h % 2 + 1) * HD)
                    c = slice((h // 2) * P, (h // 2 + 1) * P)
                    last = pe.matmul(psum[:, M0 + h % 2, c], k_b[r, c], q_b[r, c], start=True, stop=True)
                    if h >= 6:
                        last.then_inc(s["diag_mm"], 1)
                pe.wait_ge(s["qt_ready"], t + 1)
                scores(t, 0)
                level(t, 0)
                pe_project(pe, t + 1, 2)
                level(t, 1)
                turn_probs(t, 0)
                level(t, 2)
                values(t, 0)
                scores(t, 1)
                level(t, 3)
                pe_project(pe, t + 1, 3)
                level(t, 4)
                turn_probs(t, 1)
                level(t, 5)
                pe_project(pe, t + 1, 4)
                values(t, 1)
                level(t, 6)
                pe.wait_ge(s["kd_ready"], t + 1)
                pe.wait_ge(s["mix_ready"], t + 1)
                turn4(OUT_B, k_d[:, :], s["kd_turned"])
                pe_project(pe, t + 1, 5)
                pe.wait_ge(s["kdt_ready"], t + 1)
                pe.wait_ge(s["i_ready"], t + 1)
                pe.wait_ge(s["pair_ready"], t * len(LEVELS) + len(LEVELS))
                for h in range(8):
                    c = h // 2
                    last = pe.matmul(psum[(h % 2) * HD:(h % 2 + 1) * HD, M1, c * HD:(c + 1) * HD],
                                     kd_tok[:, h * HD:(h + 1) * HD], i_sb[:, h * HD:(h + 1) * HD], start=True, stop=True)
                last.then_inc(s["state_mm"], 1)
                pe_turn_x(pe, t + 2)
                pe.wait_ge(s["oa_ready"], t + 1)
                for h in range(8):
                    c = slice((h // 2) * HD, (h // 2 + 1) * HD)
                    pe.matmul(psum[:, OUT_A + h % 2, c], pair[:, h % 2, h // 2, :], i_sb[:, h * HD:(h + 1) * HD],
                              start=(h < 2), stop=False, skip_group_check=True)
                for h in range(8):
                    r = slice((h % 2) * HD, (h % 2 + 1) * HD)
                    c = slice((h // 2) * HD, (h // 2 + 1) * HD)
                    last = pe.matmul(psum[:, OUT_A + h % 2, c], q_e[r, (h // 2) * P:(h // 2 + 1) * P], state[r, h // 2, :],
                                     start=False, stop=True, skip_group_check=True)
                    if h >= 6:
                        last.then_inc(s["ob_mm"], 1)
                turn4(M2, o_a[:, :, :, :].rearrange("p g k d -> p (g k d)"), s["oa_turned"])
                turn_qf(t + 1)
            pe.wait_ge(s["ob_ready"], TP + 1)
            turn4(OUT_B, o_n, s["ob_turned"])

        @block.scalar
        def _(act):
            act.wait_ge(s["eps_made"], 1)
            act_norm(act, 0)
            for j in range(NP):
                if j == NP - 2:
                    act_norm(act, 1)
                act_project(act, 0, j)

            def probs(t, kv):
                act.wait_ge(s["top_ready"], t * 2 + (kv + 1))
                for g in range(G):
                    nc.scalar.activation(score[:, g, :], score[:, g, :], ACT.Exp, bias=neg_top[:, g:g + 1],
                                         accum_out=den[:, kv, g:g + 1])
                act.wait_ge(s["sinkgap_ready"], t * 2 + (kv + 1))
                nc.scalar.activation(sink_e[:, :], sink_e[:, :], ACT.Exp).then_inc(s["probs_ready"], 1)

            def copy_probs(t, kv):
                act.wait_ge(s["probs_turned"], t * 2 + (kv + 1))
                nc.scalar.activation(p_t[:, :, :], psum[:, M2:M2 + 2, :].rearrange("p a (n t) -> p (a n) t", t=P),
                                     ACT.Copy).then_inc(s["pt_ready"], 1)

            def gap_exp(t, i):
                act.wait_ge(s["gap_ready"], t * len(LEVELS) + (i + 1))
                nc.scalar.activation(gap[:, i % 2, :], gap[:, i % 2, :], ACT.Exp).then_inc(s["gap_exp"], 1)

            def keep_ob(before, turned):
                act.wait_ge(s["ob_turned"], turned)
                alone(act)
                tile = mix_t[:, one(before), :, :].rearrange("p a k r -> p (a k) r")
                nc.scalar.activation(tile[:, 4:8, :], f4(psum[:, OUT_B, :]), ACT.Copy).then_inc(s["mix_ready"], 1)

            act.wait_ge(b["rows_stored"], 48)
            with act.Fori(0, TP) as t:
                link = Chain(act, s["act_chain"], 0, t, 3)
                act.wait_ge(s["proj_out"], t * NP + NP)
                nc.scalar.activation(qk_sq[:, :, :].rearrange("p h d -> p (h d)"), b["p_qk"][:, :], ACT.Square).then_inc(s["qk_squared"], 1)
                act.wait_ge(s["qkss_ready"], t + 1)
                inverse_root(qk_ss[:, :], qk_rs[:, :], HD, Chain(act, s["qk_rs"], 0, t, 2))
                act.wait_ge(s["qf_turned"], t * 2 + 2)
                link(nc.scalar.activation(z_e[:, :], psum[:, M1, :], ACT.Abs))
                link(nc.scalar.activation(z_e[:, :], z_e[:, :], ACT.Exp, scale=-1.0))
                nc.scalar.activation(z_e[:, :], z_e[:, :], ACT.Ln, bias=1.0).then_inc(s["z_ready"], 1)
                nc.scalar.activation(q_b[:, :], psum[:, M0, :], ACT.Copy, scale=HD ** -0.5).then_inc(s["q_ready"], 1)
                act.wait_ge(s["qk_turned"], t + 1)
                nc.scalar.activation(q_t[:, :, :], f4(psum[:, M2, :]), ACT.Copy)
                link(nc.scalar.activation(k_t[:, 0:P], k_t[:, P:2 * P], ACT.Copy))
                nc.scalar.activation(k_t[:, P:2 * P], psum[:, M3, 0:P], ACT.Copy).then_inc(s["qt_ready"], 1)
                act.wait_ge(s["f_ready"], t + 1)
                nc.scalar.activation(k_b[:, :], k_b[:, :], ACT.Exp).then_inc(s["k_ready"], 1)
                gap_exp(t, 0)
                keep_ob((t + TP) % NT, t + 1)
                act_project(act, t + 1, 0)
                act.wait_ge(s["cum_ready"], t + 1)
                nc.scalar.activation(exp_b[:, :], cum[:, :], ACT.Exp).then_inc(s["expb_ready"], 1)
                act.wait_ge(s["kgap_ready"], t + 1)
                nc.scalar.activation(k_d[:, :], k_d[:, :], ACT.Exp).then_inc(s["kexp_ready"], 1)
                gap_exp(t, 1)
                act_project(act, t + 1, 1)
                act_norm(act, t + 2)
                gap_exp(t, 2)
                act.wait_ge(s["gneg_ready"], t + 1)
                glink = Chain(act, s["gexp_ready"], 0, t, 3)
                glink(nc.scalar.activation(gate_e[:, :], gate_e[:, :], ACT.Exp, scale=-1.0))
                glink(nc.scalar.activation(gate_e[:, :], gate_e[:, :], ACT.Ln, bias=1.0))
                glink(nc.scalar.activation(gate_e[:, :], gate_e[:, :], ACT.Exp, scale=-1.0))
                probs(t, 0)
                gap_exp(t, 3)
                act_project(act, t + 1, 2)
                copy_probs(t, 0)
                gap_exp(t, 4)
                gap_exp(t, 5)
                probs(t, 1)
                act_project(act, t + 1, 3)
                gap_exp(t, 6)
                copy_probs(t, 1)
                act_project(act, t + 1, 4)
                act.wait_ge(s["kd_turned"], t + 1)
                nc.scalar.activation(kd_tok[:, :], psum[:, OUT_B, :], ACT.Copy).then_inc(s["kdt_ready"], 1)
                act_project(act, t + 1, 5)
                act.wait_ge(s["ob_mm"], t * 2 + 2)
                nc.scalar.activation(o_sq.rearrange("p (a c) d -> p a (c d)", a=2), psum[:, OUT_A:OUT_B + 1, 0:4 * HD],
                                     ACT.Square).then_inc(s["osq_ready"], 1)
                act.wait_ge(s["oss_ready"], t + 1)
                inverse_root(o_ss[:, :], o_rs[:, :], HD, Chain(act, s["o_rs"], 0, t, 2))
                mix_cur = mix_t[:, bass.ds(t, 1), :, :].rearrange("p a k r -> p (a k) r")
                act.wait_ge(s["oa_turned"], t + 1)
                nc.scalar.activation(mix_cur[:, 0:4, :], f4(psum[:, M2, :]), ACT.Copy)
                link.done()
            keep_ob(TP - 1, TP + 1)

        @block.vector
        def _(dve):
            start = Chain(dve, s["state_ready"])
            dve.memset(eps[:, :], EPS).then_inc(s["eps_made"], 1)
            dve.memset(k_t[:, :], 0.0)
            dve.memset(v_sb[:, :, :], 0.0)
            dve.memset(scan_mask[:, :], 1.0)
            link = Chain(dve, s["dve_chain"])
            dve.wait_ge(s["dist_made"], 1)
            link(dve.scalar_tensor_tensor(out=dist[:, 1, :], in0=dist[:, 0, :], scalar=-1.0, in1=dist[:, 0, :],
                                          op0=ALU.mult, op1=ALU.max))
            dve.memset(dist[0:HD, 1, P + HD:2 * P], FAR)
            link(dve.memset(dist[HD:P, 1, 0:HD], FAR))
            link(dve.tensor_copy(dist[:, 0, :], dist[:, 1, :]))
            dve.memset(dist[:, 0, 0:P], FAR)
            link(dve.memset(f4(scan_mask[:, :])[:, :, 0:1], 0.0))
            dve.memset(o_n, 0.0).then_inc(s["ob_ready"], 1)
            start(dve.memset(state[:, :, :], 0.0))
            base = link.k
            for f in range(2):
                n = Chain(dve, s["dve_chain"], base)
                dve_h(dve, f, n)
                base += n.k

            def gaps(t, i):
                h = LEVELS[i]
                if i >= 2:
                    dve.wait_ge(s["lv_ready"], t * len(LEVELS) + (i - 1))
                c = cum[:, :].rearrange("p (n two h) -> p n two h", two=2, h=h)
                g = gap[:, i % 2, :].rearrange("p (n two h) -> p n two h", two=2, h=h)
                mid = last_bc(c[:, :, 0, h - 1:h], h)
                dve.tensor_tensor(g[:, :, 0, :], mid, c[:, :, 0, :], ALU.subtract)
                dve.tensor_tensor(g[:, :, 1, :], c[:, :, 1, :], mid, ALU.subtract).then_inc(s["gap_ready"], 1)

            def decayed(t, i):
                h = LEVELS[i]
                dve.wait_ge(s["gap_exp"], t * len(LEVELS) + (i + 1))
                if i >= 2:
                    dve.wait_ge(s["lv_mm"], t * 2 * len(LEVELS) + 2 * (i - 1))
                second = lambda a: a.rearrange("p (n two h) -> p n two h", two=2, h=h)[:, :, 1, :]
                dve.tensor_tensor(k_l[:, i % 2, :], k_b[:, :], gap[:, i % 2, :], ALU.mult)
                dve.tensor_tensor(q_l[:, i % 2, :].rearrange("p (n h) -> p n h", h=h), second(q_b[:, :]),
                                  second(gap[:, i % 2, :]), ALU.mult).then_inc(s["lv_ready"], 1)

            def place(t, i):
                h = LEVELS[i]
                dve.wait_ge(s["lv_mm"], t * 2 * len(LEVELS) + 2 * (i + 1))
                alone(dve)
                for a in range(2):
                    out = pair[:, a, :, :].rearrange("p e (n two h) -> p e n two h", two=2, h=h)[:, :, :, 1, :]
                    m = bc(b["level_mask"][:, i, :].rearrange("p (n h) -> p n h", h=h).bitcast(I32), 1, 4)
                    src = psum[:, M0 + a, 0:4 * HD].rearrange("p (e n h) -> p e n h", e=4, h=h)
                    last = dve.copy_predicated(out, m, src)
                last.then_inc(s["pair_ready"], 1)

            def tops(t, kv, link):
                dve.wait_ge(s["score_mm"], t * 2 + (kv + 1))
                first = bass.ds((t + (TP - 1)) // TP, 1)
                d = dist[:, first, :].rearrange("p a n -> p (a n)")
                for g in range(G):
                    ins = dve.scalar_tensor_tensor(out=score[:, g, :], in0=d, scalar=-slope(kv * G + g),
                                                   in1=psum[:, M2 + g // 2, (g % 2) * 256:(g % 2) * 256 + 256],
                                                   op0=ALU.mult, op1=ALU.add)
                link(ins)
                link(dve.tensor_reduce(top_s[:, :], score[:, :, :], AX_X, ALU.max))
                link(dve.tensor_tensor(top_s[:, :], top_s[:, :], sink[:, kv * G:(kv + 1) * G], ALU.max))
                dve.tensor_scalar(neg_top[:, :], top_s[:, :], -1.0, None, ALU.mult).then_inc(s["top_ready"], 1)
                dve.tensor_tensor(sink_e[:, :], sink[:, kv * G:(kv + 1) * G], top_s[:, :], ALU.subtract).then_inc(s["sinkgap_ready"], 1)

            def denominators(t, kv, link):
                dve.wait_ge(s["probs_ready"], t * 2 + (kv + 1))
                link(dve.tensor_tensor(den[:, kv, :], den[:, kv, :], sink_e[:, :], ALU.add))
                link(dve.reciprocal(rec[:, kv, :], den[:, kv, :]))

            with dve.Fori(0, TP) as t:
                link = Chain(dve, s["dve_chain"], base, t, DVE_LINKS)
                dve.wait_ge(s["qk_squared"], t + 1)
                dve.tensor_reduce(qk_ss[:, :], qk_sq[:, :, :], AX_X, ALU.add).then_inc(s["qkss_ready"], 1)
                dve.wait_ge(s["qk_rs"], t * 2 + 2)
                link(dve.tensor_tensor(qk_sq[:, :, :], b["p_qk"][:, :].rearrange("p (h d) -> p h d", d=HD), bc(qk_rs[:, :], 2, HD), ALU.mult))
                dve.tensor_tensor(qk_n[:, 0:QW].rearrange("p (g k d) -> p k g d", g=G, d=HD),
                                  qk_sq[:, 0:8, :].rearrange("p (k g) d -> p k g d", g=G),
                                  bc(bc(b["norm_w"][:, 0, :], 1, G), 1, NKV), ALU.mult)
                dve.tensor_tensor(qk_n[:, QW:QW + KW].rearrange("p (k d) -> p k d", d=HD), qk_sq[:, 8:10, :],
                                  bc(b["norm_w"][:, 1, :], 1, NKV), ALU.mult).then_inc(s["qkn_ready"], 1)
                dve.wait_ge(s["z_ready"], t + 1)
                link(dve.scalar_tensor_tensor(out=log_f[:, :], in0=psum[:, M1, :], scalar=0.0, in1=z_e[:, :],
                                              op0=ALU.min, op1=ALU.subtract))
                dve.tensor_tensor(k_b[:, :], log_f[:, :], psum[:, M1, :], ALU.subtract).then_inc(s["f_ready"], 1)
                dve.tensor_tensor_scan(cum[:, :], scan_mask[:, :], log_f[:, :], 0.0, ALU.mult, ALU.add).then_inc(s["cum_ready"], 1)
                dve.wait_ge(s["cum_ready"], t + 1)
                gaps(t, 0)
                dve.tensor_tensor(f4(k_d[:, :]), last_bc(f4(cum[:, :])[:, :, P - 1:P], P), f4(cum[:, :]), ALU.subtract).then_inc(s["kgap_ready"], 1)
                gaps(t, 1)
                dve.wait_ge(s["k_ready"], t + 1)
                dve.wait_ge(s["q_ready"], t + 1)
                decayed(t, 0)
                dve.wait_ge(s["diag_mm"], t * 2 + 2)
                dve.tensor_tensor(pair[:, :, :, :].rearrange("p a h t -> p (a h) t"), psum[:, M0:M0 + 2, :].rearrange("p a (h t) -> p (a h) t", t=P),
                                  bc(ident[:, :], 1, 8), ALU.mult).then_inc(s["pair_clear"], 1)
                gaps(t, 2)
                decayed(t, 1)
                tops(t, 0, link)
                dve.wait_ge(s["pair_clear"], t + 1)
                place(t, 0)
                gaps(t, 3)
                decayed(t, 2)
                place(t, 1)
                denominators(t, 0, link)
                gaps(t, 4)
                decayed(t, 3)
                place(t, 2)
                gaps(t, 5)
                tops(t, 1, link)
                decayed(t, 4)
                place(t, 3)
                gaps(t, 6)
                decayed(t, 5)
                place(t, 4)
                denominators(t, 1, link)
                decayed(t, 6)
                place(t, 5)
                dve.wait_ge(s["pv_mm"], t * 2 + 2)
                dve.tensor_tensor(o_a[:, :, :, :], psum[:, OUT_A, :].rearrange("p (g k d) -> p g k d", g=G, d=HD),
                                  bc(rec[:, :, :].rearrange("p k g -> p g k"), 3, HD), ALU.mult).then_inc(s["oa_ready"], 1)
                place(t, 6)
                dve_h(dve, t + 2, link)
                dve.wait_ge(s["ob_mm"], t * 2 + 2)
                link(dve.tensor_tensor(state[:, :, :], state[:, :, :],
                                       last_bc(f4(exp_b[:, :])[:, :, P - 1:P], HD), ALU.mult))
                dve.tensor_tensor(state[:, :, :], state[:, :, :], psum[:, M1, 0:4 * HD].rearrange("p (c v) -> p c v", v=HD),
                                  ALU.add).then_inc(s["state_ready"], 1)
                dve.wait_ge(s["osq_ready"], t + 1)
                dve.tensor_reduce(o_ss[:, :], o_sq[:, :, :], AX_X, ALU.add).then_inc(s["oss_ready"], 1)
                dve.wait_ge(s["o_rs"], t * 2 + 2)
                for a in range(2):
                    ins = dve.tensor_tensor(o_n.rearrange("p (c a d) -> p a c d", a=2, d=HD)[:, a],
                                            psum[:, OUT_A + a, 0:4 * HD].rearrange("p (c d) -> p c d", d=HD),
                                            bc(o_rs[:, 4 * a:4 * a + 4], 2, HD), ALU.mult)
                link(ins)
                dve.wait_ge(s["gate_ready"], t + 1)
                dve.tensor_tensor(o_n, o_n, gate[:, :], ALU.mult).then_inc(s["ob_ready"], 1)
                link.done()

        @block.gpsimd
        def _(pool):
            pool.iota(dist[:, 0, :], pattern=[[-1, 2 * P]], base=P, channel_multiplier=1,
                      allow_small_or_imprecise_dtypes=True).then_inc(s["dist_made"], 1)
            with pool.Fori(0, TP) as t:
                link = Chain(pool, s["pool_chain"], 0, t, 2)
                pool.wait_ge(s["proj_out"], t * NP + NP)
                alone(pool)
                pool.tensor_scalar(gate_e[:, :], b["p_g"][:, :], -87.0, None, ALU.max).then_inc(s["gneg_ready"], 1)
                pool.wait_ge(s["qk_turned"], t + 1)
                alone(pool)
                link(pool.tensor_copy(v_sb[:, 0, :], v_sb[:, 1, :]))
                alone(pool)
                pool.tensor_copy(v_sb[:, 1, :], b["p_v"][:, :]).then_inc(s["v_ready"], 1)
                pool.tensor_copy(i_sb[:, :], b["p_i"][:, :]).then_inc(s["i_ready"], 1)
                pool.wait_ge(s["expb_ready"], t + 1)
                pool.wait_ge(s["q_ready"], t + 1)
                pool.tensor_tensor(q_e[:, :], q_b[:, :], exp_b[:, :], ALU.mult)
                pool.wait_ge(s["kexp_ready"], t + 1)
                pool.wait_ge(s["k_ready"], t + 1)
                pool.tensor_tensor(k_d[:, :], k_b[:, :], k_d[:, :], ALU.mult).then_inc(s["kd_ready"], 1)
                pool.wait_ge(s["gexp_ready"], t * 3 + 3)
                link(pool.tensor_tensor(gate[:, :], b["p_g"][:, :], gate_e[:, :], ALU.mult))
                g3 = gate[:, :].rearrange("p (h d) -> p h d", d=HD)
                pool.tensor_tensor(g3, g3, bc(b["o_norm_w"][:, :], 1, 8), ALU.mult).then_inc(s["gate_ready"], 1)
                link.done()



def sampling(nc, b, d, sinks, cache_k, cache_v, state_in, k_sample, v_sample, s_sample):
    psum, ident, mix_t = b["psum"], b["ident"], b["mix_t"]
    KS = WIN + L
    BP = NB // 2
    FIRST_LEVEL = LEVELS.index(L // 2)
    NL = len(LEVELS) - FIRST_LEVEL
    with ExitStack() as ctx:
        def sb(name, shape, dt=F32):
            return ctx.enter_context(nc.sbuf_tensor("s_" + name, shape, dt))

        def sem(name):
            return ctx.enter_context(nc.semaphore("s_" + name))

        cache_k_sb = sb("cache_k_sb", [P, NB, KW])
        cache_v_sb = sb("cache_v_sb", [P, NB, KW])
        v_new = sb("v_new", [L, NB, KW])
        state = sb("state", [P, 4, NB, HD])
        sink = sb("sink", [P, NKV])
        rows_i = sb("rows_i", [P, 4], I32)
        frame = sb("frame", [P, 1])
        slope_p = sb("slope_p", [P, 1])
        dist = sb("dist", [P, KS])
        dist_n = sb("dist_n", [P, KS])
        penalty = sb("penalty", [P, NKV, KS])
        sq = sb("sq", [P, 10, HD])
        ss, rs = sb("ss", [P, 10]), sb("rs", [P, 10])
        eps = sb("eps", [P, 1])
        qk_n = sb("qk_n", [P, QW + KW])
        q_t = sb("q_t", [P, NB, G * L])
        k_new_t = sb("k_new_t", [P, P])
        cache_t = sb("cache_t", [P, NB, P])
        score = sb("score", [P, NKV, BP, KS])
        top_s, neg_top, sink_e = (sb(n, [P, NKV, BP]) for n in ("top_s", "neg_top", "sink_e"))
        den, rec = sb("den", [P, NKV, BP]), sb("rec", [P, NKV, BP])
        pc_t = sb("pc_t", [P, 8, P])
        pn_t = sb("pn_t", [L, 8, P])
        o_a = sb("o_a", [P, BP, NKV, HD])
        z_e, log_f, k_b, q_b, cum, scan_mask, exp_b, q_e, k_d, kd_tok, gate, gate_e, o_n = (
            sb(n, [P, QW]) for n in "z_e log_f k_b q_b cum scan_mask exp_b q_e k_d kd_tok gate gate_e o_n".split())
        gap = sb("gap", [P, NL, QW])
        k_l = gap
        q_l = sb("q_l", [P, NL, QW // 2])
        pair = sb("pair", [P, 2, 4, P])
        row_of = sb("row_of", [P, NB])
        q_m = sb("q_m", [P, 4, NB * (P + L)])
        i_m = sb("i_m", [P, 8, NB, HD])
        new_state = i_m[:, 0:4, :, :]
        o_sq = sb("o_sq", [P, 8, HD])
        o_ss, o_rs = sb("o_ss", [P, 8]), sb("o_rs", [P, 8])

        names = """cache_loaded cachev_loaded sink_loaded state_loaded vnew_loaded consts act_chain dve_chain pool_chain rows_made
            q_squared ss_ready qk_rs qkn_ready cache_turned qk_turned qf_turned cache_t_ready qt_ready z_ready
            q_ready f_ready k_ready cum_ready expb_ready kgap_ready kexp_ready qe_ready kd_ready
            gneg_ready gate_exp gate_ready gap_ready gap_exp lv_ready diag_mm pair_clear lv_mm pair_ready score_mm
            top_ready probs_ready pc_turned pt_ready pv_mm oa_ready kd_turned kdt_ready im_ready state_mm
            ob_mm osq_ready oss_ready o_rs ob_ready oa_turned ob_turned state_ready stored penalty_ready""".split()
        s = {n: sem(n) for n in names}
        block = ctx.enter_context(nc.Block())

        def f4(ap):
            return ap.rearrange("p (c t) -> p c t", t=P)

        def by_request(ap):
            return ap.rearrange("p (n l) -> p n l", l=L)

        @block.sync
        def _(sp):
            sp.dma_start(cache_k_sb[:, :, :], cache_k.rearrange("b r n -> r b n")).then_inc(s["cache_loaded"], 16)
            for n in range(NB):
                sp.dma_start(v_new[:, n, :], b["p_v"][n * L:(n + 1) * L, :]).then_inc(s["vnew_loaded"], 16)
            with nc.allow_non_contiguous_dma("one sink a row"):
                for par in range(2):
                    for g in range(G):
                        r = slice(par * HD + g * L, par * HD + (g + 1) * L)
                        sp.dma_start(sink[r, :], sinks.rearrange("(k g) -> g k", g=G)[g].partition_broadcast(L)).then_inc(s["sink_loaded"], 16)
            for n in range(NB):
                for h in range(2):
                    sp.dma_start(state[h * HD:(h + 1) * HD, :, n, :],
                                 state_in[n].rearrange("(c h) k v -> h k c v", h=2)[h]).then_inc(s["state_loaded"], 16)
            sp.dma_start(cache_v_sb[:, :, :], cache_v.rearrange("b r n -> r b n")).then_inc(s["cachev_loaded"], 16)
            sp.dma_start(v_sample, b["p_v"][:, :]).then_inc(s["stored"], 16)
            load_output_operands(sp, b, d)
            sp.wait_ge(s["qkn_ready"], 1)
            sp.dma_start(k_sample, qk_n[:, QW:QW + KW]).then_inc(s["stored"], 16)
            sp.wait_ge(s["state_ready"], 1)
            for n in range(NB):
                for h in range(2):
                    sp.dma_start(s_sample[n].rearrange("(c h) k v -> h k c v", h=2)[h],
                                 new_state[h * HD:(h + 1) * HD, :, n, :]).then_inc(s["stored"], 16)
            sp.wait_ge(s["stored"], 18 * 16)

        @block.gpsimd
        def _(pool):
            link = Chain(pool, s["pool_chain"])
            pool.iota(rows_i[:, 0:1], pattern=[[0, 1]], base=0, channel_multiplier=1).then_inc(s["rows_made"], 1)
            pool.iota(dist[:, :], pattern=[[-1, KS]], base=WIN, channel_multiplier=0,
                      allow_small_or_imprecise_dtypes=True).then_inc(s["rows_made"], 1)
            link(pool.memset(row_of[:, :], 1.0))
            link(pool.affine_select(out=row_of[:, :], in_=row_of[:, :], compare_op=ALU.is_ge, fill=0.0, base=0,
                                    pattern=[[-L, NB]], channel_multiplier=1))
            link(pool.affine_select(out=row_of[:, :], in_=row_of[:, :], compare_op=ALU.is_ge, fill=0.0, base=L - 1,
                                    pattern=[[L, NB]], channel_multiplier=-1))
            pool.tensor_scalar(gate_e[:, :], b["p_g"][:, :], -87.0, None, ALU.max).then_inc(s["gneg_ready"], 1)
            link(pool.memset(q_m[:, :, :], 0.0))
            for h in range(8):
                ins = pool.tensor_tensor(i_m[:, h, :, :], bc(b["p_i"][:, h * HD:(h + 1) * HD], 1, NB),
                                         bc(row_of[:, :], 2, HD), ALU.mult)
            ins.then_inc(s["im_ready"], 1)
            pool.wait_ge(s["expb_ready"], 1)
            pool.wait_ge(s["q_ready"], 1)
            for c in range(4):
                ins = pool.tensor_tensor(q_m[:, c, :].rearrange("p (n w) -> p n w", w=P + L)[:, :, 0:L],
                                         by_request(q_b[:, c * P:(c + 1) * P]), by_request(exp_b[:, c * P:(c + 1) * P]), ALU.mult)
            ins.then_inc(s["qe_ready"], 1)
            pool.wait_ge(s["kexp_ready"], 1)
            pool.wait_ge(s["k_ready"], 1)
            pool.tensor_tensor(k_d[:, :], k_b[:, :], k_d[:, :], ALU.mult).then_inc(s["kd_ready"], 1)
            pool.wait_ge(s["gate_exp"], 3)
            link(pool.tensor_tensor(gate[:, :], b["p_g"][:, :], gate_e[:, :], ALU.mult))
            g3 = gate[:, :].rearrange("p (h d) -> p h d", d=HD)
            pool.tensor_tensor(g3, g3, bc(b["o_norm_w"][:, :], 1, 8), ALU.mult).then_inc(s["gate_ready"], 1)

        @block.tensor
        def _(pe):
            for c in range(4):
                pe.transpose(psum[:, PJ0, c * P:(c + 1) * P], b["p_q"][:, c * P:(c + 1) * P], ident[:, :])
            for c in range(4):
                last = pe.transpose(psum[:, PJ1, c * P:(c + 1) * P], b["p_f"][:, c * P:(c + 1) * P], ident[:, :])
            last.then_inc(s["qf_turned"], 1)
            pe.wait_ge(s["cache_loaded"], 16)
            for n in range(NB):
                last = pe.transpose(psum[:, M0 + n // 4, (n % 4) * P:(n % 4 + 1) * P], cache_k_sb[:, n, :], ident[:, :])
            last.then_inc(s["cache_turned"], 1)
            pe.wait_ge(s["qkn_ready"], 1)
            for c in range(5):
                last = pe.transpose(psum[:, M2 + c // 4, (c % 4) * P:(c % 4 + 1) * P], qk_n[:, c * P:(c + 1) * P], ident[:, :])
            last.then_inc(s["qk_turned"], 1)
            pe.wait_ge(s["cache_t_ready"], 1)
            pe.wait_ge(s["qt_ready"], 1)
            for kv in range(NKV):
                r = slice(kv * HD, (kv + 1) * HD)
                for n in range(NB):
                    bp, par = n // 2, n % 2
                    o = psum[par * HD:(par + 1) * HD, M0 + 2 * kv + bp // 2, (bp % 2) * 256:(bp % 2) * 256 + KS]
                    q = q_t[r, n, :]
                    pe.matmul(o[:, 0:WIN], q, cache_t[r, n, :], start=True, stop=True)
                    last = pe.matmul(o[:, WIN:KS], q, k_new_t[r, n * L:(n + 1) * L], start=True, stop=True)
                last.then_inc(s["score_mm"], 1)
            pe.wait_ge(s["q_ready"], 1)
            pe.wait_ge(s["k_ready"], 1)
            for h in range(8):
                r = slice((h % 2) * HD, (h % 2 + 1) * HD)
                c = slice((h // 2) * P, (h // 2 + 1) * P)
                last = pe.matmul(psum[:, PJ0 + h % 2, c], k_b[r, c], q_b[r, c], start=True, stop=True)
                if h >= 6:
                    last.then_inc(s["diag_mm"], 1)

            def level(i):
                pe.wait_ge(s["lv_ready"], i + 1)
                if i == 0:
                    pe.wait_ge(s["pair_clear"], 1)
                else:
                    pe.wait_ge(s["pair_ready"], i)
                for h in range(8):
                    r = slice((h % 2) * HD, (h % 2 + 1) * HD)
                    c = h // 2
                    last = pe.matmul(psum[:, PJ0 + h % 2, c * HD:(c + 1) * HD], k_l[r, i, c * P:(c + 1) * P],
                                     q_l[r, i, c * HD:(c + 1) * HD], start=True, stop=True)
                    if h >= 6:
                        last.then_inc(s["lv_mm"], 1)

            level(0)
            level(1)
            pe.wait_ge(s["probs_ready"], 1)
            for n in range(8):
                kv, bp = n // BP, n % BP
                last = pe.transpose(psum[:, M0 + n // 4, (n % 4) * P:(n % 4 + 1) * P], score[:, kv, bp, 0:WIN], ident[:, :])
            for n in range(8):
                kv, bp = n // BP, n % BP
                last = pe.transpose(psum[0:L, M2 + n // 4, (n % 4) * P:(n % 4 + 1) * P], score[:, kv, bp, WIN:KS], ident[:, :])
            last.then_inc(s["pc_turned"], 1)
            level(2)
            level(3)
            pe.wait_ge(s["pt_ready"], 2)
            pe.wait_ge(s["cachev_loaded"], 16)
            pe.wait_ge(s["vnew_loaded"], NB * 16)
            for n in range(8):
                kv, bp = n // BP, n % BP
                v = slice(kv * HD, (kv + 1) * HD)
                for par in range(2):
                    q = slice(par * HD, (par + 1) * HD)
                    o = psum[q, OUT_A, n * HD:(n + 1) * HD]
                    pe.matmul(o, pc_t[:, n, q], cache_v_sb[:, 2 * bp + par, v], start=True, stop=False)
                    last = pe.matmul(o, pn_t[:, n, q], v_new[:, 2 * bp + par, v], start=False, stop=True)
            last.then_inc(s["pv_mm"], 1)
            pe.wait_ge(s["kd_ready"], 1)
            for c in range(4):
                last = pe.transpose(psum[:, OUT_B, c * P:(c + 1) * P], k_d[:, c * P:(c + 1) * P], ident[:, :])
            last.then_inc(s["kd_turned"], 1)
            pe.wait_ge(s["kdt_ready"], 1)
            pe.wait_ge(s["im_ready"], 1)
            pe.wait_ge(s["pair_ready"], NL)
            for h in range(8):
                last = pe.matmul(psum[(h % 2) * HD:(h % 2 + 1) * HD, M0 + h // 2, :], kd_tok[:, h * HD:(h + 1) * HD],
                                 i_m[:, h, :, :].rearrange("p n v -> p (n v)"), start=True, stop=True)
            last.then_inc(s["state_mm"], 1)
            pe.wait_ge(s["oa_ready"], 1)
            pe.wait_ge(s["qe_ready"], 1)
            pe.wait_ge(s["state_loaded"], 2 * NB * 16)
            for h in range(8):
                c = slice((h // 2) * HD, (h // 2 + 1) * HD)
                pe.matmul(psum[:, PJ0 + h % 2, c], pair[:, h % 2, h // 2, :], b["p_i"][:, h * HD:(h + 1) * HD],
                          start=(h < 2), stop=False, skip_group_check=True)
            for n in range(NB):
                for h in range(8):
                    r = slice((h % 2) * HD, (h % 2 + 1) * HD)
                    c = slice((h // 2) * HD, (h // 2 + 1) * HD)
                    last = pe.matmul(psum[:, PJ0 + h % 2, c], q_m[r, h // 2, n * P:(n + 1) * P], state[r, h // 2, n, :],
                                     start=False, stop=(n == NB - 1), skip_group_check=True)
                    if n == NB - 1 and h >= 6:
                        last.then_inc(s["ob_mm"], 1)
            for bp in range(BP):
                last = pe.transpose(psum[:, OUT_A, bp * P:(bp + 1) * P], o_a[:, bp, :, :].rearrange("p k d -> p (k d)"), ident[:, :])
            last.then_inc(s["oa_turned"], 1)
            pe.wait_ge(s["ob_ready"], 1)
            for c in range(4):
                last = pe.transpose(psum[:, OUT_B, c * P:(c + 1) * P], o_n[:, c * P:(c + 1) * P], ident[:, :])
            last.then_inc(s["ob_turned"], 1)

        @block.scalar
        def _(act):
            a = nc.scalar.activation
            link = Chain(act, s["act_chain"])

            def inverse_root(squares, out, n, link):
                link(a(out, squares, ACT.Ln, scale=1.0 / n, bias=eps[:, :]))
                link(a(out, out, ACT.Exp, scale=-0.5))

            a(sq[:, :, :].rearrange("p h d -> p (h d)"), b["p_qk"][:, :], ACT.Square).then_inc(s["q_squared"], 1)
            act.wait_ge(s["qf_turned"], 1)
            link(a(z_e[:, :], psum[:, PJ1, :], ACT.Abs))
            link(a(z_e[:, :], z_e[:, :], ACT.Exp, scale=-1.0))
            a(z_e[:, :], z_e[:, :], ACT.Ln, bias=1.0).then_inc(s["z_ready"], 1)
            a(q_b[:, :], psum[:, PJ0, :], ACT.Copy, scale=HD ** -0.5).then_inc(s["q_ready"], 1)
            act.wait_ge(s["consts"], 1)
            act.wait_ge(s["ss_ready"], 1)
            inverse_root(ss[:, :], rs[:, :], HD, Chain(act, s["qk_rs"]))
            act.wait_ge(s["cache_turned"], 1)
            a(cache_t[:, :, :], psum[:, M0:M0 + 2, :].rearrange("p a (n t) -> p (a n) t", t=P), ACT.Copy).then_inc(s["cache_t_ready"], 1)
            act.wait_ge(s["f_ready"], 1)
            a(k_b[:, :], k_b[:, :], ACT.Exp).then_inc(s["k_ready"], 1)
            act.wait_ge(s["qk_turned"], 1)
            a(q_t[:, :, :].rearrange("p n (g l) -> p g n l", g=G), psum[:, M2, :].rearrange("p (g n l) -> p g n l", g=G, l=L), ACT.Copy)
            a(k_new_t[:, :], psum[:, M3, 0:P], ACT.Copy).then_inc(s["qt_ready"], 1)
            for i in range(NL):
                act.wait_ge(s["gap_ready"], i + 1)
                a(gap[:, i, :], gap[:, i, :], ACT.Exp).then_inc(s["gap_exp"], 1)
            act.wait_ge(s["cum_ready"], 1)
            a(exp_b[:, :], cum[:, :], ACT.Exp).then_inc(s["expb_ready"], 1)
            act.wait_ge(s["kgap_ready"], 1)
            a(k_d[:, :], k_d[:, :], ACT.Exp).then_inc(s["kexp_ready"], 1)
            act.wait_ge(s["top_ready"], 2)
            for n in range(8):
                kv, bp = n // BP, n % BP
                a(score[:, kv, bp, :], score[:, kv, bp, :], ACT.Exp, bias=neg_top[:, kv, bp:bp + 1],
                  accum_out=den[:, kv, bp:bp + 1])
            a(sink_e[:, :, :], sink_e[:, :, :], ACT.Exp).then_inc(s["probs_ready"], 1)
            act.wait_ge(s["pc_turned"], 1)
            a(pc_t[:, :, :], psum[:, M0:M0 + 2, :].rearrange("p a (n t) -> p (a n) t", t=P), ACT.Copy).then_inc(s["pt_ready"], 1)
            a(pn_t[:, :, :], psum[0:L, M2:M2 + 2, :].rearrange("p a (n t) -> p (a n) t", t=P), ACT.Copy).then_inc(s["pt_ready"], 1)
            act.wait_ge(s["gneg_ready"], 1)
            glink = Chain(act, s["gate_exp"])
            glink(a(gate_e[:, :], gate_e[:, :], ACT.Exp, scale=-1.0))
            glink(a(gate_e[:, :], gate_e[:, :], ACT.Ln, bias=1.0))
            glink(a(gate_e[:, :], gate_e[:, :], ACT.Exp, scale=-1.0))
            act.wait_ge(s["kd_turned"], 1)
            a(kd_tok[:, :], psum[:, OUT_B, :], ACT.Copy).then_inc(s["kdt_ready"], 1)
            act.wait_ge(s["ob_mm"], 2)
            a(o_sq[:, :, :].rearrange("p (a c) d -> p a (c d)", a=2), psum[:, PJ0:PJ0 + 2, 0:4 * HD], ACT.Square).then_inc(s["osq_ready"], 1)
            act.wait_ge(s["oss_ready"], 1)
            inverse_root(o_ss[:, :], o_rs[:, :], HD, Chain(act, s["o_rs"]))
            act.wait_ge(s["oa_turned"], 1)
            for bp in range(BP):
                a(mix_t[:, TP, 0:G, bp * 2 * L:(bp + 1) * 2 * L].rearrange("p g (a l) -> p a g l", a=2),
                  psum[:, OUT_A, bp * P:(bp + 1) * P].rearrange("p (a g l) -> p a g l", a=2, g=G), ACT.Copy)
            act.wait_ge(s["ob_turned"], 1)
            a(mix_t[:, TP, 4:8, :], f4(psum[:, OUT_B, :]), ACT.Copy)

        @block.vector
        def _(dve):
            link = Chain(dve, s["dve_chain"])
            link(dve.memset(scan_mask[:, :], 1.0))
            dve.memset(by_request(scan_mask[:, :])[:, :, 0:1], 0.0)
            dve.memset(eps[:, :], EPS).then_inc(s["consts"], 1)
            dve.wait_ge(s["q_squared"], 1)
            dve.tensor_reduce(ss[:, :], sq[:, :, :], AX_X, ALU.add).then_inc(s["ss_ready"], 1)
            dve.wait_ge(s["z_ready"], 1)
            link(dve.scalar_tensor_tensor(out=log_f[:, :], in0=psum[:, PJ1, :], scalar=0.0, in1=z_e[:, :],
                                          op0=ALU.min, op1=ALU.subtract))
            dve.tensor_tensor(k_b[:, :], log_f[:, :], psum[:, PJ1, :], ALU.subtract).then_inc(s["f_ready"], 1)
            dve.tensor_tensor_scan(cum[:, :], scan_mask[:, :], log_f[:, :], 0.0, ALU.mult, ALU.add).then_inc(s["cum_ready"], 1)
            dve.wait_ge(s["qk_rs"], 2)
            link(dve.tensor_tensor(sq[:, :, :], b["p_qk"][:, :].rearrange("p (h d) -> p h d", d=HD), bc(rs[:, :], 2, HD), ALU.mult))
            dve.tensor_tensor(qk_n[:, 0:QW].rearrange("p (g k d) -> p k g d", g=G, d=HD),
                              sq[:, 0:8, :].rearrange("p (k g) d -> p k g d", g=G),
                              bc(bc(b["norm_w"][:, 0, :], 1, G), 1, NKV), ALU.mult)
            dve.tensor_tensor(qk_n[:, QW:QW + KW].rearrange("p (k d) -> p k d", d=HD), sq[:, 8:10, :],
                              bc(b["norm_w"][:, 1, :], 1, NKV), ALU.mult).then_inc(s["qkn_ready"], 1)
            dve.wait_ge(s["rows_made"], 2)
            link(dve.tensor_scalar(rows_i[:, 1:2], rows_i[:, 0:1], L - 1, None, ALU.bitwise_and))
            link(dve.tensor_scalar(rows_i[:, 2:3], rows_i[:, 0:1], 4, G - 1, ALU.logical_shift_right, ALU.bitwise_and))
            link(dve.tensor_scalar(rows_i[:, 2:3], rows_i[:, 2:3], -1, 126, ALU.mult, ALU.add))
            link(dve.tensor_scalar(rows_i[:, 2:3], rows_i[:, 2:3], 23, None, ALU.logical_shift_left))
            dve.tensor_copy(frame[:, :], rows_i[:, 1:2])
            link(dve.tensor_copy(slope_p[:, :], rows_i[:, 2:3].bitcast(F32)))
            link(dve.tensor_scalar(dist[:, :], dist[:, :], frame[:, 0:1], None, ALU.add))
            link(dve.tensor_scalar(dist_n[:, :], dist[:, :], -1.0, None, ALU.mult))
            link(dve.tensor_tensor(dist[:, :], dist[:, :], dist_n[:, :], ALU.max))
            link(dve.tensor_scalar(dist[:, :], dist[:, :], slope_p[:, 0:1], None, ALU.mult))
            for kv in range(NKV):
                ins = dve.tensor_scalar(penalty[:, kv, :], dist[:, :], -slope(kv * G) / slope(0), None, ALU.mult)
            link(ins)
            dve.wait_ge(s["cum_ready"], 1)
            for i in range(NL):
                h = LEVELS[FIRST_LEVEL + i]
                c = cum[:, :].rearrange("p (n two h) -> p n two h", two=2, h=h)
                g = gap[:, i, :].rearrange("p (n two h) -> p n two h", two=2, h=h)
                mid = last_bc(c[:, :, 0, h - 1:h], h)
                dve.tensor_tensor(g[:, :, 0, :], mid, c[:, :, 0, :], ALU.subtract)
                dve.tensor_tensor(g[:, :, 1, :], c[:, :, 1, :], mid, ALU.subtract).then_inc(s["gap_ready"], 1)
            dve.tensor_tensor(by_request(k_d[:, :]), last_bc(by_request(cum[:, :])[:, :, L - 1:L], L),
                              by_request(cum[:, :]), ALU.subtract).then_inc(s["kgap_ready"], 1)
            dve.wait_ge(s["score_mm"], 2)
            for kv in range(NKV):
                src = psum[:, M0 + 2 * kv:M0 + 2 * kv + 2, :].rearrange("p a (b n) -> p a b n", b=2)[:, :, :, 0:KS]
                for a in range(2):
                    ins = dve.tensor_tensor(score[:, kv, 2 * a:2 * a + 2, :], src[:, a], bc(penalty[:, kv, :], 1, 2), ALU.add)
            link(ins)
            link(dve.tensor_reduce(top_s[:, :, :].rearrange("p k n -> p (k n)"), score[:, :, :, :].rearrange("p k n j -> p (k n) j"),
                                   AX_X, ALU.max))
            dve.wait_ge(s["sink_loaded"], 8 * 16)
            link(dve.tensor_tensor(top_s[:, :, :], top_s[:, :, :], bc(sink[:, :], 2, BP), ALU.max))
            dve.tensor_scalar(neg_top[:, :, :], top_s[:, :, :], -1.0, None, ALU.mult).then_inc(s["top_ready"], 1)
            dve.tensor_tensor(sink_e[:, :, :], bc(sink[:, :], 2, BP), top_s[:, :, :], ALU.subtract).then_inc(s["top_ready"], 1)
            dve.wait_ge(s["diag_mm"], 2)
            dve.tensor_tensor(pair[:, :, :, :].rearrange("p a h t -> p (a h) t"),
                              psum[:, PJ0:PJ0 + 2, :].rearrange("p a (h t) -> p (a h) t", t=P),
                              bc(ident[:, :], 1, 8), ALU.mult).then_inc(s["pair_clear"], 1)
            dve.wait_ge(s["k_ready"], 1)
            for i in range(NL):
                h = LEVELS[FIRST_LEVEL + i]
                dve.wait_ge(s["gap_exp"], i + 1)
                second = lambda a: a.rearrange("p (n two h) -> p n two h", two=2, h=h)[:, :, 1, :]
                link(dve.tensor_tensor(q_l[:, i, :].rearrange("p (n h) -> p n h", h=h), second(q_b[:, :]),
                                       second(gap[:, i, :]), ALU.mult))
                dve.tensor_tensor(k_l[:, i, :], k_b[:, :], gap[:, i, :], ALU.mult).then_inc(s["lv_ready"], 1)
            dve.wait_ge(s["pair_clear"], 1)
            for i in range(NL):
                h = LEVELS[FIRST_LEVEL + i]
                dve.wait_ge(s["lv_mm"], 2 * (i + 1))
                for a in range(2):
                    out = pair[:, a, :, :].rearrange("p e (n two h) -> p e n two h", two=2, h=h)[:, :, :, 1, :]
                    m = bc(b["level_mask"][:, FIRST_LEVEL + i, :].rearrange("p (n h) -> p n h", h=h).bitcast(I32), 1, 4)
                    src = psum[:, PJ0 + a, 0:4 * HD].rearrange("p (e n h) -> p e n h", e=4, h=h)
                    ins = dve.copy_predicated(out, m, src)
                ins.then_inc(s["pair_ready"], 1)
            dve.wait_ge(s["probs_ready"], 1)
            link(dve.tensor_tensor(den[:, :, :], den[:, :, :], sink_e[:, :, :], ALU.add))
            link(dve.reciprocal(rec[:, :, :], den[:, :, :]))
            dve.wait_ge(s["pv_mm"], 1)
            dve.tensor_tensor(o_a[:, :, :, :], psum[:, OUT_A, :].rearrange("p (k n d) -> p n k d", k=NKV, d=HD),
                              bc(rec[:, :, :].rearrange("p k n -> p n k"), 3, HD), ALU.mult).then_inc(s["oa_ready"], 1)
            dve.wait_ge(s["state_mm"], 1)
            dve.wait_ge(s["state_loaded"], 2 * NB * 16)
            last = last_bc(by_request(exp_b[:, :])[:, :, L - 1:L], HD)
            old, new = (ap.rearrange("p c n v -> p (c n) v") for ap in (state[:, :, :, :], new_state))
            link(dve.tensor_tensor(new, old, last, ALU.mult))
            dve.tensor_tensor(new, new, psum[:, M0:M0 + 4, :].rearrange("p c (n v) -> p (c n) v", v=HD), ALU.add).then_inc(s["state_ready"], 1)
            dve.wait_ge(s["osq_ready"], 1)
            dve.tensor_reduce(o_ss[:, :], o_sq[:, :, :], AX_X, ALU.add).then_inc(s["oss_ready"], 1)
            dve.wait_ge(s["o_rs"], 2)
            for a in range(2):
                ins = dve.tensor_tensor(o_n[:, :].rearrange("p (c a d) -> p a c d", a=2, d=HD)[:, a],
                                        psum[:, PJ0 + a, 0:4 * HD].rearrange("p (c d) -> p c d", d=HD),
                                        bc(o_rs[:, 4 * a:4 * a + 4], 2, HD), ALU.mult)
            link(ins)
            dve.wait_ge(s["gate_ready"], 1)
            dve.tensor_tensor(o_n[:, :], o_n[:, :], gate[:, :], ALU.mult).then_inc(s["ob_ready"], 1)


def output(nc, b, d):
    psum, ident, mix_t = b["psum"], b["ident"], b["mix_t"]
    with ExitStack() as ctx:
        def sb(name, shape, dt=F32):
            return ctx.enter_context(nc.sbuf_tensor("r_" + name, shape, dt))

        def sem(name):
            return ctx.enter_context(nc.semaphore("r_" + name))

        w_r, x_in = b["w_r"], b["x_res"]
        w_out_half = b["w_out_a"], sb("w_out_b", [P, KC - G, D])
        table = sb("table", [P, 3, 2, D])
        x2 = sb("x2", [P, 2, D])
        w_h, w_l = sb("w_h", [P, KC, D], F32R), sb("w_l", [P, KC, D], F32R)
        lhs_h, lhs_l = sb("lhs_h", [P, KC, P], F32R), sb("lhs_l", [P, KC, P], F32R)
        h2 = sb("h2", [P, D])
        h2_t = sb("h2_t", [P, KC, P])
        zeros = sb("zeros", [P, D // 2])
        ss, rs, eps = sb("ss", [P, 1]), sb("rs", [P, 1]), sb("eps", [P, 1])

        names = """w_b_loaded table_loaded zeros_made eps_made zeros_stored wh_ready wl_ready lhs_h_ready lhs_ready lhs_used
            x1_ready x2_ready waits_alone squared rs_ready xn_ready scaled h2_ready h2_stored h2_turned h2t_ready
            logit_mm logit_ready x20_stored x21_stored""".split()
        s = {n: sem(n) for n in names}
        x_loaded = b["x_res_loaded"]
        x2_stored = (s["x20_stored"], s["x21_stored"])
        block = ctx.enter_context(nc.Block())

        def heads(t, half):
            return mix_t[:, one(t), 4 * half:4 * half + 4, :].rearrange("p a k r -> p (a k) r")

        @block.sync
        def _(sp):
            sp.dma_start(w_out_half[1][:, :, :], d["w_out"][QW:2 * QW, :].rearrange("(c p) n -> p c n", p=P)).then_inc(s["w_b_loaded"], 16)
            for i in range(3):
                sp.dma_start(table[:, i, 0, :], d["mod_rows"][0, i * D:(i + 1) * D].partition_broadcast(P)).then_inc(s["table_loaded"], 16)
                for n in range(NB):
                    sp.dma_start(table[n * L:(n + 1) * L, i, 1, :],
                                 d["mod_rows"][n + 1, i * D:(i + 1) * D].partition_broadcast(L)).then_inc(s["table_loaded"], 16)
            sp.wait_ge(s["zeros_made"], 1)
            for half in (slice(0, D // 2), slice(D // 2, D)):
                sp.dma_start(d["h2"][ROWS:TABLE, half], zeros[:, :]).then_inc(s["zeros_stored"], 16)
                sp.dma_start(d["y"][ROWS:TABLE, half], zeros[:, :]).then_inc(s["zeros_stored"], 16)

            def store(t, par):
                rows = slice(t * P, (t + 1) * P) if isinstance(t, int) else bass.ds(t * P, P)
                sp.wait_ge(s["x2_ready"], t + 1)
                sp.dma_start(d["y"][rows, :], x2[:, par, :]).then_inc(x2_stored[par], 16)
                sp.wait_ge(s["h2_ready"], t + 1)
                sp.dma_start(d["h2"][rows, :], h2[:, :]).then_inc(s["h2_stored"], 16)

            with sp.Fori(0, TP // 2) as i:
                for par in range(2):
                    store(i * 2 + par, par)
                    sp.dma_start(x_in[:, par, :], d["x"][bass.ds((i * 2 + (par + 2)) * P, P), :]).then_inc(x_loaded[par], 16)
            store(NT - 1, 0)
            sp.wait_ge(x_loaded[1], 16 * (TP // 2 + 1))
            sp.wait_ge(s["h2_stored"], 16 * NT)
            sp.wait_ge(s["zeros_stored"], 64)
            sp.wait_ge(x2_stored[0], 16 * (TP // 2 + 1))
            sp.wait_ge(x2_stored[1], 16 * (TP // 2))

        @block.gpsimd
        def _(pool):
            pool.memset(zeros[:, :], 0.0).then_inc(s["zeros_made"], 1)

        @block.tensor
        def _(pe):
            def project(t, par, half):
                pe.wait_ge(s["lhs_ready"], t * 2 + (half + 1))
                if half == 0 and not (isinstance(t, int) and t < 2):
                    pe.wait_ge(s["x1_ready"], t - 1)
                for k in range(4 * half, 4 * half + 4):
                    for n in range(2):
                        cols = slice(n * 512, (n + 1) * 512)
                        wh, wl = w_h[:, k, cols], w_l[:, k, cols]
                        out = psum[:, par * 2 + n, :]
                        pe.matmul(out, lhs_h[:, k, :], wh, start=(k == 0), stop=False)
                        pe.matmul(out, lhs_h[:, k, :], wl, start=False, stop=False)
                        last = pe.matmul(out, lhs_l[:, k, :], wh, start=False, stop=(k == KC - 1))
                last.then_inc(s["lhs_used"], 1)

            def turn(t):
                pe.wait_ge(s["h2_ready"], t + 1)
                for k in range(KC):
                    last = pe.transpose(psum[:, 4 + k // 4, (k % 4) * P:(k % 4 + 1) * P], h2[:, k * P:(k + 1) * P], ident[:, :])
                last.then_inc(s["h2_turned"], 1)

            def logits(t):
                pe.wait_ge(s["h2t_ready"], t + 1)
                if not (isinstance(t, int) and t == 0):
                    pe.wait_ge(s["logit_ready"], t)
                for k in range(KC):
                    last = pe.matmul(psum[:, 6, 0:NE], h2_t[:, k, :], w_r[:, k, :], start=(k == 0), stop=(k == KC - 1))
                last.then_inc(s["logit_mm"], 1)

            def turn_one(t, par):
                project(t, par, 0)
                if not (isinstance(t, int) and t < 2):
                    logits(t - 2)
                project(t, par, 1)
                turn(t - 1)

            pe.wait_ge(b["w_r_loaded"], 16)
            pe.wait_ge(s["wl_ready"], KC // 2)
            project(0, 0, 0)
            pe.wait_ge(s["wl_ready"], KC)
            project(0, 0, 1)
            turn_one(1, 1)
            turn_one(2, 0)
            with pe.Fori(1, TP // 2) as i:
                turn_one(i * 2 + 1, 1)
                turn_one(i * 2 + 2, 0)
            logits(NT - 2)
            turn(NT - 1)
            logits(NT - 1)

        @block.scalar
        def _(act):
            a = nc.scalar.activation

            def norm(t, par):
                act.wait_ge(s["x2_ready"], t + 1)
                x2t = x2[:, par, :]
                a(h2[:, :], x2t, ACT.Square, accum_out=ss[:, :]).then_inc(s["squared"], 1)
                act.wait_ge(s["squared"], t + 1)
                link = Chain(act, s["rs_ready"], 0, t, 2)
                link(a(rs[:, :], ss[:, :], ACT.Ln, scale=1.0 / D, bias=eps[:, :]))
                link(a(rs[:, :], rs[:, :], ACT.Exp, scale=-0.5))
                a(h2[:, :], x2t, ACT.Copy, scale=rs[:, 0:1]).then_inc(s["xn_ready"], 1)

            def keep(t):
                act.wait_ge(s["h2_turned"], t + 1)
                a(h2_t[:, :, :], psum[:, 4:6, :].rearrange("p a (k r) -> p (a k) r", r=P), ACT.Copy).then_inc(s["h2t_ready"], 1)

            def high(t, half):
                if not (isinstance(t, int) and t == 0):
                    act.wait_ge(s["lhs_used"], t * 2 + (half - 1))
                    act.sem_inc(s["waits_alone"], 1)
                a(lhs_h[:, 4 * half:4 * half + 4, :], heads(t, half), ACT.Copy).then_inc(s["lhs_h_ready"], 1)

            act.wait_ge(b["w_out_loaded"], 32)
            high(0, 0)
            for k in range(KC):
                if k == KC // 2:
                    high(0, 1)
                    act.wait_ge(s["w_b_loaded"], 16)
                a(w_h[:, k, :], w_out_half[k // 4][:, k % 4, :], ACT.Copy).then_inc(s["wh_ready"], 1)
            act.wait_ge(s["eps_made"], 1)

            def turn(i, par):
                t = i * 2 + (2 - par)
                high(t, 0)
                high(t, 1)
                if not (isinstance(t, int) and t == 1):
                    keep(t - 2)
                    act.wait_ge(s["h2_stored"], (t - 1) * 16)
                norm(t - 1, 1 - par)

            turn(0, 1)
            turn(0, 0)
            with act.Fori(1, TP // 2) as i:
                turn(i, 1)
                turn(i, 0)
            keep(TP - 1)
            act.wait_ge(s["h2_stored"], TP * 16)
            norm(TP, 0)
            keep(TP)

        @block.vector
        def _(dve):
            dve.memset(eps[:, :], EPS).then_inc(s["eps_made"], 1)

            def row(i, t):
                return table[:, i, tile_kind(t), :].rearrange("p a n -> p (a n)")

            def residual(t, par):
                x2t = x2[:, par, :]
                dve.wait_ge(s["lhs_used"], t * 2 + 2)
                dve.tensor_tensor(x2t.rearrange("p (a n) -> p a n", a=2), psum[:, par * 2:par * 2 + 2, :],
                                  row(0, t).rearrange("p (a n) -> p a n", a=2), ALU.mult).then_inc(s["x1_ready"], 1)
                dve.wait_ge(s["x1_ready"], t + 1)
                dve.tensor_tensor(x2t, x2t, x_in[:, par, :], ALU.add).then_inc(s["x2_ready"], 1)
                dve.wait_ge(s["xn_ready"], t + 1)
                dve.tensor_tensor(h2[:, :], h2[:, :], row(2, t), ALU.mult).then_inc(s["scaled"], 1)
                dve.wait_ge(s["scaled"], t + 1)
                dve.tensor_tensor(h2[:, :], h2[:, :], row(1, t), ALU.add).then_inc(s["h2_ready"], 1)

            def keep_logits(t):
                dve.wait_ge(s["logit_mm"], t + 1)
                dve.tensor_copy(b["logit"][:, one(t), :].rearrange("p a n -> p (a n)"), psum[:, 6, 0:NE]).then_inc(s["logit_ready"], 1)

            def rest(t, half):
                dve.wait_ge(s["lhs_h_ready"], t * 2 + (half + 1))
                part = slice(4 * half, 4 * half + 4)
                dve.tensor_tensor(lhs_l[:, part, :], heads(t, half), lhs_h[:, part, :].bitcast(F32), ALU.subtract).then_inc(s["lhs_ready"], 1)

            rest(0, 0)
            for k in range(KC):
                if k == KC // 2:
                    rest(0, 1)
                dve.wait_ge(s["wh_ready"], k + 1)
                dve.tensor_tensor(w_l[:, k, :], w_out_half[k // 4][:, k % 4, :], w_h[:, k, :].bitcast(F32), ALU.subtract).then_inc(s["wl_ready"], 1)
            dve.wait_ge(s["table_loaded"], 27 * 16)

            def turn(i, par):
                t = i * 2 + (2 - par)
                rest(t, 0)
                rest(t, 1)
                dve.wait_ge(x_loaded[1 - par], (i + 1) * 16)
                if not (isinstance(t, int) and t < 3):
                    dve.wait_ge(x2_stored[1 - par], i * 16)
                residual(t - 1, 1 - par)
                if not (isinstance(t, int) and t == 1):
                    keep_logits(t - 2)

            turn(0, 1)
            turn(0, 0)
            with dve.Fori(1, TP // 2) as i:
                turn(i, 1)
                turn(i, 0)
            keep_logits(TP - 1)
            dve.wait_ge(x_loaded[0], (TP // 2 + 1) * 16)
            dve.wait_ge(x2_stored[0], TP // 2 * 16)
            residual(TP, 0)
            keep_logits(TP)


def route(nc, b, d, router_bias):
    psum, ident = b["psum"], b["ident"]
    with ExitStack() as ctx:
        def sb(name, shape, dt=F32):
            return ctx.enter_context(nc.sbuf_tensor("q_" + name, shape, dt))

        def sem(name):
            return ctx.enter_context(nc.semaphore("q_" + name))

        NG4 = NT * NG
        bias = sb("bias", [P, NE])
        aff, sel, tmp = (sb(n, [P, NT, NE]) for n in ("aff", "sel", "tmp"))
        beats, equal = (sb(n, [P, NG4, 4, 4]) for n in ("beats", "equal"))
        lower = sb("lower", [P, 4, 4])
        rank, best2, vs = (sb(n, [P, NG4, 4]) for n in ("rank", "best2", "vs"))
        g_score, g_rank, g_sel = (sb(n, [P, NT, NG]) for n in ("g_score", "g_rank", "g_sel"))
        pick = sb("pick", [P, 2, NT, NE])
        both = sb("both", [P, NT, NE])
        before_row = sb("before_row", [P, P])
        ones = sb("ones", [P, P])
        tile_sum, before = sb("tile_sum", [P, NT, NE]), sb("before", [P, NT, NE])
        count, n_list, end, first, ones_e = (sb(n, [P, NE]) for n in ("count", "n_list", "end", "first", "ones_e"))
        steps = sb("steps", [P, NT])
        many = sb("many", [P, NE, NT])
        place = sb("place", [P, NT, NE])
        chosen = sb("chosen", [P, 2, NT, NE])
        pos = sb("pos", [P, 2, NT])
        pos_i, list_i = sb("pos_i", [P, 2, NT], I32), sb("list_i", [P, 2, NT], I32)
        place_f, list_f = sb("place_f", [P, 2, NT]), sb("list_f", [P, 2, NT])
        row_no = sb("row_no", [P, NT])
        at_place = sb("at_place", [P, 2 * NT, P])
        in_list = sb("in_list", [P, 2 * NT, SLOTS])
        entry = sb("entry", [P, 2 * NT, 3, SLOTS])
        place_no, empty = sb("place_no", [P, P]), sb("empty", [P, SLOTS])
        empty_row = sb("empty_row", [P, 1])
        w_k, w_sum = sb("w_k", [P, 2, NT]), sb("w_sum", [P, NT])
        list_no = sb("list_no", [P, SLOTS])
        over = sb("over", [P, SLOTS, NE])
        expert = sb("expert", [P, SLOTS])
        other, next_e, others = (sb(n, [P, SLOTS - 1]) for n in ("other", "next_e", "others"))
        kind = sb("kind", [P, SLOTS], I32)

        names = "bias_loaded pool_made chain nlogit_ready e_ready counted both_ready entries_ready lists_made".split()
        s = {n: sem(n) for n in names}
        block = ctx.enter_context(nc.Block())

        @block.sync
        def _(sp):
            sp.dma_start(bias[:, :], router_bias.partition_broadcast(P)).then_inc(s["bias_loaded"], 16)
            sp.sem_inc(b["gu_loaded"][1], 1)
            sp.sem_inc(b["dn_loaded"][1], 1)
            for e in range(2):
                load_expert(sp, b, d, e, e)

        @block.gpsimd
        def _(pool):
            small = dict(allow_small_or_imprecise_dtypes=True)
            pool.iota(place_no[:, :], pattern=[[1, P]], base=0, channel_multiplier=0, **small)
            pool.iota(empty_row[:, :], pattern=[[0, 1]], base=ROWS, channel_multiplier=1, **small)
            pool.iota(row_no[:, :], pattern=[[P, NT]], base=0, channel_multiplier=1, **small)
            pool.iota(steps[:, :], pattern=[[P, NT]], base=0, channel_multiplier=0, **small)
            pool.iota(list_no[:, :], pattern=[[1, SLOTS]], base=0, channel_multiplier=0, **small)
            pool.memset(ones[:, :], 1.0)
            pool.memset(ones_e[:, :], 1.0)
            pool.memset(before[:, 0, :], 0.0).then_inc(s["pool_made"], 1)
            pool.wait_ge(s["pool_made"], 1)
            pool.affine_select(out=before_row[:, :], in_=ones[:, :], compare_op=ALU.is_gt, fill=0.0, base=0,
                               pattern=[[1, P]], channel_multiplier=-1)
            pool.affine_select(out=lower[:, :, :], in_=ones[:, 0:16].rearrange("p (e j) -> p e j", e=4), compare_op=ALU.is_gt,
                               fill=0.0, base=0, pattern=[[1, 4], [-1, 4]], channel_multiplier=0).then_inc(s["pool_made"], 1)

        @block.scalar
        def _(act):
            act.wait_ge(s["nlogit_ready"], 1)
            nc.scalar.activation(tmp[:, :, :], tmp[:, :, :], ACT.Exp, scale=-1.0).then_inc(s["e_ready"], 1)

        @block.tensor
        def _(pe):
            pe.wait_ge(s["pool_made"], 2)
            pe.wait_ge(s["both_ready"], 1)
            flat = both[:, :, :].rearrange("p t e -> p (t e)")
            pe.matmul(psum[:, 0, 0:NT * NE], before_row[:, :], flat, start=True, stop=True)
            pe.matmul(psum[:, 1, 0:NT * NE], ones[:, :], flat, start=True, stop=True).then_inc(s["counted"], 1)
            pe.wait_ge(s["entries_ready"], 1)
            for n in range(2 * NT):
                last = pe.matmul(psum[:, 2, 0:3 * SLOTS], at_place[:, n, :], entry[:, n, :, :].rearrange("p a s -> p (a s)"),
                                 start=(n == 0), stop=(n == 2 * NT - 1))
            last.then_inc(s["lists_made"], 1)

        @block.vector
        def _(dve):
            link = Chain(dve, s["chain"])

            def outrank(values, out, n):
                v_e, v_j = bc(values, 3, 4), bc(values, 2, 4)
                link(dve.tensor_tensor(beats[:, 0:n], v_j, v_e, ALU.is_gt))
                link(dve.tensor_tensor(equal[:, 0:n], v_j, v_e, ALU.is_equal))
                link(dve.tensor_tensor(equal[:, 0:n], equal[:, 0:n], bc(lower[:, :, :], 1, n), ALU.mult))
                link(dve.tensor_tensor(beats[:, 0:n], beats[:, 0:n], equal[:, 0:n], ALU.add))
                link(dve.tensor_reduce(out, beats[:, 0:n], AX_X, ALU.add))

            dve.tensor_scalar(tmp[:, :, :], b["logit"][:, :, :], -87.0, None, ALU.max).then_inc(s["nlogit_ready"], 1)
            dve.wait_ge(s["e_ready"], 1)
            link(dve.tensor_scalar(tmp[:, :, :], tmp[:, :, :], 1.0, None, ALU.add))
            link(dve.reciprocal(aff[:, :, :], tmp[:, :, :]))
            dve.wait_ge(s["bias_loaded"], 16)
            link(dve.tensor_tensor(sel[:, :, :], aff[:, :, :], bc(bias[:, :], 1, NT), ALU.add))
            dve.wait_ge(s["pool_made"], 2)
            by_group = sel[:, :, :].rearrange("p t (g e) -> p (t g) e", e=4)
            outrank(by_group, rank[:, :, :], NG4)
            link(dve.tensor_scalar(best2[:, :, :], rank[:, :, :], 1.5, None, ALU.is_lt))
            link(dve.tensor_tensor(vs[:, :, :], by_group, best2[:, :, :], ALU.mult))
            link(dve.tensor_reduce(g_score[:, :, :].rearrange("p t g -> p (t g)"), vs[:, :, :], AX_X, ALU.add))
            outrank(g_score[:, :, :], g_rank[:, :, :], NT)
            link(dve.tensor_scalar(g_sel[:, :, :], g_rank[:, :, :], 0.5, None, ALU.is_lt))
            g_all = g_sel[:, :, :].rearrange("p t g -> p (t g)")
            for k in range(2):
                ins = dve.scalar_tensor_tensor(out=pick[:, k].rearrange("p t (g e) -> p (t g) e", e=4), in0=rank[:, :, :],
                                               scalar=float(k), in1=bc(g_all, 2, 4), op0=ALU.is_equal, op1=ALU.mult)
            link(ins)
            dve.tensor_tensor(both[:, :, :], pick[:, 0], pick[:, 1], ALU.add).then_inc(s["both_ready"], 1)
            link(dve.tensor_tensor(chosen[:, :, :, :], pick[:, :, :, :], bc(aff[:, :, :], 1, 2), ALU.mult))
            link(dve.tensor_reduce(w_k[:, :, :], chosen[:, :, :, :], AX_X, ALU.add))
            link(dve.tensor_tensor(w_sum[:, :], w_k[:, 0], w_k[:, 1], ALU.add))
            link(dve.reciprocal(w_sum[:, :], w_sum[:, :]))
            link(dve.tensor_tensor(w_k[:, :, :], w_k[:, :, :], bc(w_sum[:, :], 1, 2), ALU.mult))
            dve.wait_ge(s["counted"], 1)
            link(dve.tensor_copy(tile_sum[:, :, :].rearrange("p t e -> p (t e)"), psum[:, 1, 0:NT * NE]))
            for t in range(1, NT):
                link(dve.tensor_tensor(before[:, t, :], before[:, t - 1, :], tile_sum[:, t - 1, :], ALU.add))
            link(dve.tensor_tensor(count[:, :], before[:, NT - 1, :], tile_sum[:, NT - 1, :], ALU.add))
            link(dve.tensor_tensor(many[:, :, :], bc(count[:, :], 2, NT), bc(steps[:, :], 1, NE), ALU.is_gt))
            link(dve.tensor_reduce(n_list[:, :], many[:, :, :], AX_X, ALU.add))
            link(dve.tensor_tensor_scan(end[:, :], ones_e[:, :], n_list[:, :], 0.0, ALU.mult, ALU.add))
            link(dve.tensor_tensor(first[:, :], end[:, :], n_list[:, :], ALU.subtract))
            link(dve.tensor_tensor(place[:, :, :].rearrange("p t e -> p (t e)"), psum[:, 0, 0:NT * NE],
                                   before[:, :, :].rearrange("p t e -> p (t e)"), ALU.add))
            link(dve.scalar_tensor_tensor(out=place[:, :, :], in0=bc(first[:, :], 1, NT), scalar=float(P), in1=place[:, :, :],
                                          op0=ALU.mult, op1=ALU.add))
            link(dve.tensor_tensor(chosen[:, :, :, :], pick[:, :, :, :], bc(place[:, :, :], 1, 2), ALU.mult))
            link(dve.tensor_reduce(pos[:, :, :], chosen[:, :, :, :], AX_X, ALU.add))
            link(dve.tensor_copy(pos_i[:, :, :], pos[:, :, :]))
            link(dve.tensor_scalar(list_i[:, :, :], pos_i[:, :, :], 7, None, ALU.logical_shift_right))
            link(dve.tensor_scalar(pos_i[:, :, :], pos_i[:, :, :], P - 1, None, ALU.bitwise_and))
            dve.tensor_copy(list_f[:, :, :], list_i[:, :, :])
            link(dve.tensor_copy(place_f[:, :, :], pos_i[:, :, :]))
            flat = lambda ap: ap.rearrange("p k t -> p (k t)")
            dve.tensor_tensor(at_place[:, :, :], bc(place_no[:, :], 1, 2 * NT), bc(flat(place_f[:, :, :]), 2, P), ALU.is_equal)
            link(dve.tensor_tensor(in_list[:, :, :], bc(list_no[:, :], 1, 2 * NT), bc(flat(list_f[:, :, :]), 2, SLOTS), ALU.is_equal))
            dve.tensor_copy(entry[:, :, 2, :], in_list[:, :, :])
            for k in range(2):
                tiles = slice(k * NT, (k + 1) * NT)
                dve.tensor_tensor(entry[:, tiles, 0, :], in_list[:, tiles, :], bc(row_no[:, :], 2, SLOTS), ALU.mult)
            dve.tensor_tensor(entry[:, :, 1, :], in_list[:, :, :], bc(flat(w_k[:, :, :]), 2, SLOTS), ALU.mult).then_inc(s["entries_ready"], 1)
            link(dve.tensor_tensor(over[:, :, :], bc(list_no[:, :], 2, NE), bc(end[:, :], 1, SLOTS), ALU.is_ge))
            link(dve.tensor_reduce(expert[:, :], over[:, :, :], AX_X, ALU.add))
            dve.tensor_copy(b["list_info"][:, 0:SLOTS], expert[0:1, :])
            dve.tensor_copy(b["list_info"][:, ENDS:ENDS + NE], end[0:1, :])
            link(dve.tensor_tensor(other[:, :], expert[:, 1:SLOTS], expert[:, 0:SLOTS - 1], ALU.is_gt))
            link(dve.scalar_tensor_tensor(out=other[:, :], in0=list_no[:, 1:SLOTS], scalar=end[:, NE - 1:NE], in1=other[:, :],
                                          op0=ALU.is_lt, op1=ALU.mult))
            link(dve.tensor_tensor(next_e[:, :], other[:, :], expert[:, 1:SLOTS], ALU.mult))
            link(dve.tensor_tensor_scan(others[:, :], ones[:, 0:SLOTS - 1], other[:, :], 0.0, ALU.mult, ALU.add))
            dve.tensor_copy(b["list_info"][:, SPLIT:SPLIT + SLOTS - 1], next_e[0:1, :])
            dve.tensor_copy(b["list_info"][:, NTH:NTH + SLOTS - 1], others[0:1, :])
            dve.tensor_scalar(b["list_info"][:, LAST:LAST + 1], end[0:1, NE - 1:NE], -1.0, None, ALU.add)
            dve.wait_ge(s["lists_made"], 1)
            dve.tensor_copy(b["list_gate"][:, :], psum[:, 2, SLOTS:2 * SLOTS])
            link(dve.tensor_scalar(empty[:, :], psum[:, 2, 2 * SLOTS:3 * SLOTS], 0.5, None, ALU.is_lt))
            link(dve.scalar_tensor_tensor(out=b["list_row"][:, :], in0=empty[:, :], scalar=empty_row[:, 0:1], in1=psum[:, 2, 0:SLOTS],
                                          op0=ALU.mult, op1=ALU.add))
            link(dve.tensor_scalar(kind[:, :], b["list_row"][:, :], -(TP * P - L), 0, ALU.add, ALU.max))
            link(dve.tensor_scalar(kind[:, :], kind[:, :], 4, None, ALU.logical_shift_right))
            link(dve.tensor_scalar(b["list_kind"][:, :], kind[:, :], NB, None, ALU.min))


def experts(nc, b, d):
    psum, ident = b["psum"], b["ident"]
    KD = DE // P
    with ExitStack() as ctx:
        def sb(name, shape, dt=F32):
            return ctx.enter_context(nc.sbuf_tensor("e_" + name, shape, dt))

        def sem(name):
            return ctx.enter_context(nc.semaphore("e_" + name))

        w_gu, w_dn, gu_loaded, dn_loaded = b["w_gu"], b["w_dn"], b["gu_loaded"], b["dn_loaded"]
        free = b["mix_t"][:, :, :, :].rearrange("p t k r -> p (t k r)")
        x_g, y_s, gate_g = (free[:, i * 2 * D:(i + 1) * 2 * D].rearrange("p (a n) -> p a n", a=2) for i in range(3))
        y_end = free[:, 6 * D:7 * D]
        w_h = sb("w_h", [P, 2, 2, KC, DE], F32R)
        x_h, x_l = sb("x_h", [P, KC, P], F32R), sb("x_l", [P, KC, P], F32R)
        silu, u, u_t = (free[:, 7 * D + i * DE:7 * D + (i + 1) * DE] for i in range(3))
        u_t = u_t.rearrange("p (k r) -> p k r", r=P)
        from_now = [sb(f"from{par}", [P, 1], I32) for par in range(2)]
        kind_now = [sb(f"kind{par}", [P, 1], I32) for par in range(2)]
        to_now = [sb(f"to{par}", [P, 1], I32) for par in range(2)]
        to_end = sb("to_end", [P, 1], I32)

        def by_parity(name):
            return [sem(f"{name}{par}") for par in range(2)]

        gathered, gates_in, stored = (by_parity(n) for n in ("gathered", "gates_in", "stored"))
        names = "index_ready waits_alone x_turned xh_ready xl_ready wh_ready gu_mm silu_ready u_ready u_turned ut_ready dn_mm y_ready end_stored".split()
        s = {n: sem(n) for n in names}
        block = ctx.enter_context(nc.Block())


        def steps(eng, body):
            end = eng.value_load(b["list_info"][0:1, LAST:LAST + 1], min_val=2 * NT - 1, max_val=LISTS - 1)
            body(0, 0, -1)
            body(1, 1, 0)
            body(2, 0, 0)
            with eng.Fori(1, (LISTS - 1) // 2) as i:
                with eng.If(end > i * 2):
                    body(i * 2 + 1, 1, i)
                with eng.If(end > i * 2 + 1):
                    body(i * 2 + 2, 0, i)
            return end

        def after(base, t):
            return slice(base + t, base + t + 1) if isinstance(t, int) else bass.ds(t + base, 1)

        def part(w, slot, k):
            return w[:, slot, :, k, :].rearrange("p a j n -> p (a j) n")

        def is_first(t):
            return isinstance(t, int) and t == 0

        def stored_before(eng, t, par, i):
            if not isinstance(t, int):
                eng.wait_ge(stored[1 - par], i * 16)

        @block.sync
        def _(sp):
            def load(e, par):
                done = sp.value_load(b["list_info"][0:1, bass.ds(e + (SLOTS - 2), 1)], min_val=0, max_val=LISTS)
                load_expert(sp, b, d, e, par, (s["gu_mm"], done + 1), (s["dn_mm"], done + 1))

            with sp.Fori(1, NE // 2) as i:
                load(i * 2, 0)
                load(i * 2 + 1, 1)
            for par in range(2):
                sp.wait_ge(gu_loaded[par], NE * 16 + par)
                sp.wait_ge(dn_loaded[par], NE // 2 * 16 + par)

        @block.gpsimd
        def _(pool):
            def index(now, of, count):
                alone()
                pool.tensor_copy(now[:, :], of).then_inc(s["index_ready"], 1)
                pool.wait_ge(s["index_ready"], count)

            def alone():
                pool.sem_inc(s["waits_alone"], 1)

            def fetch(par):
                alone()
                pool.indirect_dma_start(out=x_g[:, par, :], out_offset=None, in_=d["h2"],
                                        in_offset=bass.IndirectOffsetOnAxis(ap=from_now[par][:, 0:1], axis=0)).then_inc(gathered[par], 16)

            def fetch_gates(par):
                alone()
                pool.indirect_dma_start(out=gate_g[:, par, :], out_offset=None, in_=d["out_gate"],
                                        in_offset=bass.IndirectOffsetOnAxis(ap=kind_now[par][:, 0:1], axis=0)).then_inc(gates_in[par], 16)

            for par in range(2):
                index(from_now[par], b["list_row"][:, par:par + 1], par * 2 + 1)
                fetch(par)
                index(kind_now[par], b["list_kind"][:, par:par + 1], par * 2 + 2)
                fetch_gates(par)

            def step(t, par, i):
                pool.wait_ge(s["x_turned"], t + 1)
                index(from_now[par], b["list_row"][:, one(t + 2)], t * 3 + (5 if is_first(t) else 3))
                fetch(par)
                if not is_first(t):
                    stored_before(pool, t, par, i)
                    index(to_now[1 - par], b["list_row"][:, one(t - 1)], t * 3 + 4)
                    if not (isinstance(t, int) and t < 2):
                        pool.wait_ge(stored[par], (i + (1 - par)) * 16)
                        alone()
                    pool.wait_ge(s["y_ready"], t + 1)
                    alone()
                    pool.indirect_dma_start(out=d["y"], out_offset=bass.IndirectOffsetOnAxis(ap=to_now[1 - par][:, 0:1], axis=0),
                                            in_=y_s[:, 1 - par, :], in_offset=None, compute_op=ALU.add).then_inc(stored[1 - par], 16)
                    index(kind_now[1 - par], b["list_kind"][:, one(t + 1)], t * 3 + 5)
                    fetch_gates(1 - par)

            end = steps(pool, step)
            index(to_end, b["list_row"][:, bass.ds(end, 1)], end * 3 + 6)
            pool.wait_ge(s["y_ready"], end + 2)
            alone()
            pool.wait_ge(stored[0], (end + 1) // 2 * 16)
            alone()
            pool.wait_ge(stored[1], end // 2 * 16)
            alone()
            pool.indirect_dma_start(out=d["y"], out_offset=bass.IndirectOffsetOnAxis(ap=to_end[:, 0:1], axis=0),
                                    in_=y_end[:, :], in_offset=None, compute_op=ALU.add).then_inc(s["end_stored"], 16)
            pool.wait_ge(s["end_stored"], 16)
            pool.wait_ge(gathered[0], (end + 4) // 2 * 16)
            pool.wait_ge(gathered[1], (end + 3) // 2 * 16)
            pool.wait_ge(gates_in[0], (end + 3) // 2 * 16)
            pool.wait_ge(gates_in[1], (end + 2) // 2 * 16)

        @block.tensor
        def _(pe):
            pe.sem_inc(s["gu_mm"], 1)
            pe.sem_inc(s["dn_mm"], 1)

            def expert(t):
                return pe.value_load(b["list_info"][0:1, one(t)], min_val=0, max_val=NE - 1)

            def turn_x(t, par, nth):
                pe.wait_ge(gathered[par], nth * 16)
                for k in range(KC):
                    last = pe.transpose(psum[:, 2 + k // 4, (k % 4) * P:(k % 4 + 1) * P], x_g[:, par, k * P:(k + 1) * P], ident[:, :])
                last.then_inc(s["x_turned"], 1)

            def hidden(t):
                slot = bass.ds(expert(t) % 2, 1)
                pe.wait_ge(s["xl_ready"], t + 1)
                if not is_first(t):
                    pe.wait_ge(s["u_ready"], t)
                for k in range(KC):
                    for j in range(2):
                        wh = w_h[:, slot, j, k, :].rearrange("p a n -> p (a n)")
                        wl = w_gu[:, slot, j, k, :].rearrange("p a n -> p (a n)").bitcast(F32R)
                        pe.matmul(psum[:, j, :], x_h[:, k, :], wh, start=(k == 0), stop=False)
                        pe.matmul(psum[:, j, :], x_h[:, k, :], wl, start=False, stop=False)
                        last = pe.matmul(psum[:, j, :], x_l[:, k, :], wh, start=False, stop=(k == KC - 1))
                last.then_inc(s["gu_mm"], 1)

            def down(t):
                e = expert(t)
                slot = bass.ds(e % 2, 1)
                pe.wait_ge(dn_loaded[0], (e // 2 + 1) * 16)
                pe.wait_ge(dn_loaded[1], (e + 1) // 2 * 16 + 1)
                pe.wait_ge(s["ut_ready"], t + 1)
                pe.wait_ge(s["y_ready"], t + 1)
                for k in range(KD):
                    for j in range(2):
                        w = w_dn[:, slot, k, j * 512:(j + 1) * 512].rearrange("p a n -> p (a n)")
                        last = pe.matmul(psum[:, 5 + j, :], u_t[:, k, :], w, start=(k == 0), stop=(k == KD - 1))
                last.then_inc(s["dn_mm"], 1)

            def turn_u(t):
                pe.wait_ge(s["u_ready"], t + 1)
                for k in range(KD):
                    last = pe.transpose(psum[:, 4, k * P:(k + 1) * P], u[:, k * P:(k + 1) * P], ident[:, :])
                last.then_inc(s["u_turned"], 1)

            turn_x(0, 0, 1)

            def step(t, par, i):
                hidden(t)
                turn_x(t + 1, 1 - par, i + 2)
                if not is_first(t):
                    down(t - 1)
                turn_u(t)

            end = steps(pe, step)
            down(end)

        @block.scalar
        def _(act):
            act.sem_inc(s["y_ready"], 1)

            def keep_x(t):
                act.wait_ge(s["x_turned"], t + 1)
                nc.scalar.activation(x_h[:, :, :], psum[:, 2:4, :].rearrange("p a (k r) -> p (a k) r", r=P), ACT.Copy).then_inc(s["xh_ready"], 1)

            def split(e):
                slot = bass.ds(e % 2, 1)
                act.wait_ge(gu_loaded[0], (e // 2 + 1) * 32)
                act.wait_ge(gu_loaded[1], (e + 1) // 2 * 32 + 1)
                for k in range(KC):
                    act.sem_inc(s["waits_alone"], 1)
                    nc.scalar.activation(part(w_h, slot, k), part(w_gu, slot, k), ACT.Copy).then_inc(s["wh_ready"], 1)

            split(act.value_load(b["list_info"][0:1, 0:1], min_val=0, max_val=NE - 1))
            keep_x(0)

            def step(t, par, i):
                e = act.value_load(b["list_info"][0:1, after(SPLIT, t)], min_val=0, max_val=NE - 1)
                with act.If(e > 0):
                    split(e)
                if not is_first(t):
                    act.wait_ge(s["u_ready"], t)
                act.wait_ge(s["gu_mm"], t + 2)
                nc.scalar.activation(silu[:, :], psum[:, 0, :], ACT.Silu).then_inc(s["silu_ready"], 1)
                keep_x(t + 1)

            steps(act, step)

        @block.vector
        def _(dve):
            def gated(out, t, gates):
                n = lambda ap: ap.rearrange("p (a n) -> p a n", a=2)
                dve.scalar_tensor_tensor(out=n(out), in0=psum[:, 5:7, :], scalar=b["list_gate"][:, one(t)], in1=n(gates),
                                         op0=ALU.mult, op1=ALU.mult).then_inc(s["y_ready"], 1)

            def rest_of_x(t):
                dve.wait_ge(s["xh_ready"], t + 1)
                dve.tensor_tensor(x_l[:, :, :], psum[:, 2:4, :].rearrange("p a (k r) -> p (a k) r", r=P),
                                  x_h[:, :, :].bitcast(F32), ALU.subtract).then_inc(s["xl_ready"], 1)

            def split(e, nth):
                slot = bass.ds(e % 2, 1)
                for k in range(KC):
                    dve.wait_ge(s["wh_ready"], nth * KC + (k + 1))
                    w = part(w_gu, slot, k)
                    dve.tensor_tensor(w.bitcast(F32R), w, part(w_h, slot, k).bitcast(F32), ALU.subtract)

            split(dve.value_load(b["list_info"][0:1, 0:1], min_val=0, max_val=NE - 1), 0)
            rest_of_x(0)

            def step(t, par, i):
                e = dve.value_load(b["list_info"][0:1, after(SPLIT, t)], min_val=0, max_val=NE - 1)
                nth = dve.value_load(b["list_info"][0:1, after(NTH, t)], min_val=0, max_val=NE - 1)
                with dve.If(e > 0):
                    split(e, nth)
                dve.wait_ge(s["silu_ready"], t + 1)
                dve.tensor_tensor(u[:, :], silu[:, :], psum[:, 1, :], ALU.mult).then_inc(s["u_ready"], 1)
                rest_of_x(t + 1)
                if not is_first(t):
                    dve.wait_ge(s["dn_mm"], t + 1)
                    stored_before(dve, t, par, i)
                    dve.wait_ge(gates_in[1 - par], (i + 1) * 16)
                    gated(y_s[:, 1 - par, :], t - 1, gate_g[:, 1 - par, :])
                dve.wait_ge(s["u_turned"], t + 1)
                dve.tensor_copy(u_t[:, :, :], psum[:, 4, :].rearrange("p (k r) -> p k r", r=P)).then_inc(s["ut_ready"], 1)

            end = steps(dve, step)
            dve.wait_ge(s["dn_mm"], end + 2)
            dve.wait_ge(gates_in[0], (end + 2) // 2 * 16)
            dve.wait_ge(gates_in[1], (end + 1) // 2 * 16)
            gated(y_end[:, :], end, gate_g[:, bass.ds(end % 2, 1), :].rearrange("p a n -> p (a n)"))


def program(nc, args):
    stream_layer(nc, *args)


_OUTS = [(TABLE, D), (P, KW), (P, KW), (8, HD, HD), (P, KW), (P, KW), (NB, 8, HD, HD)]


def kernel(**inputs):
    import numpy as np
    import concourse.bacc as bacc
    from concourse.bass_utils import run_bass_kernel_spmd

    a = {k: np.asarray(v) for k, v in inputs.items()}
    nc = bacc.Bacc("TRN2", target_bir_lowering=False, num_devices=1)
    arrays = {
        "x": np.concatenate([a["x_prompt"].reshape(-1, D), a["x_sample"].reshape(-1, D), np.zeros((P, D), np.float32)]),
        "cond": np.concatenate([a["c_prompt"], a["c_sample"]]),
        "cache_k": a["cache_k"][0].reshape(NB, WIN, KW),
        "cache_v": a["cache_v"][0].reshape(NB, WIN, KW),
        "state_in": a["state_hgrn"][0],
        **{k: a[k][0] for k in ("w_ada", "b_ada", "ln1", "ln2", "w_in", "q_norm", "k_norm", "sinks", "o_norm", "w_out")},
        "w_router": a["w_router"], "router_bias": a["router_bias"],
        **{k: a[k][0] for k in ("w_e_gate", "w_e_up", "w_e_down")},
    }
    arrays = {f"in_{k}": np.ascontiguousarray(v) for k, v in arrays.items()}
    args = [nc.dram_tensor(k, v.shape, F32, kind="ExternalInput").ap() for k, v in arrays.items()]
    args += [nc.dram_tensor(f"out_{i}", s, F32, kind="ExternalOutput").ap() for i, s in enumerate(_OUTS)]
    program(nc, args)
    r = run_bass_kernel_spmd(nc, [arrays], core_ids=[0]).results[0]
    y, kp, vp, sp, ks, vs, ss = (r[f"out_{i}"] for i in range(len(_OUTS)))
    return (y[:TP * P].reshape(1, TP * P, D), y[TP * P:ROWS].reshape(NB, L, D), kp.reshape(1, 1, P, NKV, HD),
            vp.reshape(1, 1, P, NKV, HD), sp.reshape(1, 1, 8, HD, HD), ks.reshape(1, NB, L, NKV, HD),
            vs.reshape(1, NB, L, NKV, HD), ss.reshape(1, NB, 8, HD, HD))
```
